# Optimizing a Trainium2 kernel written in Bass

```python
import math
import jax
import jax.numpy as jnp
from jax import lax
import numpy as np
import jax, jax.numpy as jnp

D_MODEL = 1024
BATCH = 1
SEQ = 256
DEPTH = 1

CTX_LEN = 256
GRID_W = 64
EPS = 1e-6

ATT_HEADS = 8
ATT_KV_HEADS = 2
ATT_GROUP = ATT_HEADS // ATT_KV_HEADS
HEAD_DIM = 128
ROPE_PAIRS_PER_AXIS = HEAD_DIM // 4
ROPE_THETA = 10000.0
Q_BLOCK = 128

GLA_HEADS = 4
GLA_DK = 64
GLA_DV = 128
GLA_RANK = 16
GLA_TAU = 16.0
GLA_CHUNK = 64

HY_WIDTH = 512
HY_ORDER = 2
HY_BANDS = 16
HY_EMB = 1 + 2 * HY_BANDS
HY_FFN = 64
HY_DECAY_SLOW = -math.log(1e-2) / 1.5
HY_DECAY_FAST = -math.log(1e-2) / 0.3

N_EXPERTS = 16
N_GROUPS = 4
EXPERTS_PER_GROUP = N_EXPERTS // N_GROUPS
TOP_K = 2
D_EXPERT = 512

N_BRANCH = 3
ATT_Q_W = ATT_HEADS * HEAD_DIM
ATT_KV_W = ATT_KV_HEADS * HEAD_DIM
GLA_K_W = GLA_HEADS * GLA_DK
GLA_V_W = GLA_HEADS * GLA_DV
KV_SPLITS = (ATT_KV_W, ATT_KV_W, GLA_K_W, GLA_V_W, 2 * GLA_RANK)
REST_SPLITS = (ATT_Q_W, GLA_K_W, GLA_V_W, 3 * HY_WIDTH, N_BRANCH * D_MODEL)
N_KV_COLS = sum(KV_SPLITS)
N_IN = N_KV_COLS + sum(REST_SPLITS)


def rms_norm(x, g):
    xf = x.astype(jnp.float32)
    y = xf * lax.rsqrt(jnp.mean(xf * xf, axis=-1, keepdims=True) + EPS)
    return (y * g.astype(jnp.float32)).astype(x.dtype)

def split_cols(t, sizes):
    cuts = [int(v) for v in np.cumsum(sizes)[:-1]]
    return jnp.split(t, cuts, axis=-1)

def modulate(h, shift, scale):
    return h * (1 + scale[..., None, :]) + shift[..., None, :]

def to_heads(t, n_heads):
    b, n, w = t.shape
    return t.reshape(b, n, n_heads, w // n_heads).transpose(0, 2, 1, 3)

def q_heads(t):
    b, n, _ = t.shape
    return t.reshape(b, n, ATT_KV_HEADS, ATT_GROUP, HEAD_DIM).transpose(0, 2, 3, 1, 4)

def tflip(t):
    return jnp.flip(t, axis=2)

def axial_rope_tables(n_tokens):
    rows = n_tokens // GRID_W
    row = jnp.broadcast_to(jnp.arange(rows)[:, None], (rows, GRID_W)).reshape(-1).astype(jnp.float32)
    col = jnp.broadcast_to(jnp.arange(GRID_W)[None, :], (rows, GRID_W)).reshape(-1).astype(jnp.float32)
    inv_freq = ROPE_THETA ** (-jnp.arange(ROPE_PAIRS_PER_AXIS, dtype=jnp.float32) / ROPE_PAIRS_PER_AXIS)
    ang = jnp.concatenate([row[:, None] * inv_freq, col[:, None] * inv_freq], axis=-1)
    return jnp.cos(ang), jnp.sin(ang)

def apply_rope(x, cos, sin):
    xf = x.astype(jnp.float32)
    x1, x2 = xf[..., 0::2], xf[..., 1::2]
    out = jnp.stack([x1 * cos - x2 * sin, x1 * sin + x2 * cos], axis=-1)
    return out.reshape(x.shape).astype(x.dtype)

def gqa_latent(q, k, v):
    b, hkv, g, s, hd = q.shape
    nb = s // Q_BLOCK
    qb = jnp.moveaxis(q.reshape(b, hkv, g, nb, Q_BLOCK, hd), 3, 0)
    scale = HEAD_DIM ** -0.5

    def one_block(qblk):
        sc = jnp.einsum('bkgqd,bknd->bkgqn', qblk, k).astype(jnp.float32) * scale
        p = jax.nn.softmax(sc, axis=-1).astype(v.dtype)
        return jnp.einsum('bkgqn,bknd->bkgqd', p, v)

    o = lax.map(one_block, qb)
    return o.transpose(1, 0, 4, 2, 3, 5).reshape(b, s, hkv * g * hd)

def gqa_context(q, k, v):
    b, hkv, g, n, hd = q.shape
    sc = jnp.einsum('bkgqd,bknd->bkgqn', q, k).astype(jnp.float32) * HEAD_DIM ** -0.5
    p = jax.nn.softmax(sc, axis=-1).astype(v.dtype)
    o = jnp.einsum('bkgqn,bknd->bkgqd', p, v)
    return o.transpose(0, 3, 1, 2, 4).reshape(b, n, hkv * g * hd)

def gla_q(t):
    return to_heads(t, GLA_HEADS).astype(jnp.float32) * GLA_DK ** -0.5

def gla_log_decay(a_low, w_a2, b_a):
    z = (a_low @ w_a2 + b_a).astype(jnp.float32)
    return to_heads(jax.nn.log_sigmoid(z) / GLA_TAU, GLA_HEADS)

def gla_chunked(q, k, v, log_a, s0):
    b, h, n_tok, dk = q.shape
    dv = v.shape[-1]
    n = n_tok // GLA_CHUNK

    def rs(t):
        return t.reshape(b, h, n, GLA_CHUNK, t.shape[-1])

    q, k, v, log_a = rs(q), rs(k), rs(v), rs(log_a)
    cum = jnp.cumsum(log_a, axis=3)
    cum_last = cum[:, :, :, -1:, :]
    q_dec = q * jnp.exp(cum)
    k_inv = k * jnp.exp(-cum)
    k_to_end = k * jnp.exp(cum_last - cum)
    mask = jnp.tril(jnp.ones((GLA_CHUNK, GLA_CHUNK), dtype=bool))
    att = jnp.where(mask, jnp.einsum('bhnqd,bhnsd->bhnqs', q_dec, k_inv), 0.0)
    o_intra = jnp.einsum('bhnqs,bhnsv->bhnqv', att, v)
    chunk_state = jnp.einsum('bhnsd,bhnsv->bhndv', k_to_end, v)
    chunk_decay = jnp.exp(cum_last[:, :, :, 0, :])

    def step(state, xs):
        dec, cs = xs
        return dec[..., None] * state + cs, state

    s_final, s_prev = lax.scan(step, s0, (jnp.moveaxis(chunk_decay, 2, 0), jnp.moveaxis(chunk_state, 2, 0)))
    s_prev = jnp.moveaxis(s_prev, 0, 2)
    o_inter = jnp.einsum('bhnqd,bhndv->bhnqv', q_dec, s_prev)
    return (o_intra + o_inter).reshape(b, h, n_tok, dv), s_final

def gla_final_state(k, v, log_a):
    cum = jnp.cumsum(log_a, axis=2)
    w = jnp.exp(cum[:, :, -1:, :] - cum)
    return jnp.einsum('bhld,bhlv->bhdv', k * w, v)

def gla_bidir(q, k, v, la_f, la_b, s0_f, s0_b):
    o_f, s_f = gla_chunked(q, k, v, la_f, s0_f)
    o_b, s_b = gla_chunked(tflip(q), tflip(k), tflip(v), tflip(la_b), s0_b)
    return o_f + tflip(o_b), s_f, s_b

def gla_output(o, og, norm_g):
    b, h, n, dv = o.shape
    on = rms_norm(o, norm_g).transpose(0, 2, 1, 3).reshape(b, n, h * dv)
    return (on * jax.nn.silu(og.astype(jnp.float32))).astype(og.dtype)

def hyena_filters(n, P):
    f32 = jnp.float32
    t = jnp.arange(n, dtype=f32)
    t_norm = t / n
    bands = jnp.linspace(1e-4, HY_BANDS - 1, HY_BANDS, dtype=f32)
    phase = (2 * math.pi / n) * t[:, None] * bands[None, :]
    z = jnp.concatenate([t_norm[:, None], jnp.cos(phase), -jnp.sin(phase)], axis=-1)
    freq = P['hy_sin_freq'].astype(f32)
    hid = jnp.sin(freq * (z @ P['hy_pos_w1'].astype(f32) + P['hy_pos_b1'].astype(f32)))
    hid = jnp.sin(freq * (hid @ P['hy_pos_w2'].astype(f32) + P['hy_pos_b2'].astype(f32)))
    filt = (hid @ P['hy_pos_w3'].astype(f32)).reshape(n, HY_ORDER, 2, HY_WIDTH)
    filt = filt * jnp.exp(-t_norm[:, None, None, None] * jnp.abs(P['hy_decay'].astype(f32)))
    fwd, bwd = filt[:, :, 0], filt[:, :, 1]
    taps = jnp.concatenate([fwd, jnp.zeros_like(fwd[:1]), jnp.flip(bwd[1:], axis=0)], axis=0)
    taps = taps / (jnp.sum(jnp.abs(taps), axis=0, keepdims=True) + EPS)
    return jnp.fft.rfft(taps, axis=0)

def short_conv(u, w, b):
    up = jnp.pad(u, ((0, 0), (1, 1), (0, 0)))
    return up[:, :-2] * w[0] + up[:, 1:-1] * w[1] + up[:, 2:] * w[2] + b

def hyena_mix(u, P):
    n = u.shape[1]
    filt = hyena_filters(n, P)
    uc = short_conv(u, P['hy_conv_w'], P['hy_conv_b']).astype(jnp.float32)
    x1, x2, z = jnp.split(uc, 3, axis=-1)
    skip = P['hy_skip'].astype(jnp.float32)
    for o, gate in enumerate((x1, x2)):
        zf = jnp.fft.rfft(z, n=2 * n, axis=1)
        conv = jnp.fft.irfft(zf * filt[None, :, o], n=2 * n, axis=1)[:, :n]
        z = gate * (conv + skip[o] * z)
    return z.astype(u.dtype)

def merge_branches(y_hy, y_gla, y_att, br_g, P):
    g_hy, g_gla, g_att = jnp.split(br_g, N_BRANCH, axis=-1)
    m = (jax.nn.sigmoid(g_hy) * (y_hy @ P['w_br_hy'])
         + jax.nn.sigmoid(g_gla) * (y_gla @ P['w_br_gla'])
         + jax.nn.sigmoid(g_att) * (y_att @ P['w_br_att']))
    return m @ P['w_out']

def token_mixer(h, hc, P, last):
    f32 = jnp.float32
    b, s, _ = h.shape
    cos, sin = axial_rope_tables(s)
    proj = h @ P['w_in']
    a_k, a_v, g_k, g_v, g_a = split_cols(proj[..., :N_KV_COLS], KV_SPLITS)
    a_q, g_q, g_og, hy_u, br_g = split_cols(proj[..., N_KV_COLS:], REST_SPLITS)
    cproj = hc @ (P['w_in'][:, :N_KV_COLS] if last else P['w_in'])
    c_ak, c_av, c_gk, c_gv, c_ga = split_cols(cproj[..., :N_KV_COLS], KV_SPLITS)

    k_ctx = rms_norm(to_heads(c_ak, ATT_KV_HEADS), P['k_norm_g'])
    v_ctx = to_heads(c_av, ATT_KV_HEADS)
    k_lat = apply_rope(rms_norm(to_heads(a_k, ATT_KV_HEADS), P['k_norm_g']), cos, sin)
    q_lat = apply_rope(rms_norm(q_heads(a_q), P['q_norm_g']), cos, sin)
    keys = jnp.concatenate([k_lat, k_ctx], axis=2)
    vals = jnp.concatenate([to_heads(a_v, ATT_KV_HEADS), v_ctx], axis=2)
    y_att = gqa_latent(q_lat, keys, vals)

    c_k = to_heads(c_gk, GLA_HEADS).astype(f32)
    c_v = to_heads(c_gv, GLA_HEADS).astype(f32)
    c_la_f = gla_log_decay(c_ga[..., :GLA_RANK], P['gla_wa2'][0], P['gla_ba'][0])
    c_la_b = gla_log_decay(c_ga[..., GLA_RANK:], P['gla_wa2'][1], P['gla_ba'][1])
    if last:
        s_f = gla_final_state(c_k, c_v, c_la_f)
        s_b = gla_final_state(tflip(c_k), tflip(c_v), tflip(c_la_b))
    else:
        c_aq, c_gq, c_og, c_hy, c_brg = split_cols(cproj[..., N_KV_COLS:], REST_SPLITS)
        s0 = jnp.zeros((b, GLA_HEADS, GLA_DK, GLA_DV), f32)
        c_o, s_f, s_b = gla_bidir(gla_q(c_gq), c_k, c_v, c_la_f, c_la_b, s0, s0)
    la_f = gla_log_decay(g_a[..., :GLA_RANK], P['gla_wa2'][0], P['gla_ba'][0])
    la_b = gla_log_decay(g_a[..., GLA_RANK:], P['gla_wa2'][1], P['gla_ba'][1])
    o_lat, _, _ = gla_bidir(gla_q(g_q), to_heads(g_k, GLA_HEADS).astype(f32),
                            to_heads(g_v, GLA_HEADS).astype(f32), la_f, la_b, s_f, s_b)
    y_gla = gla_output(o_lat, g_og, P['gla_norm_g'])

    y_hy = hyena_mix(hy_u, P)

    out = merge_branches(y_hy, y_gla, y_att, br_g, P)
    if last:
        return out, None
    yc_att = gqa_context(rms_norm(q_heads(c_aq), P['q_norm_g']), k_ctx, v_ctx)
    yc_gla = gla_output(c_o, c_og, P['gla_norm_g'])
    yc_hy = hyena_mix(c_hy, P)
    return out, merge_branches(yc_hy, yc_gla, yc_att, c_brg, P)

def grouped_moe(h, router_w, router_b, w_gate, w_up, w_down):
    f32 = jnp.float32
    shape = h.shape
    ht = h.reshape(-1, shape[-1])
    scores = jax.nn.sigmoid((ht @ router_w).astype(f32))
    sel = scores + router_b.astype(f32)
    group_score = lax.top_k(sel.reshape(-1, N_GROUPS, EXPERTS_PER_GROUP), TOP_K)[0].sum(-1)
    group = jnp.argmax(group_score, axis=-1)
    in_group = (jnp.arange(N_EXPERTS) // EXPERTS_PER_GROUP)[None, :] == group[:, None]
    _, idx = lax.top_k(jnp.where(in_group, sel, -jnp.inf), TOP_K)
    w = jnp.take_along_axis(scores, idx, axis=-1)
    w = w / jnp.sum(w, axis=-1, keepdims=True)
    gates = jnp.sum(jax.nn.one_hot(idx, N_EXPERTS, dtype=f32) * w[..., None], axis=1).astype(h.dtype)
    out = jnp.zeros_like(ht)
    for e in range(N_EXPERTS):
        hid = jax.nn.silu(ht @ w_gate[e]) * (ht @ w_up[e])
        out = out + gates[:, e:e + 1] * (hid @ w_down[e])
    return out.reshape(shape)

def first_inputs(seed: int = 0) -> dict:
    key = jax.random.key(seed)
    keys = iter(jax.random.split(key, 48))

    def nrm(shape, scale):
        return jax.random.normal(next(keys), shape, jnp.float32) * scale

    D = D_MODEL
    decay_base = jnp.linspace(HY_DECAY_SLOW, HY_DECAY_FAST, HY_WIDTH, dtype=jnp.float32)
    return {
        'x': nrm((BATCH, SEQ, D), 1.0),
        'c': nrm((BATCH, D), 1.0),
        'ctx': nrm((BATCH, CTX_LEN, D), 1.0),
        'c_ctx': nrm((D,), 1.0),
        'w_mod': nrm((DEPTH, D, 6 * D), 0.5 * D ** -0.5),
        'b_mod': nrm((DEPTH, 6 * D), 0.02),
        'norm1_g': 1.0 + nrm((DEPTH, D), 0.05),
        'norm2_g': 1.0 + nrm((DEPTH, D), 0.05),
        'w_in': nrm((DEPTH, D, N_IN), D ** -0.5),
        'q_norm_g': 1.0 + nrm((DEPTH, HEAD_DIM), 0.05),
        'k_norm_g': 1.0 + nrm((DEPTH, HEAD_DIM), 0.05),
        'gla_wa2': nrm((DEPTH, 2, GLA_RANK, GLA_K_W), GLA_RANK ** -0.5),
        'gla_ba': nrm((DEPTH, 2, GLA_K_W), 0.02),
        'gla_norm_g': 1.0 + nrm((DEPTH, GLA_DV), 0.05),
        'hy_conv_w': nrm((DEPTH, 3, 3 * HY_WIDTH), 3 ** -0.5),
        'hy_conv_b': nrm((DEPTH, 3 * HY_WIDTH), 0.02),
        'hy_pos_w1': nrm((DEPTH, HY_EMB, HY_FFN), HY_EMB ** -0.5),
        'hy_pos_b1': nrm((DEPTH, HY_FFN), 0.02),
        'hy_sin_freq': 1.0 + nrm((DEPTH, HY_FFN), 0.05),
        'hy_pos_w2': nrm((DEPTH, HY_FFN, HY_FFN), HY_FFN ** -0.5),
        'hy_pos_b2': nrm((DEPTH, HY_FFN), 0.02),
        'hy_pos_w3': nrm((DEPTH, HY_FFN, HY_ORDER * 2 * HY_WIDTH), HY_FFN ** -0.5),
        'hy_decay': decay_base * (1.0 + nrm((DEPTH, HY_ORDER, 2, HY_WIDTH), 0.05)),
        'hy_skip': nrm((DEPTH, HY_ORDER, HY_WIDTH), 1.0),
        'w_br_hy': nrm((DEPTH, HY_WIDTH, D), HY_WIDTH ** -0.5),
        'w_br_gla': nrm((DEPTH, GLA_V_W, D), GLA_V_W ** -0.5),
        'w_br_att': nrm((DEPTH, ATT_Q_W, D), ATT_Q_W ** -0.5),
        'w_out': nrm((DEPTH, D, D), D ** -0.5),
        'router_w': nrm((D, N_EXPERTS), D ** -0.5),
        'router_b': nrm((N_EXPERTS,), 0.01),
        'moe_w_gate': nrm((DEPTH, N_EXPERTS, D, D_EXPERT), D ** -0.5),
        'moe_w_up': nrm((DEPTH, N_EXPERTS, D, D_EXPERT), D ** -0.5),
        'moe_w_down': nrm((DEPTH, N_EXPERTS, D_EXPERT, D), D_EXPERT ** -0.5),
    }

def first_block(x, c, ctx, c_ctx, w_mod, b_mod, norm1_g, norm2_g, w_in, q_norm_g, k_norm_g,
              gla_wa2, gla_ba, gla_norm_g, hy_conv_w, hy_conv_b, hy_pos_w1, hy_pos_b1,
              hy_sin_freq, hy_pos_w2, hy_pos_b2, hy_pos_w3, hy_decay, hy_skip,
              w_br_hy, w_br_gla, w_br_att, w_out, router_w, router_b,
              moe_w_gate, moe_w_up, moe_w_down):
    xc = ctx
    sc = jax.nn.silu(c)
    scc = jax.nn.silu(c_ctx)
    for l in range(DEPTH):
        last = l == DEPTH - 1
        P = {
            'w_in': w_in[l], 'q_norm_g': q_norm_g[l], 'k_norm_g': k_norm_g[l],
            'gla_wa2': gla_wa2[l], 'gla_ba': gla_ba[l], 'gla_norm_g': gla_norm_g[l],
            'hy_conv_w': hy_conv_w[l], 'hy_conv_b': hy_conv_b[l],
            'hy_pos_w1': hy_pos_w1[l], 'hy_pos_b1': hy_pos_b1[l], 'hy_sin_freq': hy_sin_freq[l],
            'hy_pos_w2': hy_pos_w2[l], 'hy_pos_b2': hy_pos_b2[l], 'hy_pos_w3': hy_pos_w3[l],
            'hy_decay': hy_decay[l], 'hy_skip': hy_skip[l],
            'w_br_hy': w_br_hy[l], 'w_br_gla': w_br_gla[l], 'w_br_att': w_br_att[l], 'w_out': w_out[l],
        }
        shift1, scale1, gate1, shift2, scale2, gate2 = jnp.split(sc @ w_mod[l] + b_mod[l], 6, axis=-1)
        n_cmod = 2 if last else 6
        cmods = jnp.split(scc @ w_mod[l][:, :n_cmod * D_MODEL] + b_mod[l][:n_cmod * D_MODEL], n_cmod, axis=-1)

        h = modulate(rms_norm(x, norm1_g[l]), shift1, scale1)
        hc = modulate(rms_norm(xc, norm1_g[l]), cmods[0], cmods[1])
        y, yc = token_mixer(h, hc, P, last)
        x = x + gate1[:, None, :] * y
        h = modulate(rms_norm(x, norm2_g[l]), shift2, scale2)
        x = x + gate2[:, None, :] * grouped_moe(h, router_w, router_b, moe_w_gate[l], moe_w_up[l], moe_w_down[l])
        if not last:
            xc = xc + cmods[2] * yc
            hc = modulate(rms_norm(xc, norm2_g[l]), cmods[3], cmods[4])
            xc = xc + cmods[5] * grouped_moe(hc, router_w, router_b, moe_w_gate[l], moe_w_up[l], moe_w_down[l])
    return x


DEPTH_2 = 2

PLE_DIM = 256
ROPE_THETA_2 = 500000.0
MAX_POS_OFFSET = 4096
A_HEAD_DIM = 64
A_HEADS = D_MODEL // (2 * A_HEAD_DIM)
A_ROT = A_HEAD_DIM // 4
A_PATTERNS = ((128, 1), (512, 4), (2048, 16))
B_HEADS = D_MODEL // 128
B_Q_LORA = 3 * D_MODEL // 8
B_KV_LORA = D_MODEL // 4
B_NOPE = 64
B_ROPE = 32
B_V = 64
C_HEAD_DIM = 64
C_HEADS = D_MODEL // (2 * C_HEAD_DIM)
C_ROT = C_HEAD_DIM // 4
D_FF = 256 * math.ceil(8 * D_MODEL / 3 / 256)
CONV_WIDTH = 3
LN_EPS = 1e-5
RMS_EPS = 1e-6
NEG_INF = -1e30
N_AB = (DEPTH_2 + 1) // 2
N_C = DEPTH_2 // 2
ALPHA = (2 * DEPTH_2) ** 0.25
BETA = (8 * DEPTH_2) ** -0.25
A_WIDTH = A_HEADS * A_HEAD_DIM
AB_IN = 3 * A_WIDTH + B_Q_LORA + B_KV_LORA + B_ROPE
AB_MIX = A_WIDTH + B_HEADS * B_V
C_QK = C_HEADS * 2 * C_HEAD_DIM
C_MIX = C_HEADS * 2 * C_HEAD_DIM


def layer_norm(x, g, b):
    xf = x.astype(jnp.float32)
    mu = jnp.mean(xf, axis=-1, keepdims=True)
    var = jnp.mean(jnp.square(xf - mu), axis=-1, keepdims=True)
    y = (xf - mu) * lax.rsqrt(var + LN_EPS)
    return (y * g.astype(jnp.float32) + b.astype(jnp.float32)).astype(x.dtype)

def rms_norm_2(x, g, eps):
    xf = x.astype(jnp.float32)
    y = xf * lax.rsqrt(jnp.mean(jnp.square(xf), axis=-1, keepdims=True) + eps)
    return (y * g.astype(jnp.float32)).astype(x.dtype)

def rope_tables(positions, rot):
    inv_freq = 1.0 / (ROPE_THETA_2 ** (jnp.arange(0, rot, 2, dtype=jnp.float32) / rot))
    ang = positions.astype(jnp.float32)[..., None] * inv_freq
    return jnp.cos(ang), jnp.sin(ang)

def apply_rope_2(x, cos, sin, rot):
    bshape = cos.shape[:2] + (1,) * (x.ndim - 3) + cos.shape[-1:]
    c = cos.reshape(bshape).astype(x.dtype)
    s = sin.reshape(bshape).astype(x.dtype)
    half = rot // 2
    x1, x2, rest = x[..., :half], x[..., half:rot], x[..., rot:]
    return jnp.concatenate([x1 * c - x2 * s, x2 * c + x1 * s, rest], axis=-1)

def dilated_window_attention(q, k, v, window, dilation):
    B, H, S, dh = q.shape
    n_side = window // (2 * dilation)
    L = S // dilation
    blk = n_side
    nb = -(-L // blk)
    Lp = nb * blk

    def strided(t):
        return t.reshape(B, H, L, dilation, dh).transpose(0, 1, 3, 2, 4)

    def slabs(t):
        tp = jnp.pad(t, ((0, 0), (0, 0), (0, 0), (blk, Lp - L + blk), (0, 0)))
        tp = tp.reshape(B, H, dilation, nb + 2, blk, dh)
        return jnp.concatenate([tp[:, :, :, 0:nb], tp[:, :, :, 1:nb + 1], tp[:, :, :, 2:nb + 2]], axis=4)

    qb = jnp.pad(strided(q), ((0, 0), (0, 0), (0, 0), (0, Lp - L), (0, 0))).reshape(B, H, dilation, nb, blk, dh)
    kb = slabs(strided(k))
    vb = slabs(strided(v))
    s = jnp.einsum("bhrnqd,bhrnkd->bhrnqk", qb, kb) * (dh ** -0.5)
    qi = jnp.arange(nb)[:, None, None] * blk + jnp.arange(blk)[None, :, None]
    ki = jnp.arange(nb)[:, None, None] * blk - blk + jnp.arange(3 * blk)[None, None, :]
    valid = (ki >= 0) & (ki < L) & (jnp.abs(ki - qi) <= n_side)
    s = jnp.where(valid, s, NEG_INF)
    m = jnp.max(s, axis=-1, keepdims=True)
    e = jnp.exp(s - m)
    l = jnp.sum(e, axis=-1)
    o = jnp.einsum("bhrnqk,bhrnkd->bhrnqd", e, vb) / l[..., None]
    lse = m[..., 0] + jnp.log(l)
    o = o.reshape(B, H, dilation, Lp, dh)[:, :, :, :L].transpose(0, 1, 3, 2, 4).reshape(B, H, S, dh)
    lse = lse.reshape(B, H, dilation, Lp)[..., :L].transpose(0, 1, 3, 2).reshape(B, H, S)
    return o, lse

def dilated_mixture(q, k, v):
    B, S, H, dh = q.shape
    qf, kf, vf = (t.astype(jnp.float32).transpose(0, 2, 1, 3) for t in (q, k, v))
    outs, lses = [], []
    for window, dilation in A_PATTERNS:
        o, lse = dilated_window_attention(qf, kf, vf, window, dilation)
        outs.append(o)
        lses.append(lse)
    w = jax.nn.softmax(jnp.stack(lses), axis=0)
    o = jnp.sum(w[..., None] * jnp.stack(outs), axis=0)
    return o.transpose(0, 2, 1, 3).reshape(B, S, H * dh)

def dense_attention(q, k, v, scale):
    B, S, H, dq = q.shape
    dv = v.shape[-1]
    nq = S // Q_BLOCK
    kf = k.astype(jnp.float32).transpose(0, 2, 1, 3)
    vf = v.astype(jnp.float32).transpose(0, 2, 1, 3)
    qb = q.astype(jnp.float32).transpose(0, 2, 1, 3).reshape(B, H, nq, Q_BLOCK, dq).transpose(2, 0, 1, 3, 4)

    def block(qi):
        s = jnp.einsum("bhqd,bhkd->bhqk", qi, kf) * scale
        return jnp.einsum("bhqk,bhkd->bhqd", jax.nn.softmax(s, axis=-1), vf)

    o = lax.map(block, qb)
    return o.transpose(1, 0, 3, 2, 4).reshape(B, S, H * dv)

def diff_attention(q, k, v, lam):
    B, S, H, _, dh = q.shape
    dv = v.shape[-1]
    nq = S // Q_BLOCK
    kf = k.astype(jnp.float32).transpose(0, 2, 3, 1, 4)
    vf = v.astype(jnp.float32).transpose(0, 2, 1, 3)
    qb = q.astype(jnp.float32).transpose(0, 2, 3, 1, 4).reshape(B, H, 2, nq, Q_BLOCK, dh).transpose(3, 0, 1, 2, 4, 5)

    def block(qi):
        s = jnp.einsum("bhcqd,bhckd->bhcqk", qi, kf) * (dh ** -0.5)
        a = jax.nn.softmax(s, axis=-1)
        return jnp.einsum("bhqk,bhkd->bhqd", a[:, :, 0] - lam * a[:, :, 1], vf)

    o = lax.map(block, qb)
    return o.transpose(1, 0, 3, 2, 4).reshape(B, S, H, dv)

def mixer_ab(x, cos_a, sin_a, cos_b, sin_b, w_in, q_norm, w_q_up, kv_norm, w_kv_up, w_out):
    B, S, _ = x.shape
    h = x @ w_in
    o1 = A_WIDTH
    o2 = 2 * A_WIDTH
    o3 = 3 * A_WIDTH
    o4 = o3 + B_Q_LORA
    o5 = o4 + B_KV_LORA
    shape_a = (B, S, A_HEADS, A_HEAD_DIM)
    qa = apply_rope_2(h[..., :o1].reshape(shape_a), cos_a, sin_a, A_ROT)
    ka = apply_rope_2(h[..., o1:o2].reshape(shape_a), cos_a, sin_a, A_ROT)
    va = h[..., o2:o3].reshape(shape_a)
    out_a = dilated_mixture(qa, ka, va).astype(x.dtype)
    cq = rms_norm_2(h[..., o3:o4], q_norm, RMS_EPS)
    qb = (cq @ w_q_up).reshape(B, S, B_HEADS, B_NOPE + B_ROPE)
    q_pe = apply_rope_2(qb[..., B_NOPE:], cos_b, sin_b, B_ROPE)
    qb = jnp.concatenate([qb[..., :B_NOPE], q_pe], axis=-1)
    ckv = rms_norm_2(h[..., o4:o5], kv_norm, RMS_EPS)
    kv = (ckv @ w_kv_up).reshape(B, S, B_HEADS, B_NOPE + B_V)
    k_pe = apply_rope_2(h[..., o5:].reshape(B, S, 1, B_ROPE), cos_b, sin_b, B_ROPE)
    kb = jnp.concatenate([kv[..., :B_NOPE], jnp.broadcast_to(k_pe, (B, S, B_HEADS, B_ROPE))], axis=-1)
    vb = kv[..., B_NOPE:]
    out_b = dense_attention(qb, kb, vb, (B_NOPE + B_ROPE) ** -0.5).astype(x.dtype)
    return jnp.concatenate([out_a, out_b], axis=-1) @ w_out

def mixer_c(x, cos_c, sin_c, w_qkv, lam_params, subln, w_out, lambda_init):
    B, S, _ = x.shape
    h = x @ w_qkv
    q = apply_rope_2(h[..., :C_QK].reshape(B, S, C_HEADS, 2, C_HEAD_DIM), cos_c, sin_c, C_ROT)
    k = apply_rope_2(h[..., C_QK:2 * C_QK].reshape(B, S, C_HEADS, 2, C_HEAD_DIM), cos_c, sin_c, C_ROT)
    v = h[..., 2 * C_QK:].reshape(B, S, C_HEADS, 2 * C_HEAD_DIM)
    lp = lam_params.astype(jnp.float32)
    lam = jnp.exp(jnp.sum(lp[0] * lp[1])) - jnp.exp(jnp.sum(lp[2] * lp[3])) + lambda_init
    o = diff_attention(q, k, v, lam)
    o = rms_norm_2(o, subln, LN_EPS) * (1.0 - lambda_init)
    return o.reshape(B, S, C_MIX).astype(x.dtype) @ w_out

def conv_ffn(x, w_gate, w_up, conv_w, conv_b, w_down):
    S = x.shape[1]
    a = x @ w_gate
    u = x @ w_up
    pad = CONV_WIDTH // 2
    ap = jnp.pad(a, ((0, 0), (pad, pad), (0, 0)))
    c = conv_b
    for j in range(CONV_WIDTH):
        c = c + conv_w[j] * ap[:, j:j + S]
    return (jax.nn.gelu(c) * u) @ w_down

def second_inputs(seed: int = 0) -> dict:
    key = jax.random.key(seed)
    ks = jax.random.split(key, 24)
    f32 = jnp.float32

    def w(k, shape, fan_in, gain=1.0):
        return jax.random.normal(k, shape, f32) * (gain * fan_in ** -0.5)

    def gain_init(k, shape):
        return 1.0 + 0.02 * jax.random.normal(k, shape, f32)

    def bias_init(k, shape):
        return 0.02 * jax.random.normal(k, shape, f32)

    x = jax.random.normal(ks[0], (BATCH, SEQ, D_MODEL), f32)
    p = jax.random.normal(ks[1], (DEPTH_2, BATCH, SEQ, PLE_DIM), f32)
    positions = (jnp.arange(SEQ, dtype=jnp.int32)[None, :]
                 + jax.random.randint(ks[2], (BATCH, 1), 0, MAX_POS_OFFSET, dtype=jnp.int32))
    return {
        "x": x,
        "p": p,
        "positions": positions,
        "ab_w_in": w(ks[3], (N_AB, D_MODEL, AB_IN), D_MODEL),
        "ab_q_norm": gain_init(ks[4], (N_AB, B_Q_LORA)),
        "ab_w_q_up": w(ks[5], (N_AB, B_Q_LORA, B_HEADS * (B_NOPE + B_ROPE)), B_Q_LORA),
        "ab_kv_norm": gain_init(ks[6], (N_AB, B_KV_LORA)),
        "ab_w_kv_up": w(ks[7], (N_AB, B_KV_LORA, B_HEADS * (B_NOPE + B_V)), B_KV_LORA),
        "ab_w_out": w(ks[8], (N_AB, AB_MIX, D_MODEL), AB_MIX, BETA),
        "c_w_qkv": w(ks[9], (N_C, D_MODEL, 2 * C_QK + C_MIX), D_MODEL),
        "c_lambda": 0.1 * jax.random.normal(ks[10], (N_C, 4, C_HEAD_DIM), f32),
        "c_subln": gain_init(ks[11], (N_C, 2 * C_HEAD_DIM)),
        "c_w_out": w(ks[12], (N_C, C_MIX, D_MODEL), C_MIX, BETA),
        "ln_mix_g": gain_init(ks[13], (DEPTH_2, D_MODEL)),
        "ln_mix_b": bias_init(ks[14], (DEPTH_2, D_MODEL)),
        "ffn_w_gate": w(ks[15], (DEPTH_2, D_MODEL, D_FF), D_MODEL),
        "ffn_w_up": w(ks[16], (DEPTH_2, D_MODEL, D_FF), D_MODEL),
        "ffn_conv_w": w(ks[17], (DEPTH_2, CONV_WIDTH, D_FF), CONV_WIDTH),
        "ffn_conv_b": bias_init(ks[18], (DEPTH_2, D_FF)),
        "ffn_w_down": w(ks[19], (DEPTH_2, D_FF, D_MODEL), D_FF, BETA),
        "ln_ffn_g": gain_init(ks[20], (DEPTH_2, D_MODEL)),
        "ln_ffn_b": bias_init(ks[21], (DEPTH_2, D_MODEL)),
        "ple_w_gate": w(ks[22], (DEPTH_2, D_MODEL, D_MODEL), D_MODEL),
        "ple_w_proj": w(ks[23], (DEPTH_2, PLE_DIM, D_MODEL), PLE_DIM),
    }

def second_block(x, p, positions, ab_w_in, ab_q_norm, ab_w_q_up, ab_kv_norm, ab_w_kv_up, ab_w_out,
              c_w_qkv, c_lambda, c_subln, c_w_out, ln_mix_g, ln_mix_b, ffn_w_gate, ffn_w_up,
              ffn_conv_w, ffn_conv_b, ffn_w_down, ln_ffn_g, ln_ffn_b, ple_w_gate, ple_w_proj):
    cos_a, sin_a = rope_tables(positions, A_ROT)
    cos_b, sin_b = rope_tables(positions, B_ROPE)
    cos_c, sin_c = rope_tables(positions, C_ROT)
    for i in range(DEPTH_2):
        j = i // 2
        if i % 2 == 0:
            y = mixer_ab(x, cos_a, sin_a, cos_b, sin_b, ab_w_in[j], ab_q_norm[j], ab_w_q_up[j],
                         ab_kv_norm[j], ab_w_kv_up[j], ab_w_out[j])
        else:
            lambda_init = 0.8 - 0.6 * math.exp(-0.3 * i)
            y = mixer_c(x, cos_c, sin_c, c_w_qkv[j], c_lambda[j], c_subln[j], c_w_out[j], lambda_init)
        x = layer_norm(ALPHA * x + y, ln_mix_g[i], ln_mix_b[i])
        f = conv_ffn(x, ffn_w_gate[i], ffn_w_up[i], ffn_conv_w[i], ffn_conv_b[i], ffn_w_down[i])
        x = layer_norm(ALPHA * x + f, ln_ffn_g[i], ln_ffn_b[i])
        x = x + jax.nn.sigmoid(x @ ple_w_gate[i]) * (p[i] @ ple_w_proj[i])
    return x


def setup_inputs(seed=0):
    out = dict(first_inputs(seed))
    for name, value in second_inputs(seed + 1).items():
        if name != "x":
            out[name + "_2"] = value
    return out


def reference(
    x, c, ctx, c_ctx, w_mod, b_mod, norm1_g, norm2_g, w_in, q_norm_g, k_norm_g, gla_wa2, gla_ba,
    gla_norm_g, hy_conv_w, hy_conv_b, hy_pos_w1, hy_pos_b1, hy_sin_freq, hy_pos_w2, hy_pos_b2,
    hy_pos_w3, hy_decay, hy_skip, w_br_hy, w_br_gla, w_br_att, w_out, router_w, router_b,
    moe_w_gate, moe_w_up, moe_w_down, p_2, positions_2, ab_w_in_2, ab_q_norm_2, ab_w_q_up_2,
    ab_kv_norm_2, ab_w_kv_up_2, ab_w_out_2, c_w_qkv_2, c_lambda_2, c_subln_2, c_w_out_2,
    ln_mix_g_2, ln_mix_b_2, ffn_w_gate_2, ffn_w_up_2, ffn_conv_w_2, ffn_conv_b_2, ffn_w_down_2,
    ln_ffn_g_2, ln_ffn_b_2, ple_w_gate_2, ple_w_proj_2,
):
    x = first_block(
        x, c, ctx, c_ctx, w_mod, b_mod, norm1_g, norm2_g, w_in, q_norm_g, k_norm_g, gla_wa2,
        gla_ba, gla_norm_g, hy_conv_w, hy_conv_b, hy_pos_w1, hy_pos_b1, hy_sin_freq, hy_pos_w2,
        hy_pos_b2, hy_pos_w3, hy_decay, hy_skip, w_br_hy, w_br_gla, w_br_att, w_out, router_w,
        router_b, moe_w_gate, moe_w_up, moe_w_down,
    )
    return second_block(
        x, p_2, positions_2, ab_w_in_2, ab_q_norm_2, ab_w_q_up_2, ab_kv_norm_2, ab_w_kv_up_2,
        ab_w_out_2, c_w_qkv_2, c_lambda_2, c_subln_2, c_w_out_2, ln_mix_g_2, ln_mix_b_2,
        ffn_w_gate_2, ffn_w_up_2, ffn_conv_w_2, ffn_conv_b_2, ffn_w_down_2, ln_ffn_g_2,
        ln_ffn_b_2, ple_w_gate_2, ple_w_proj_2,
    )


_drawn_inputs = setup_inputs


def setup_inputs(seed=0):
    import zlib

    import numpy as np

    out = dict(_drawn_inputs(seed))
    spreads = {}
    factors = {'q_norm_g': 8.0,
     'k_norm_g': 8.0,
     'gla_ba': 8.0,
     'gla_norm_g': 5.134,
     'hy_conv_b': 4.454,
     'hy_pos_b1': 8.0,
     'hy_sin_freq': 8.0,
     'hy_pos_b2': 5.719,
     'hy_decay': 2.85,
     'ab_q_norm_2': 8.0,
     'ab_kv_norm_2': 8.0,
     'c_subln_2': 8.0,
     'ffn_conv_b_2': 8.0}
    for name, (base, spread) in spreads.items():
        noise = np.random.default_rng([zlib.crc32(name.encode()), seed]).standard_normal(out[name].shape)
        drawn = base * np.exp(spread * noise) if base else spread * noise
        out[name] = jnp.asarray(drawn.astype(out[name].dtype))
    for name, factor in factors.items():
        out[name] = (out[name] * factor).astype(out[name].dtype)
    return out
```

```python
from collections import namedtuple
from contextlib import ExitStack
import math

import numpy as np

import concourse.bass as bass
from concourse import mybir

F32 = mybir.dt.float32
I32 = mybir.dt.int32
ALU = mybir.AluOpType
ACT = mybir.ActivationFunctionType
AX = mybir.AxisListType

Tok = namedtuple("Tok", "sem n")

NT = 256
EPS = 1e-6
ALPHA = 4 ** 0.25
LAMBDA_INIT = 0.8 - 0.6 * math.exp(-0.3)
SLOTS = 5
SLOT = 4096
ARENA = 22800
MAGIC = 12582912.0
TWO_PI = 2 * math.pi
C1 = 6.28125
C2 = float(np.float32(math.floor((TWO_PI - C1) * 2 ** 20) / 2 ** 20))
C3 = float(np.float32(TWO_PI - C1 - C2))
PI_F = float(np.nextafter(np.float32(math.pi), np.float32(0)))

VECS = [("b_mod", 48), ("norm1_g", 8), ("norm2_g", 8), ("q_norm_g", 1), ("k_norm_g", 1), ("gla_norm_g", 1),
        ("hy_conv_w", 36), ("hy_conv_b", 12), ("hy_skip", 8), ("ab_q_norm_2", 3), ("ab_kv_norm_2", 2),
        ("c_subln_2", 1), ("ln_mix_g_2", 16), ("ln_mix_b_2", 16), ("ffn_conv_w_2", 132),
        ("ffn_conv_b_2", 44), ("ln_ffn_g_2", 16), ("ln_ffn_b_2", 16)]
VOFF = {}
_n = 0
for _name, _k in VECS:
    VOFF[_name] = _n
    _n += _k
NV = _n


class Lane:

    def __init__(self, sem):
        self.sem, self.n, self.queue = sem, 0, []

    def __call__(self, emit, *after):
        self.queue.append((emit, after, self.sem, 1))
        self.n += 1
        return Tok(self.sem, self.n)

    def dma(self, emit, sem, *after):
        self.queue.append((emit, after, sem, 16))

    def wait(self, *after):
        self.queue.append((None, after, None, 0))

    def now(self):
        return Tok(self.sem, self.n)

    def run(self, eng):
        seen = {}

        def hold(t):
            if isinstance(t, Tok):
                if t.n > seen.get(id(t.sem), 0):
                    eng.wait_ge(t.sem, t.n)
                    seen[id(t.sem)] = t.n
            else:
                for u in t:
                    hold(u)

        for emit, after, sem, k in self.queue:
            hold(after)
            if emit is not None:
                emit(eng).then_inc(sem, k)


def shape_constants():
    f = np.float32
    i = np.arange(128)
    s, t = i[:, None], i[None, :]
    same = (s // 64) == (t // 64)
    out = {"ident": np.eye(128), "ones": np.ones((128, 128)),
           "Tf": (s <= t) & same, "Tb": (s >= t) & same,
           "SGf": (s > t) & same, "SGb": (s < t) & same, "SFf": s > t, "SFb": s < t}
    rax = np.zeros((128, 128))
    rax[i[1::2], i[0::2]] = -1
    rax[i[0::2], i[1::2]] = 1
    ra = np.zeros((128, 128))
    for b in (0, 64):
        for k in range(8):
            ra[b + 8 + k, b + k] = -1
            ra[b + k, b + 8 + k] = 1
    rb = np.zeros((128, 128))
    for k in range(16):
        rb[80 + k, 64 + k] = -1
        rb[64 + k, 80 + k] = 1
    out |= {"Rax": rax, "Ra": ra, "Rb": rb}
    tok = np.arange(NT)
    inv = np.power(f(10000.0), -np.arange(32, dtype=f) / f(32)).astype(f)
    ang = np.concatenate([(tok // 64).astype(f)[:, None] * inv, (tok % 64).astype(f)[:, None] * inv], axis=1)
    ang = np.repeat(ang, 2, axis=1).T.astype(np.float64)
    out |= {"cosx": np.cos(ang), "sinx": np.sin(ang)}
    fa = 1.0 / np.power(f(500000.0), np.arange(0, 16, 2, dtype=f) / f(16))
    fb = 1.0 / np.power(f(500000.0), np.arange(0, 32, 2, dtype=f) / f(32))
    fq = np.zeros((128, 2))
    for b in (0, 8, 64, 72):
        fq[b:b + 8, 0] = fa
    for b in (64, 80):
        fq[b:b + 16, 1] = fb
    tn = np.stack([-(i / 256.0), -((i + 128) / 256.0)], axis=1)
    out |= {"freq": fq, "negt": tn, "row0": (i > 0)[:, None] * 1.0,
            "rank": np.tile(16.0 - np.arange(16), (128, 1))}
    small = ["ident", "ones", "Tf", "Tb", "SGf", "SGb", "SFf", "SFb", "Rax", "Ra", "Rb", "cosx", "sinx",
             "freq", "negt", "row0", "rank"]
    at, n = {}, 0
    for k in small:
        at[k] = (n, out[k].shape[1])
        n += out[k].shape[1]
    consts = np.concatenate([np.asarray(out[k], f) for k in small], axis=1)

    m = np.arange(256)[:, None]
    k = np.arange(256)[None, :]
    w = 2 * np.pi * ((m * k) % 512) / 512
    cos, sin = np.cos(w), np.sin(w)
    alt = 1.0 - 2.0 * (m[:, 0] % 2)
    nyq_i = -sin[:, :128].copy()
    nyq_i[:, 0] = alt
    nyq_r = cos[:, :128].copy()
    nyq_r[:, 0] = alt
    fwd = np.concatenate([cos, -sin, nyq_i, nyq_r], axis=1)
    fwd = fwd.reshape(2, 128, 768).transpose(1, 0, 2).reshape(128, 1536)
    gr = 2 * cos.T / 512
    gr[0] /= 2
    gi = -2 * sin.T / 512
    gi[0] = alt / 512
    inv_t = np.concatenate([gr, gi], axis=0).reshape(4, 128, 256).transpose(1, 0, 2).reshape(128, 1024)
    dft = np.concatenate([fwd, inv_t], axis=1).astype(f)

    q = np.arange(128)[:, None, None] + 128 * np.arange(2)[None, :, None]
    d = np.abs(q - np.arange(256)[None, None, :])
    count = (d <= 64) * 1.0 + (d % 4 == 0) + (d % 16 == 0)
    neg = np.where(count > 0, 0.0, -1e30)
    mask = np.concatenate([count.reshape(128, 512), neg.reshape(128, 512)], axis=1).astype(f)
    sel = np.zeros((16, 16, 128), f)
    for e in range(16):
        sel[e, e] = 1
    t = np.arange(256, dtype=f)
    bands = np.linspace(1e-4, 15, 16, dtype=f)
    phase = f(2 * math.pi / 256) * t[:, None] * bands[None, :]
    z = np.concatenate([(t / f(256))[:, None], np.cos(phase), -np.sin(phase)], axis=-1)
    return consts, at, dft, mask, sel.reshape(16, 2048), np.ascontiguousarray(z.T.astype(f))


CONSTS, CAT, DFT, AMASK, SEL, POSEMB = shape_constants()


def build(nc, D, out, probe=()):
    ctx = ExitStack()
    sem = lambda name: ctx.enter_context(nc.semaphore(name))
    PE, V, A, G, SP = (Lane(sem(n)) for n in ("s_pe", "s_dve", "s_act", "s_pool", "s_sp"))
    lanes = (PE, V, A, G)

    def sb(name, cols, parts=128):
        return ctx.enter_context(nc.sbuf_tensor(name, [parts, cols], F32))

    ring = [sb(f"ring{i}", SLOT) for i in range(SLOTS)]
    cst = sb("cst", CONSTS.shape[1])
    vec = sb("vec", NV)
    XT_ = sb("XT", 2048)
    HC_ = sb("HC", 4096)
    modt = sb("mod", 96)
    stat = sb("stat", 1200)
    arena = sb("arena", ARENA)
    bank = [ctx.enter_context(nc.psum_tensor(f"bank{i}", [128, 512], F32)) for i in range(8)]
    XT = XT_[:, :].rearrange("p (k t) -> p k t", k=8)
    HC = HC_[:, :].rearrange("p (k t) -> p k t", k=8)
    mark = [0]

    def mem(cols, split=None):
        o = mark[0]
        mark[0] += cols
        assert mark[0] <= ARENA, mark[0]
        ap = arena[:, o:o + cols]
        return ap if split is None else ap.rearrange("p (a b) -> p a b", a=split)

    st_at = [0]

    def cols(n):
        o = st_at[0]
        st_at[0] += n
        assert st_at[0] <= 1200
        return stat[:, o:o + n]

    def C(name):
        o, n = CAT[name]
        return cst[:, o:o + n]

    def vcol(name, i=0, n=1):
        return vec[:, VOFF[name] + i:VOFF[name] + i + n]

    def wide(ap, n):
        return ap.unsqueeze(1).broadcast_to([ap.shape[0], n, ap.shape[1]])

    def long(ap, n):
        return ap.unsqueeze(2).broadcast_to([ap.shape[0], ap.shape[1], n])

    read = [()] * 8
    turn = [0]

    def pick(among=(4, 5, 6, 7)):
        turn[0] += 1
        return among[turn[0] % len(among)]

    ring_sem = [sem(f"s_ring{i}") for i in range(SLOTS)]
    ring_use = [0] * SLOTS
    ring_free = [()] * SLOTS
    loads = [0]

    def load(src, view):
        i = loads[0] % SLOTS
        loads[0] += 1
        assert ring_free[i] is not None
        ring_use[i] += 1
        dst = view(ring[i])
        SP.dma(lambda e: e.dma_start(dst, src), ring_sem[i], ring_free[i])
        ring_free[i] = None
        return dst, Tok(ring_sem[i], 16 * ring_use[i]), i

    def done(slot, *toks):
        ring_free[slot] = toks

    def col_block(w, c0, n, nk=8):
        return load(w[:, c0:c0 + n].rearrange("(k p) n -> p k n", p=128),
                    lambda r: r[:, 0:nk * n].rearrange("p (k n) -> p k n", k=nk))

    def row_block(w, r0, nk, n=1024):
        return load(w[r0 * 128:(r0 + nk) * 128, :].rearrange("(k p) n -> p k n", p=128),
                    lambda r: r[:, 0:nk * n].rearrange("p (k n) -> p k n", k=nk))

    def fetch(dst, src, lane, name):
        s = sem(name)
        lane.dma(lambda e: e.dma_start(dst, src), s)
        return Tok(s, 16)

    def handover():
        t = [x.now() for x in lanes]
        for x in lanes:
            x.wait(t)
        return t

    out_sems = []

    def dump(name, ap, *after):
        if name in probe:
            s = sem("d_" + name)
            dst = probe[name](ap.shape)
            G.dma(lambda e: e.dma_start(dst, ap), s, *after)
            G.wait(Tok(s, 16))

    def vtt(o, a, b, op, *after):
        return V(lambda e: e.tensor_tensor(o, a, b, op), *after)

    def vts(o, a, s1, s2, op0, op1, *after):
        if s2 is None:
            return V(lambda e: e.tensor_scalar(o, a, s1, None, op0), *after)
        return V(lambda e: e.tensor_scalar(o, a, s1, s2, op0, op1), *after)

    def stt(o, a, s, b, op0, op1, *after):
        return V(lambda e: e.scalar_tensor_tensor(out=o, in0=a, scalar=s, in1=b, op0=op0, op1=op1), *after)

    def vcopy(o, a, *after):
        return V(lambda e: e.tensor_copy(o, a), *after)

    def act(o, a, f, *after, **kw):
        return A(lambda e: e.activation(o, a, f, **kw), *after)

    def mms(jobs, *after):
        def emit(e):
            for o, l, r, s0, s1 in jobs:
                last = e.matmul(o, l, r, start=s0, stop=s1, skip_group_check=True)
            return last
        return PE(emit, *after)

    def chain(o, pairs):
        n = len(pairs)
        return [(o, l, r, i == 0, i == n - 1) for i, (l, r) in enumerate(pairs)]

    def turned(jobs, *after):
        def emit(e):
            for o, i in jobs:
                last = e.transpose(o, i, C("ident")[0:i.shape[0], 0:i.shape[0]])
            return last
        return PE(emit, *after)

    def inv_root(sums, n, d, eps, dst, *after):
        t = vts(dst, sums, 1.0 / d, eps, ALU.mult, ALU.add, *after)
        t2 = act(dst, dst, ACT.Sqrt, t)
        return t, V(lambda e: e.reciprocal(dst, dst), t2)

    def ones_sum(srcs, n, b, *after):
        return mms(chain(bank[b][:, 0:n], [(C("ones"), s) for s in srcs]), *after, read[b])

    t_cst = fetch(cst[:, :], D["consts"], A, "s_cst")
    t_vec = fetch(vec[:, :], D["vecs"], A, "s_vec")

    YHY = mem(1024, 4)
    keep_y = mark[0]
    cc = mem(16)
    sc = mem(16, 8)
    t_cc = fetch(cc, D["cc"], A, "s_cc")
    XC = mem(2048, 8)
    t_x = fetch(XT, D["xT"], A, "s_x")
    t_xc = fetch(XC, D["ctxT"], A, "s_xc")
    HF = mem(5120)
    DF = mem(2560)
    t_dft = fetch(DF, D["dft"], A, "s_dft")
    DFf = DF[:, 0:1536].rearrange("p (k n) -> p k n", k=2)
    DFi = DF[:, 1536:2560].rearrange("p (k n) -> p k n", k=4)
    keep_after_filters = mark[0]

    w3 = mem(2048)
    t_w3 = fetch(w3[0:64, :], D["hy_pos_w3"], A, "s_w3")
    dec = mem(4096, 2)
    dcy = mem(2048)
    t_dcy = fetch(dcy, D["hy_decay"].partition_broadcast(128), A, "s_dcy")
    w1 = mem(64)
    t_w1 = fetch(w1[0:33, :], D["hy_pos_w1"], A, "s_w1")
    w2 = mem(64)
    t_w2 = fetch(w2[0:64, :], D["hy_pos_w2"], A, "s_w2")
    h64 = mem(3)
    t_h64 = fetch(h64[0:64, :], D["hy64"], A, "s_h64")
    pemb = mem(256)
    t_pe = fetch(pemb[0:33, :], D["posemb"], A, "s_pemb")

    t_sc = act(sc.rearrange("p k c -> p (k c)"), cc, ACT.Silu, t_cc)

    def mod_chunk(c):
        w, tw, s = col_block(D["w_mod"], 512 * c, 512)
        jobs = []
        for m in range(4):
            o = 2 * (4 * c + m)
            jobs += chain(bank[0][:, o:o + 2], [(w[:, k, m * 128:m * 128 + 128], sc[:, k, :]) for k in range(8)])
        t = mms(jobs, tw, t_sc)
        done(s, t)
        return t

    def reduce_angle(r, a, k, *after):
        t = vts(k, a, 1 / TWO_PI, MAGIC, ALU.mult, ALU.add, *after)
        t = vts(k, k, MAGIC, None, ALU.subtract, None, t)
        t = stt(r, k, -C1, a, ALU.mult, ALU.add, t)
        t = stt(r, k, -C2, r, ALU.mult, ALU.add, t)
        return stt(r, k, -C3, r, ALU.mult, ALU.add, t)

    ang = mem(256)
    kk = mem(256)
    hid = mem(256)
    for c in range(3):
        mod_chunk(c)
    t = mms(chain(bank[4][0:64, 0:256], [(w1[0:33, :], pemb[0:33, :])]), t_w1, t_pe)
    for layer in range(2):
        b = 4 + layer
        t = vts(ang[0:64, :], bank[b][0:64, 0:256], h64[0:64, 2 * layer:2 * layer + 1] if layer else h64[0:64, 0:1],
                h64[0:64, 1:2], ALU.add, ALU.mult, t, t_h64)
        t = reduce_angle(ang[0:64, :], ang[0:64, :], kk[0:64, :], t)
        t = vts(ang[0:64, :], ang[0:64, :], PI_F, -PI_F, ALU.min, ALU.max, t)
        t = act(hid[0:64, :], ang[0:64, :], ACT.Sin, t)
        if layer == 0:
            t = mms(chain(bank[5][0:64, 0:256], [(w2[0:64, :], hid[0:64, :])]), t, t_w2)
    dump("hid", hid[0:64, :], t)
    t_hid = t
    t = act(dcy, dcy, ACT.Abs, t_dcy)
    t_dec = []
    for i in range(2):
        t_dec.append(act(dec[:, i, :], dcy, ACT.Exp, t, t_cst, scale=C("negt")[:, i:i + 1]))
    F = HC_[:, :].rearrange("p (i n) -> p i n", i=2)
    t_f = []
    for i in range(2):
        for q in range(4):
            b = pick()
            if (i, q) in ((0, 0), (0, 2), (1, 0), (1, 2)):
                mod_chunk(3 + i * 2 + q // 2)
            t = mms(chain(bank[b][:, :], [(hid[0:64, i * 128:i * 128 + 128], w3[0:64, q * 512:q * 512 + 512])]),
                    t_hid, t_w3, read[b])
            dst, dd = F[:, i, q * 512:q * 512 + 512], dec[:, i, q * 512:q * 512 + 512]
            if i == 0 and q % 2 == 1:
                t = stt(dst, bank[b][:, :], C("row0"), dd, ALU.mult, ALU.mult, t, t_dec[i])
            else:
                t = vtt(dst, bank[b][:, :], dd, ALU.mult, t, t_dec[i])
            read[b] = (t,)
            t_f.append(t)
    last_filter = PE.now()
    PM = dec[:, :, :].rearrange("p i n -> p (i n)").rearrange("p (s i o n) -> p s i o n", s=2, i=2, o=2)
    AB = w3.rearrange("p (i d n) -> p i d n", i=2, d=2)
    recn = cols(1)
    rec = dcy[:, 0:512]
    t_abs_read = last_filter
    hf_off = {"A0": 0, "A1": 1, "B0": 2, "B1": 3, "D0": 4}

    def Hf(o, name):
        k = 5 * o + hf_off[name]
        return HF[:, 512 * k:512 * k + 512]

    t_hf = []
    t_rec_free = ()
    for o in range(2):
        fwd = [F[:, i, (2 * o) * 512:(2 * o) * 512 + 512] for i in range(2)]
        bwd = [F[:, i, (2 * o + 1) * 512:(2 * o + 1) * 512 + 512] for i in range(2)]
        t_ab = [act(AB[:, i, d, :], (fwd, bwd)[d][i], ACT.Abs, t_f, t_abs_read) for i in range(2) for d in range(2)]
        b = pick()
        t = ones_sum([AB[:, i, d, :] for i in range(2) for d in range(2)], 512, b, t_ab, t_cst)
        t_abs_read = t
        t = vts(rec, bank[b][:, :], EPS, None, ALU.add, None, t, t_rec_free, t_dec)
        read[b] = (t,)
        t_rec = V(lambda e: e.reciprocal(rec, rec), t)
        t_pm = []
        for i in range(2):
            for s, op in ((0, ALU.add), (1, ALU.subtract)):
                t = vtt(PM[:, s, i, o, :], fwd[i], bwd[i], op, t_f)
                t_pm.append(vtt(PM[:, s, i, o, :], PM[:, s, i, o, :], rec, ALU.mult, t, t_rec))
        t_rec_free = t_pm[-1]
        mod_chunk(7 + 2 * o)
        for name, c0, s in (("A0", 0, 0), ("A1", 128, 0), ("B0", 256, 1), ("B1", 384, 1), ("D0", 640, 0)):
            b = pick()
            t = mms(chain(bank[b][:, :], [(DFf[:, i, c0:c0 + 128], PM[:, s, i, o, :]) for i in range(2)]),
                    t_pm, t_dft, read[b])
            t = act(Hf(o, name), bank[b][:, :], ACT.Copy, t)
            read[b] = (t,)
            t_hf.append(t)
        mod_chunk(8 + 2 * o)
    dump("HF", HF[:, :], t_hf)
    t = mod_chunk(11)
    mod = modt[:, :].rearrange("p (m c) -> p m c", c=2)
    t_mod = vtt(mod, bank[0][:, 0:96].rearrange("p (m c) -> p m c", c=2), long(vcol("b_mod", 0, 48), 2), ALU.add,
                t, t_vec)
    read[0] = (t_mod,)
    dump("mod", modt[:, :], t_mod)

    handover()
    mark[0] = keep_after_filters

    T1 = mem(2048, 8)
    SR = mem(512)
    scl = cols(24)

    def modulated(X, n_x, scale_cols, gname, shift, dst, *after):
        t_s = stt(scale_cols, shift[1], 1.0, vcol(gname, 0, 8), ALU.add, ALU.mult, t_mod, *after)
        t = act(T1, X, ACT.Square, *after)
        b = pick()
        t = ones_sum([T1[:, k, :] for k in range(8)], NT, b, t, t_cst)
        t_r, t = inv_root(bank[b][:, 0:NT], NT, 1024, EPS, SR[:, n_x * NT:n_x * NT + NT], t)
        read[b] = (t_r,)
        t = vtt(T1, X, wide(SR[:, n_x * NT:n_x * NT + NT], 8), ALU.mult, t)
        for k in range(8):
            t_o = vts(dst[:, k, :], T1[:, k, :], scale_cols[:, k:k + 1], shift[0][:, k:k + 1], ALU.mult, ALU.add,
                      t, t_s)
        return t_o

    t_h = modulated(XT, 0, scl[:, 0:8], "norm1_g", (mod[:, 0:8, 0], mod[:, 8:16, 0]), HC[:, :, 0:256], t_x)
    t_hc = modulated(XC, 1, scl[:, 8:16], "norm1_g", (mod[:, 0:8, 1], mod[:, 8:16, 1]), HC[:, :, 256:512], t_xc, t_h)
    dump("HC", HC_[:, :], t_hc)
    XCv = XC

    def project(w, tw, X, nk, tiles, n, evac, *after, banks=(4, 5, 6, 7)):
        per = 512 // n
        for m0 in range(0, tiles, per):
            b = pick(banks)
            jobs = []
            for m in range(m0, min(m0 + per, tiles)):
                o = (m - m0) * n
                jobs += chain(bank[b][:, o:o + n],
                              [(w[:, k, m * 128:m * 128 + 128], X[:, k, 0:n]) for k in range(nk)])
            t = mms(jobs, tw, after, read[b])
            read[b] = evac(m0, b, t)
        return t

    W = D["w_in"]
    HX = HC[:, :, 0:256]

    UV = mem(3072, 12)
    t_uv = []

    def conv_evac(base):
        def evac(m0, b, t):
            ts, t1 = [], []
            for j in range(2):
                m = base + m0 + j
                t1.append(act(UV[:, m, :], bank[b][:, j * 256:j * 256 + 256], ACT.Identity, t,
                              scale=vcol("hy_conv_w", 12 + m), bias=vcol("hy_conv_b", m)))
            for j in range(2):
                m = base + m0 + j
                src = bank[b][:, j * 256:j * 256 + 256]
                dst = UV[:, m, :]
                t2 = stt(dst[:, 1:256], src[:, 0:255], vcol("hy_conv_w", m), dst[:, 1:256], ALU.mult, ALU.add, t1)
                t3 = stt(dst[:, 0:255], src[:, 1:256], vcol("hy_conv_w", 24 + m), dst[:, 0:255], ALU.mult, ALU.add, t2)
                ts.append(t3)
            t_uv.extend(ts)
            return tuple(ts)
        return evac

    for c in (2, 0, 1):
        w, tw, s = col_block(W, 3104 + 512 * c, 512)
        t = project(w, tw, HX, 8, 4, 256, conv_evac(4 * c), t_h, t_vec)
        done(s, t)
    dump("UV", UV, t_uv)

    ZT = mem(1024, 2)
    XF = mem(2048, 4)
    YF = mem(2048, 4)
    TP = mem(512)
    hy = {}

    def hyena_spectrum(o, z, *after):
        tz = []
        for i in range(2):
            b = pick()
            t = turned([(bank[b][:, c * 128:c * 128 + 128], z[:, c, i * 128:i * 128 + 128]) for c in range(4)],
                       *after, t_cst, read[b])
            t = act(ZT[:, i, :], bank[b][:, :], ACT.Copy, t, hy.get("zt", ()))
            read[b] = (t,)
            tz.append(t)
        tx = []
        for j, c0 in enumerate((0, 128, 512, 384)):
            b = pick()
            t = mms(chain(bank[b][:, :], [(DFf[:, i, c0:c0 + 128], ZT[:, i, :]) for i in range(2)]), tz, read[b])
            hy["zt"] = t
            t = act(XF[:, j, :], bank[b][:, :], ACT.Copy, t, hy.get("xf", ()))
            read[b] = (t,)
            tx.append(t)
        ty = []
        for j in range(2):
            R, I = XF[:, j, :], XF[:, 2 + j, :]
            a, bb = Hf(o, f"A{j}"), Hf(o, f"B{j}")
            d = Hf(o, "D0") if j == 0 else a
            t = vtt(YF[:, j, :], R, a, ALU.mult, tx, hy.get("yf", ()))
            t2 = vtt(TP, I, bb, ALU.mult, t)
            t = vtt(YF[:, j, :], YF[:, j, :], TP, ALU.subtract, t2)
            t2 = vtt(YF[:, 2 + j, :], R, bb, ALU.mult, t)
            t3 = vtt(TP, I, d, ALU.mult, t2)
            t4 = vtt(YF[:, 2 + j, :], YF[:, 2 + j, :], TP, ALU.add, t3)
            ty += [t, t4]
        hy["xf"] = t4
        return ty

    def hyena_back(o, z, gate, dst, ty):
        res = []
        for c0 in (0, 2):
            b = pick()
            jobs = []
            for c in (c0, c0 + 1):
                jobs += chain(bank[b][:, (c - c0) * 256:(c - c0) * 256 + 256],
                              [(YF[:, j, c * 128:c * 128 + 128], DFi[:, j, :]) for j in range(4)])
            t = mms(jobs, ty, read[b])
            hy["yf"] = t
            rs = []
            for c in (c0, c0 + 1):
                t1 = stt(z[:, c, :], z[:, c, :], vcol("hy_skip", 4 * o + c),
                         bank[b][:, (c - c0) * 256:(c - c0) * 256 + 256], ALU.mult, ALU.add, t)
                rs.append(t1)
                res.append(vtt(dst[:, c, :], z[:, c, :], gate[:, c, :], ALU.mult, t1))
            read[b] = tuple(rs)
        return res

    z = UV[:, 8:12, :]
    ty = hyena_spectrum(0, z, t_uv)
    tz1 = hyena_back(0, z, UV[:, 0:4, :], z, ty)
    ty = hyena_spectrum(1, z, tz1)
    t_yhy = hyena_back(1, z, UV[:, 4:8, :], YHY, ty)
    dump("YHY", YHY, t_yhy)

    handover()
    mark[0] = keep_y
    YATT = mem(2048, 8)
    keep_y = mark[0]
    KT = mem(1024, 2)
    VV = mem(1024, 4)
    QT = mem(2048, 8)
    RW = mem(512)
    RQ = mem(512)
    RR = mem(512)
    RN = mem(512)
    RC = mem(512)

    hn = {"free": ()}

    def rope(src, n, R, cos, sin, dst, parts, *after, rows=None):
        lo, hi = rows or (0, parts)
        b = pick()
        t = mms(chain(bank[b][0:parts, 0:n * 256], [(R, src)]), *after, read[b])
        s3 = src.rearrange("p (n t) -> p n t", n=n)
        c3 = RC[:, 0:n * 256].rearrange("p (n t) -> p n t", n=n)
        b3 = bank[b][:, 0:n * 256].rearrange("p (n t) -> p n t", n=n)
        t1 = vtt(c3[lo:hi], b3[lo:hi], wide(sin[lo:hi, :], n), ALU.mult, t, hn.get("rc", ()))
        read[b] = (t1,)
        t2 = vtt(dst[lo:hi], s3[lo:hi], wide(cos[lo:hi, :], n), ALU.mult, t1, *after)
        t3 = vtt(dst[lo:hi], dst[lo:hi], c3[lo:hi], ALU.add, t2)
        hn["rc"] = t3
        return t3, t

    def head_norm(b, tok, gcol, dst, n, d=128, eps=EPS):
        t1 = act(RQ[:, 0:n], bank[b][:, 0:n], ACT.Square, tok, hn.get("rq", ()))
        b2 = pick()
        t = ones_sum([RQ[:, 0:n]], n, b2, t1, t_cst)
        hn["rq"] = t
        t_r, t = inv_root(bank[b2][:, 0:n], n, d, eps, RR[:, 0:n], t, hn.get("rr", ()))
        read[b2] = (t_r,)
        t = stt(dst, bank[b][:, 0:n], gcol, RR[:, 0:n], ALU.mult, ALU.mult, t, hn.get("rn", ()))
        hn["rr"] = t
        return t

    w, tw, s = col_block(W, 0, 512)
    t_k = []
    for h in range(2):
        b = pick()
        t = mms(chain(bank[b][:, :], [(w[:, k, h * 128:h * 128 + 128], HC[:, k, :]) for k in range(8)]),
                tw, t_h, t_hc, read[b])
        t = head_norm(b, t, vcol("k_norm_g"), RN, 512)
        read[b] = (t,)
        t1, t2 = rope(RN[:, 0:256], 1, C("Rax"), C("cosx"), C("sinx"), KT[:, h:h + 1, 0:256], 128, t)
        t3 = vcopy(KT[:, h, 256:512], RN[:, 256:512], t)
        hn["rn"] = (t1, t2, t3)
        t_k += [t1, t3]
    t_v = []
    for i0 in (0, 2):
        b = pick()
        jobs = []
        for i in (i0, i0 + 1):
            jobs += chain(bank[b][:, (i - i0) * 256:(i - i0) * 256 + 256],
                          [(HC[:, k, i * 128:i * 128 + 128], w[:, k, 256:512]) for k in range(8)])
        t = mms(jobs, read[b])
        done(s, t)
        t = act(VV[:, i0:i0 + 2, :], bank[b][:, :].rearrange("p (i n) -> p i n", i=2), ACT.Copy, t)
        read[b] = (t,)
        t_v.append(t)
    t_q = []
    for c in range(2):
        w, tw, s = col_block(W, 1312 + 512 * c, 512)

        def evac(m0, b, t, c=c):
            t = head_norm(b, t, vcol("q_norm_g"), RN, 512)
            m = 4 * c + m0
            t1, t2 = rope(RN, 2, C("Rax"), C("cosx"), C("sinx"), QT[:, m:m + 2, :], 128, t)
            hn["rn"] = (t1, t2)
            t_q.append(t1)
            return (t,)
        t = project(w, tw, HX, 8, 4, 256, evac, t_h)
        done(s, t)
    dump("KT", KT, t_k)
    dump("QT", QT, t_q)

    E_ = [mem(512), mem(512)]
    PT_ = [mem(512), mem(512)]
    E2_ = [mem(512), mem(512)]
    at = {}

    def softmax(u, b, tok, g, scale, masked=False, E=None, key="e", factor=None):
        n = 512 // g
        c = cols(4 * g)
        mx, nm, l, r = (c[:, g * i:g * i + g] for i in range(4))
        src = bank[b][:, :].rearrange("p (g n) -> p g n", g=g)
        e3 = E.rearrange("p (g n) -> p g n", g=g)
        held = at.get((key, u % 2), ())
        if masked:
            tok = stt(E, bank[b][:, :], scale, AM[:, 512:1024], ALU.mult, ALU.add, tok, held)
            read[b] = (tok,)
            src, scale = e3, 1.0
        t = V(lambda e: e.tensor_reduce(mx, src, AX.X, ALU.max), tok)
        t = vts(nm, mx, -scale, None, ALU.mult, None, t)
        te = []
        for i in range(g):
            kw = {} if masked else {"accum_out": l[:, i:i + 1]}
            te.append(A(lambda e, i=i, kw=kw: e.activation(e3[:, i, :], src[:, i, :], ACT.Exp, bias=nm[:, i:i + 1],
                                                         scale=scale, **kw), t, held))
        if not masked:
            read[b] = (te[-1], t)
        if masked:
            t = vtt(E, E, AM[:, 0:512], ALU.mult, te)
            t = V(lambda e: e.tensor_reduce(l, e3, AX.X, ALU.add), t)
        else:
            t = te
        t = V(lambda e: e.reciprocal(r, l), t)
        if factor is not None:
            t = vts(r, r, factor, None, ALU.mult, None, t)
        for i in range(g):
            t2 = vts(e3[:, i, :], e3[:, i, :], r[:, i:i + 1], None, ALU.mult, None, t)
        return t2

    def flip(u, E, tok, order):
        b = 6 + u % 2
        t = turned([(bank[b][:, j * 128:j * 128 + 128], E[:, o * 128:o * 128 + 128]) for j, o in enumerate(order)],
                   tok, t_cst, read[b])
        at[("e", u % 2)] = t
        t = act(PT_[u % 2], bank[b][:, :], ACT.Copy, t, at.get(("pt", u % 2), ()))
        read[b] = (t,)
        return t

    def staged(n, first, second, third):
        a, b = {}, {}
        for i in range(n + 2):
            if i < n:
                a[i] = first(i)
            if 1 <= i <= n:
                b[i - 1] = second(i - 1, a[i - 1])
            if i >= 2:
                third(i - 2, b[i - 2])

    t_yatt = []

    def first(u):
        h, i = u // 2, u % 2
        b = 4 + u % 2
        t = mms(chain(bank[b][:, :], [(QT[:, h, i * 128:i * 128 + 128], KT[:, h // 4, :])]), t_q, t_k, read[b])
        return softmax(u, b, t, 1, 128 ** -0.5, E=E_[u % 2])

    def second(u, t):
        return flip(u, E_[u % 2], t, (0, 1, 2, 3))

    def third(u, t):
        h, i = u // 2, u % 2
        b = u % 4
        PT = PT_[u % 2]
        t = mms(chain(bank[b][:, 0:128], [(VV[:, j, (h // 4) * 128:(h // 4) * 128 + 128], PT[:, j * 128:j * 128 + 128])
                                          for j in range(4)]), t, t_v, read[b])
        at[("pt", u % 2)] = t
        t = act(YATT[:, h, i * 128:i * 128 + 128], bank[b][:, 0:128], ACT.Copy, t)
        read[b] = (t,)
        t_yatt.append(t)

    staged(16, first, second, third)
    dump("YATT", YATT, t_yatt)

    handover()
    mark[0] = keep_y
    YGLA = mem(1024, 4)
    keep_y = mark[0]
    GKT = mem(1024, 2)
    GKK = mem(1024, 4)
    GV = mem(2048, 4)
    GA = mem(512)
    GQ = mem(512, 2)
    OG = mem(1024, 4)
    LA = mem(2048, 4)
    W2 = mem(512)
    EP = mem(1024).rearrange("p (d j t) -> p d j t", d=2, j=2)
    EN = mem(1024).rearrange("p (d j t) -> p d j t", d=2, j=2)
    KE = mem(2048).rearrange("p (i d f) -> p i d f", i=4, d=2)
    SS = mem(2048).rearrange("p (d j c v) -> p d j c v", d=2, j=2, c=4)
    AT = [mem(512), mem(512)]
    RQ, RR = mem(512), mem(512)
    hn = {}
    hand = [x.now() for x in lanes]
    s_w2 = sem("s_w2z")
    G.dma(lambda e: e.dma_start(W2[0:33, :], D["w2z"]), s_w2, hand)
    t_w2z = Tok(s_w2, 16)
    t_one = V(lambda e: e.memset(GA[32:33, :], 1.0))

    w, tw, s = col_block(W, 1024, 288)
    b = pick()
    t = mms(chain(bank[b][0:32, :], [(w[:, k, 256:288], HC[:, k, :]) for k in range(8)]), tw, read[b])
    t_ga = act(GA[0:32, :], bank[b][0:32, :], ACT.Copy, t)
    read[b] = (t_ga,)
    t_gv = []

    def token_major(w, c0, n, dst_fn, *after):
        for i0 in (0, 2):
            b = pick()
            jobs = []
            for i in (i0, i0 + 1):
                jobs += chain(bank[b][:, (i - i0) * n:(i - i0) * n + n],
                              [(HC[:, k, i * 128:i * 128 + 128], w[:, k, c0:c0 + n]) for k in range(8)])
            t_m = mms(jobs, *after, read[b])
            t = act(dst_fn(i0), bank[b][:, 0:2 * n].rearrange("p (i n) -> p i n", i=2), ACT.Copy, t_m)
            read[b] = (t,)
            t_gv.append(t)
        return t_m

    t = token_major(w, 0, 256, lambda i: GV[:, i:i + 2, 256:512], tw)
    done(s, t)
    w, tw, s = col_block(W, 512, 512)
    t_gk = []
    for j in range(2):
        b = pick()
        t = mms(chain(bank[b][:, :], [(w[:, k, j * 128:j * 128 + 128], HC[:, k, :]) for k in range(8)]), tw, read[b])
        t = act(GKT[:, j, :], bank[b][:, :], ACT.Copy, t)
        read[b] = (t,)
        t_gk.append(t)
    t = token_major(w, 256, 256, lambda i: GV[:, i:i + 2, 0:256], tw)
    done(s, t)
    t_la = []
    for i in range(4):
        b = pick()
        t = mms(chain(bank[b][:, :], [(GA[0:33, i * 128:i * 128 + 128], W2[0:33, :])]), t_ga, t_one, t_w2z, read[b])
        lw = EP.rearrange("p d j t -> p (d j t)")[:, (i % 2) * 512:(i % 2) * 512 + 512]
        t2 = act(lw, bank[b][:, :], ACT.Abs, t, hn.get(("lw", i % 2), ()))
        t1 = vts(LA[:, i, :], bank[b][:, :], 0.0, None, ALU.min, None, t2)
        read[b] = (t1, t2)
        t = act(lw, lw, ACT.Exp, t2, scale=-1.0)
        t = act(lw, lw, ACT.Ln, t, bias=1.0)
        t = vtt(LA[:, i, :], LA[:, i, :], lw, ALU.subtract, t, t1)
        hn[("lw", i % 2)] = t
        t_la.append(t)
    dump("LA", LA, t_la)
    t_kk = []
    for i0 in (0, 2):
        b = pick()
        t = turned([(bank[b][:, (i - i0) * 256 + j * 128:(i - i0) * 256 + j * 128 + 128],
                     GKT[:, j, i * 128:i * 128 + 128]) for i in (i0, i0 + 1) for j in range(2)],
                   t_gk, t_cst, read[b])
        t = act(GKK[:, i0:i0 + 2, :], bank[b][:, :].rearrange("p (i n) -> p i n", i=2), ACT.Copy, t)
        read[b] = (t,)
        t_kk.append(t)
    w, tw, s = col_block(W, 2336, 256)
    t_gq = []

    def evac(m0, b, t):
        t = act(GQ, bank[b][:, :].rearrange("p (j t) -> p j t", j=2), ACT.Copy, t)
        t_gq.append(t)
        return (t,)
    done(s, project(w, tw, HX, 8, 2, 256, evac))
    t_ep, t_en = [], []
    for d, name in enumerate(("Tf", "Tb")):
        b = pick()
        jobs = []
        for j in range(2):
            for i in range(2):
                o = j * 256 + i * 128
                jobs += chain(bank[b][:, o:o + 128], [(LA[:, i, d * 256 + j * 128:d * 256 + j * 128 + 128], C(name))])
        t = mms(jobs, t_la, t_cst, read[b])
        src = bank[b][:, :].rearrange("p (j t) -> p j t", j=2)
        t1 = act(EP[:, d, :, :], src, ACT.Exp, t, t_la, scale=1 / 16)
        t2 = act(EN[:, d, :, :], src, ACT.Exp, t, scale=-1 / 16)
        read[b] = (t1, t2)
        t_ep.append(t1)
        t_en.append(t2)
    t_ke = []
    for i in range(4):
        b = pick()
        jobs = []
        for d in range(2):
            name = ("SG" if i < 2 else "SF") + "fb"[d]
            pairs = [(C(name), LA[:, i, d * 256:d * 256 + 256])]
            if (i, d) == (2, 0):
                pairs.append((C("ones"), LA[:, 3, 0:256]))
            if (i, d) == (3, 1):
                pairs.append((C("ones"), LA[:, 2, 256:512]))
            jobs += chain(bank[b][:, d * 256:d * 256 + 256], pairs)
        t = mms(jobs, read[b])
        t = act(KE[:, i, :, :], bank[b][:, :].rearrange("p (d f) -> p d f", d=2), ACT.Exp, t, scale=1 / 16)
        read[b] = (t,)
        t_ke.append(vtt(KE[:, i, :, :], KE[:, i, :, :], wide(GKK[:, i, :], 2), ALU.mult, t, t_kk))
    DC = cols(16).rearrange("p (d j c) -> p d j c", d=2, j=2)
    t_dc = [vcopy(DC[:, d, :, :], EP[:, d, :, (63 if d == 0 else 0)::64], t_ep) for d in range(2)]
    t_qd = [stt(EP[:, d, :, :], GQ, 0.125, EP[:, d, :, :], ALU.mult, ALU.mult, t_gq, t_dc) for d in range(2)]
    t_ki = [vtt(EN[:, d, :, :], GKT[:, :, 0:256], EN[:, d, :, :], ALU.mult, t_gk, t_en) for d in range(2)]
    t_ss = {}
    for d in range(2):
        c0 = 0 if d == 0 else 3
        b = pick()
        jobs = []
        for j in range(2):
            jobs += chain(bank[b][:, j * 256:j * 256 + 256],
                          [(KE[:, 2 + i, d, j * 128:j * 128 + 128], GV[:, 2 + i, j * 256:j * 256 + 256]) for i in range(2)])
        t = mms(jobs, t_ke, t_gv, read[b])
        b4 = bank[b][:, :].rearrange("p (j h v) -> p j h v", j=2, h=2)
        ts = [vcopy(SS[64 * h:64 * h + 64, d, :, c0, :], b4[64 * h:64 * h + 64, :, h, :], t) for h in range(2)]
        read[b] = tuple(ts)
        t_ss[d] = ts
    for n in range(3):
        for d in range(2):
            c = n if d == 0 else 3 - n
            nx = c + 1 if d == 0 else c - 1
            b = pick()
            r0 = 64 * (c % 2)
            jobs = []
            for j in range(2):
                jobs += chain(bank[b][:, j * 256:j * 256 + 256],
                              [(KE[r0:r0 + 64, c // 2, d, j * 128:j * 128 + 128],
                                GV[r0:r0 + 64, c // 2, j * 256:j * 256 + 256])])
            t = mms(jobs, t_ke, t_gv, read[b])
            ts = []
            for j in range(2):
                for h in range(2):
                    p = slice(64 * h, 64 * h + 64)
                    ts.append(stt(SS[p, d, j, nx, :], SS[p, d, j, c, :], DC[p, d, j, c:c + 1],
                                  bank[b][p, j * 256 + h * 128:j * 256 + h * 128 + 128], ALU.mult, ALU.add,
                                  t, t_ss[d], t_dc))
            read[b] = tuple(ts)
            t_ss[d] = ts
    dump("SS", SS, t_ss[0], t_ss[1])
    w, tw, s = col_block(W, 2592, 512)
    t_og = []

    def evac(m0, b, t):
        t = act(OG[:, m0:m0 + 2, :], bank[b][:, :].rearrange("p (j t) -> p j t", j=2), ACT.Silu, t)
        t_og.append(t)
        return (t,)
    done(s, project(w, tw, HX, 8, 4, 256, evac))
    t_at = {}
    maskv = cst[:, CAT["Tf"][0]:CAT["Tf"][0] + 256].rearrange("p (d t) -> p d t", d=2)
    t_ygla = []
    for h in range(4):
        j, hh = h // 2, h % 2
        p = slice(64 * hh, 64 * hh + 64)
        b = 4 + h % 2
        jobs = []
        for d in range(2):
            for i in range(2):
                o = (d * 2 + i) * 128
                jobs += chain(bank[b][:, o:o + 128], [(EN[p, d, j, i * 128:i * 128 + 128],
                                                       EP[p, d, j, i * 128:i * 128 + 128])])
        t = mms(jobs, t_qd, t_ki, read[b])
        am = AT[h % 2].rearrange("p (d i t) -> p d i t", d=2, i=2)
        t = vtt(am, bank[b][:, :].rearrange("p (d i t) -> p d i t", d=2, i=2),
                maskv.unsqueeze(2).broadcast_to([128, 2, 2, 128]), ALU.mult, t, t_at.get(h % 2, ()))
        read[b] = (t,)
        bo = 2 * (h // 2)
        o0 = 256 * (h % 2)
        jobs = []
        for i in range(2):
            for d in range(2):
                jobs.append((bank[bo][:, o0 + i * 128:o0 + i * 128 + 128], GV[:, i, h * 128:h * 128 + 128],
                             am[:, d, i, :], i == 0 and d == 0, False))
        for d in range(2):
            for c in range(4):
                jobs.append((bank[bo][:, o0 + c * 64:o0 + c * 64 + 64], SS[p, d, j, c, :],
                             EP[p, d, j, c * 64:c * 64 + 64], False, (d, c) == (1, 3)))
        t = mms(jobs, t, t_ss[0], t_ss[1], t_gv, read[bo])
        t_at[h % 2] = t
        if h % 2 == 1:
            t = head_norm(bo, t, vcol("gla_norm_g"), YGLA[:, h - 1:h + 1, :].rearrange("p a t -> p (a t)"), 512)
            read[bo] = (t,)
            t_ygla.append(vtt(YGLA[:, h - 1:h + 1, :], YGLA[:, h - 1:h + 1, :], OG[:, h - 1:h + 1, :], ALU.mult,
                              t, t_og))
    dump("YGLA", YGLA, t_ygla)

    handover()
    mark[0] = keep_y
    BG = mem(6144, 24)
    MT = mem(2048, 8)
    TM = [mem(512), mem(512)]
    t_bg = {}
    for c in range(6):
        w, tw, s = col_block(W, 4640 + 512 * c, 512)

        def evac(m0, b, t, c=c):
            m = 4 * c + m0
            t = act(BG[:, m:m + 2, :], bank[b][:, :].rearrange("p (j t) -> p j t", j=2), ACT.Sigmoid, t)
            t_bg[m] = t
            return (t,)
        done(s, project(w, tw, HX, 8, 4, 256, evac))
    t_m = {}
    tm = {}
    for br, (name, Y, ty, nk) in enumerate((("w_br_hy", YHY, t_yhy, 4), ("w_br_gla", YGLA, t_ygla, 4),
                                            ("w_br_att", YATT, t_yatt, 8))):
        for c in range(2):
            w, tw, s = col_block(D[name], 512 * c, 512, nk)

            def evac(m0, b, t, c=c, br=br):
                m = 4 * c + m0
                src = bank[b][:, :].rearrange("p (j t) -> p j t", j=2)
                g = BG[:, 8 * br + m:8 * br + m + 2, :]
                if br == 0:
                    t_m[m] = vtt(MT[:, m:m + 2, :], src, g, ALU.mult, t, t_bg[8 * br + m])
                    return (t_m[m],)
                x = TM[(m // 2) % 2].rearrange("p (j t) -> p j t", j=2)
                t1 = vtt(x, src, g, ALU.mult, t, t_bg[8 * br + m])
                t_m[m] = vtt(MT[:, m:m + 2, :], MT[:, m:m + 2, :], x, ALU.add, t1, t_m[m])
                return (t1,)
            done(s, project(w, tw, Y, nk, 4, 256, evac, ty))
    dump("MT", MT, list(t_m.values()))
    t_x1 = []

    def residual(gate0, toks):
        def outer(c):
            def evac(m0, b, t):
                ts = []
                for j in range(2):
                    m = 4 * c + m0 + j
                    ts.append(stt(XT[:, m, :], bank[b][:, j * 256:j * 256 + 256], mod[:, gate0 + m, 0:1], XT[:, m, :],
                                  ALU.mult, ALU.add, t, t_mod))
                toks.extend(ts)
                return tuple(ts)
            return evac
        return outer

    res = residual(16, t_x1)
    for c in range(2):
        w, tw, s = col_block(D["w_out"], 512 * c, 512)
        done(s, project(w, tw, MT, 8, 4, 256, res(c), list(t_m.values())))
    dump("X1", XT, t_x1)

    handover()
    mark[0] = 0
    T1 = mem(2048, 8)
    SR = mem(512)
    H2 = HC_[:, 0:2048].rearrange("p (k t) -> p k t", k=8)
    t_h2 = modulated(XT, 0, scl[:, 16:24], "norm2_g", (mod[:, 24:32, 0], mod[:, 32:40, 0]), H2, t_x1)
    dump("H2", H2, t_h2)
    RWT = mem(128, 8)
    RB = mem(16)
    SL = mem(2048)
    hand = [x.now() for x in lanes]
    s_rw = sem("s_rw")
    for dst, src in ((RWT, D["router_w"].rearrange("(k p) e -> p k e", p=128)),
                     (RB, D["router_b"].partition_broadcast(128)), (SL[0:16, :], D["sel"])):
        G.dma(lambda e, dst=dst, src=src: e.dma_start(dst, src), s_rw, hand)
    t_rw = Tok(s_rw, 48)
    b = pick()
    jobs = []
    for i in range(2):
        jobs += chain(bank[b][:, i * 16:i * 16 + 16], [(H2[:, k, i * 128:i * 128 + 128], RWT[:, k, :]) for k in range(8)])
    t = mms(jobs, t_h2, t_rw, read[b])
    S3 = mem(32, 2)
    SEL3 = mem(32, 2)
    t_s = act(S3, bank[b][:, 0:32].rearrange("p (i e) -> p i e", i=2), ACT.Sigmoid, t)
    read[b] = (t_s,)
    t = vtt(SEL3, S3, wide(RB, 2), ALU.add, t_s)
    q4 = SEL3.rearrange("p i (g e) -> p (i g) e", g=4)
    PR = mem(48, 8)
    t1 = vtt(PR[:, :, 0:3], q4[:, :, 0:3], q4[:, :, 1:4], ALU.add, t)
    t2 = vtt(PR[:, :, 3:5], q4[:, :, 0:2], q4[:, :, 2:4], ALU.add, t)
    t3 = vtt(PR[:, :, 5:6], q4[:, :, 0:1], q4[:, :, 3:4], ALU.add, t)
    GS = mem(8, 2)
    t = V(lambda e: e.tensor_reduce(GS.rearrange("p i g -> p (i g)"), PR, AX.X, ALU.max), t1, t2, t3)

    def first_of_largest(x, n, hot, rank, *after):
        mx = cols(2)
        t = V(lambda e: e.tensor_reduce(mx, x, AX.X, ALU.max), *after)
        t = vtt(hot, x, long(mx, n), ALU.is_equal, t)
        t = vtt(hot, hot, wide(rank, 2), ALU.mult, t, t_cst)
        t = V(lambda e: e.tensor_reduce(mx, hot, AX.X, ALU.max), t)
        return vtt(hot, hot, long(mx, n), ALU.is_equal, t)

    GH = mem(8, 2)
    t = first_of_largest(GS, 4, GH, C("rank")[:, 0:4], t)
    KG = mem(8, 2)
    t1 = vts(KG, GH, 1.0, 1e30, ALU.subtract, ALU.mult, t)
    sm = SEL3.rearrange("p i (g e) -> p (i g) e", g=4)
    gh2 = long(GH.rearrange("p i g -> p (i g)"), 4)
    kg2 = long(KG.rearrange("p i g -> p (i g)"), 4)
    t = vtt(sm, sm, gh2, ALU.mult, t)
    t = vtt(sm, sm, kg2, ALU.add, t, t1)
    O1 = mem(32, 2)
    O2 = mem(32, 2)
    t_o1 = first_of_largest(SEL3, 16, O1, C("rank"), t)
    t = stt(SEL3, O1, -1e30, SEL3, ALU.mult, ALU.add, t_o1)
    t = first_of_largest(SEL3, 16, O2, C("rank"), t)
    t = vtt(O1, O1, O2, ALU.add, t)
    t = vtt(O1, O1, S3, ALU.mult, t)
    ws = cols(2)
    t = V(lambda e: e.tensor_reduce(ws, O1, AX.X, ALU.add), t)
    t = V(lambda e: e.reciprocal(ws, ws), t)
    t = vtt(O1, O1, long(ws, 16), ALU.mult, t)
    dump("gates", O1, t)
    b = pick()
    t = turned([(bank[b][0:16, i * 128:i * 128 + 128], O1[:, i, :]) for i in range(2)], t, read[b])
    GT = mem(256)
    t_gt = vcopy(GT[0:16, :], bank[b][0:16, 0:256], t)
    read[b] = (t_gt,)
    GB = mem(4096, 16)
    t_gb = []
    for e0 in range(0, 16, 2):
        b = pick()
        jobs = []
        for j in range(2):
            jobs += chain(bank[b][:, j * 256:j * 256 + 256], [(SL[0:16, (e0 + j) * 128:(e0 + j) * 128 + 128], GT[0:16, :])])
        t = mms(jobs, t_gt, t_rw, read[b])
        t = act(GB[:, e0:e0 + 2, :], bank[b][:, :].rearrange("p (j t) -> p j t", j=2), ACT.Copy, t)
        read[b] = (t,)
        t_gb.append(t)
    HD = [mem(1024, 4), mem(1024, 4)]
    SG = [mem(512), mem(512)]
    t_hd = {}
    hd_free = {}
    sg_free = {}

    def hidden(e):
        wg, tg, sg_slot = col_block(D["moe_w_gate"][e], 0, 512)
        wu, tu, su_slot = col_block(D["moe_w_up"][e], 0, 512)
        ts = []
        for half in range(2):
            bg, bu = 4 + 2 * half, 5 + 2 * half
            jobs = []
            for m in range(2):
                mm = 2 * half + m
                jobs += chain(bank[bg][:, m * 256:m * 256 + 256],
                              [(wg[:, k, mm * 128:mm * 128 + 128], H2[:, k, :]) for k in range(8)])
            t1 = mms(jobs, tg, t_h2, read[bg])
            jobs = []
            for m in range(2):
                mm = 2 * half + m
                jobs += chain(bank[bu][:, m * 256:m * 256 + 256],
                              [(wu[:, k, mm * 128:mm * 128 + 128], H2[:, k, :]) for k in range(8)])
            t2 = mms(jobs, tu, read[bu])
            t3 = act(SG[half], bank[bg][:, :], ACT.Silu, t1, sg_free.get(half, ()))
            read[bg] = (t3,)
            dst = HD[e % 2][:, 2 * half:2 * half + 2, :]
            t4 = vtt(SG[half], SG[half], bank[bu][:, :], ALU.mult, t3, t2)
            read[bu] = (t4,)
            t5 = vtt(dst, SG[half].rearrange("p (j t) -> p j t", j=2), wide(GB[:, e, :], 2), ALU.mult, t4, t_gb,
                     hd_free.get(e % 2, ()))
            sg_free[half] = t5
            ts.append(t5)
        done(sg_slot, t1)
        done(su_slot, t2)
        t_hd[e] = ts

    def accumulate(w, tw, X, nk, first, last, *after):
        jobs = []
        for m in range(8):
            for k in range(nk):
                jobs.append((bank[m // 2][:, (m % 2) * 256:(m % 2) * 256 + 256], w[:, k, m * 128:m * 128 + 128],
                             X[:, k, :], first and k == 0 and m % 2 == 0, last and k == nk - 1))
        return mms(jobs, tw, *after)

    def down(e):
        w, tw, s = row_block(D["moe_w_down"][e], 0, 4)
        t = accumulate(w, tw, HD[e % 2], 4, e == 0, e == 15, t_hd[e], read[0:4] if e == 0 else ())
        done(s, t)
        hd_free[e % 2] = t
        return t

    for e in range(17):
        if e < 16:
            hidden(e)
        if e >= 1:
            t_y = down(e - 1)
    t_x = []
    for m in range(8):
        t = stt(XT[:, m, :], bank[m // 2][:, (m % 2) * 256:(m % 2) * 256 + 256], mod[:, 40 + m, 0:1], XT[:, m, :],
                ALU.mult, ALU.add, t_y)
        read[m // 2] = (t,)
        t_x.append(t)
    dump("X2", XT, t_x)

    handover()
    mark[0] = 0
    hand = [x.now() for x in lanes]
    T1 = HC_[:, 0:2048].rearrange("p (k t) -> p k t", k=8)
    SR = mem(512)
    RC = mem(512)
    ROT = mem(1024, 4)
    PP = mem(1024, 4)
    s_pp = sem("s_pp")
    G.dma(lambda e: e.dma_start(PP, D["pT"]), s_pp, hand)
    t_pp = Tok(s_pp, 16)
    POS = mem(256)
    POSI = mem(256)
    s_pos = sem("s_pos")
    G.dma(lambda e: e.dma_start(POSI.bitcast(I32), D["positions"].partition_broadcast(128)), s_pos, hand)
    t = vcopy(POS, POSI.bitcast(I32), Tok(s_pos, 16))
    K1, K2 = mem(256), mem(256)
    t_rot = []
    tk = ()
    for n in range(2):
        cosn, sinn = ROT[:, 2 * n, :], ROT[:, 2 * n + 1, :]
        t1 = vts(sinn, POS, C("freq")[:, n:n + 1], None, ALU.mult, None, t, t_cst)
        t1 = reduce_angle(sinn, sinn, K1, t1)
        t1 = vts(cosn, sinn, math.pi / 2, None, ALU.add, None, t1)
        t2 = vts(K2, cosn, math.pi, -TWO_PI, ALU.is_gt, ALU.mult, t1)
        t2 = vtt(cosn, cosn, K2, ALU.add, t2)
        t3 = vts(cosn, cosn, PI_F, -PI_F, ALU.min, ALU.max, t2)
        t4 = vts(sinn, sinn, PI_F, -PI_F, ALU.min, ALU.max, t2)
        t_rot.append(act(ROT[:, 2 * n:2 * n + 2, :], ROT[:, 2 * n:2 * n + 2, :], ACT.Sin, t3, t4))
    dump("ROT", ROT, t_rot)
    cosA, sinA, cosB, sinB = (ROT[:, i, :] for i in range(4))
    QT = mem(2048, 8)
    KT = mem(2048, 8)
    VV = mem(2048, 2)
    MX = HC_[:, 2048:4096].rearrange("p (k t) -> p k t", k=8)
    AM = mem(1024)
    s_am = sem("s_am")
    G.dma(lambda e: e.dma_start(AM, D["amask"]), s_am, hand)
    t_am = Tok(s_am, 16)
    E_ = [mem(512), mem(512)]
    E2_ = [mem(512), mem(512)]
    PT_ = [mem(512), mem(512)]
    RN = mem(512)
    RQ, RR = mem(512), mem(512)
    base = mark[0]
    hn = {}
    at = {}

    W = D["ab_w_in"]

    def rope_proj(dst, c0, nm, cos, sin, R, *after):
        w, tw, s = col_block(W, c0, 128 * nm)
        ts = []

        def evac(m0, b, t):
            t = act(RN, bank[b][:, :], ACT.Copy, t, hn.get("rn", ()))
            t1, t2 = rope(RN, 2, R, cos, sin, dst[:, m0:m0 + 2, :], 128, t, t_rot)
            hn["rn"] = (t1, t2)
            ts.append(t1)
            return (t,)
        done(s, project(w, tw, XT, 8, nm, 256, evac, *after))
        return ts

    t_q = rope_proj(QT, 0, 4, cosA, sinA, C("Ra"), t_x)
    t_k = rope_proj(KT, 512, 4, cosA, sinA, C("Ra"), t_x)

    def values(w, tw, X, nk, n, dst, *after):
        ts = []
        for i in range(2):
            b = pick()
            t_m = mms(chain(bank[b][:, 0:n], [(X[:, k, i * 128:i * 128 + 128], w[:, k, 0:n]) for k in range(nk)]),
                      tw, *after, read[b])
            t = act(dst(i), bank[b][:, 0:n], ACT.Copy, t_m)
            read[b] = (t,)
            ts.append(t)
        return ts, t_m

    w, tw, s = col_block(W, 1024, 512)
    t_v, t = values(w, tw, XT, 8, 512, lambda i: VV[:, i, 0:512])
    done(s, t)
    t_mx = []

    def pair_scores(u, q, k, p, *after):
        b = 4 + u % 2
        jobs = []
        for i in range(2):
            jobs += chain(bank[b][:, i * 256:i * 256 + 256], [(q[:, i * 128:i * 128 + 128], k)])
        return b, mms(jobs, *after, read[b])

    def first(u):
        p = slice(64 * (u % 2), 64 * (u % 2) + 64)
        b, t = pair_scores(u, QT[p, u // 2, :], KT[p, u // 2, :], p, t_q, t_k)
        return softmax(u, b, (t, t_am), 2, 0.125, masked=True, E=E_[u % 2])

    def second(u, t):
        return flip(u, E_[u % 2], t, (0, 2, 1, 3))

    def third_half(u, t, col, tile):
        b = u % 4
        p = slice(64 * (u % 2), 64 * (u % 2) + 64)
        PT = PT_[u % 2]
        t = mms(chain(bank[b][p, 0:256], [(VV[:, j, col:col + 64], PT[:, j * 256:j * 256 + 256]) for j in range(2)]),
                t, t_v, read[b])
        at[("pt", u % 2)] = t
        t = act(MX[p, tile, :], bank[b][p, 0:256], ACT.Copy, t)
        read[b] = (t,)
        t_mx.append(t)

    staged(8, first, second, lambda u, t: third_half(u, t, 64 * u, u // 2))
    dump("MXA", MX[:, 0:4, :], t_mx)
    qk_read = PE.now()

    CQ = mem(768, 3)
    CK = mem(512, 2)
    CR = mem(256)
    CS = mem(768, 3)
    w, tw, s = col_block(W, 1536, 416)
    w2_, tw2, s2 = col_block(W, 1952, 256)
    t_c = []
    for wt, tok, sl, c0, dsts in ((w, tw, s, 0, (CQ[:, 0, :], CQ[:, 1, :])), (w, tw, s, 256, (CQ[:, 2, :],)),
                                  (w2_, tw2, s2, -32, (CK[:, 0, :], CK[:, 1, :]))):
        b = pick()
        jobs = []
        for j in range(len(dsts)):
            cc0 = c0 + j * 128 if c0 >= 0 else 1920 - 1952 + j * 128
            if c0 < 0 and j == 0:
                jobs += chain(bank[b][0:32, 0:256], [(w[:, k, 384:416], XT[:, k, :]) for k in range(8)])
                jobs += chain(bank[b][32:64, 0:256], [(w2_[:, k, 0:32], XT[:, k, :]) for k in range(8)])
                jobs += chain(bank[b][64:128, 0:256], [(w2_[:, k, 32:96], XT[:, k, :]) for k in range(8)])
            else:
                jobs += chain(bank[b][:, j * 256:j * 256 + 256],
                              [(wt[:, k, cc0:cc0 + 128], XT[:, k, :]) for k in range(8)])
        t_m = mms(jobs, tok, tw2 if c0 < 0 else (), read[b])
        for j, dst in enumerate(dsts):
            t = act(dst, bank[b][:, j * 256:j * 256 + 256], ACT.Copy, t_m)
            t_c.append(t)
        read[b] = (t,)
    b = pick()
    t_m = mms(chain(bank[b][64:96, 0:256], [(w2_[:, k, 224:256], XT[:, k, :]) for k in range(8)]), read[b])
    t_z = V(lambda e: e.memset(CR[0:64, :], 0.0))
    t_cr = act(CR[64:96, :], bank[b][64:96, 0:256], ACT.Copy, t_m)
    read[b] = (t_cr,)
    done(s, t_m)
    done(s2, t_m)

    def plain_norm(X, nk, d, eps, gname, *after):
        t = act(CS[:, 0:nk, :], X, ACT.Square, *after, hn.get("cs", ()))
        b = pick()
        t = ones_sum([CS[:, k, :] for k in range(nk)], NT, b, t)
        hn["cs"] = t
        t_r, t = inv_root(bank[b][:, 0:NT], NT, d, eps, SR[:, 0:NT], t, hn.get("sr", ()))
        read[b] = (t_r,)
        ts = [stt(X[:, k, :], X[:, k, :], vcol(gname, k), SR[:, 0:NT], ALU.mult, ALU.mult, t) for k in range(nk)]
        hn["sr"] = ts
        return ts

    t_cq = plain_norm(CQ, 3, 384, EPS, "ab_q_norm_2", t_c)
    t_ck = plain_norm(CK, 2, 256, EPS, "ab_kv_norm_2", t_c)
    t_kr, _ = rope(CR[0:96, :], 1, C("Rb")[0:96, 0:96], cosB, sinB, CR.unsqueeze(1), 96, t_z, t_cr, t_rot, rows=(64, 96))
    w, tw, s = load(D["ab_w_q_up"].rearrange("(k p) n -> p k n", p=128),
                    lambda r: r[:, 0:2304].rearrange("p (k n) -> p k n", k=3))
    t_q = []
    for h0 in range(0, 8, 2):
        b = pick()
        jobs = []
        for j in range(2):
            jobs += chain(bank[b][0:96, j * 256:j * 256 + 256],
                          [(w[:, k, (h0 + j) * 96:(h0 + j) * 96 + 96], CQ[:, k, :]) for k in range(3)])
        t_m = mms(jobs, tw, t_cq, read[b])
        t = act(RN[0:96, :], bank[b][0:96, :], ACT.Copy, t_m, hn.get("rn", ()))
        read[b] = (t,)
        t1, t2 = rope(RN[0:96, :], 2, C("Rb")[0:96, 0:96], cosB, sinB, QT[:, h0:h0 + 2, :], 96, t, qk_read)
        hn["rn"] = (t1, t2)
        t_q.append(t1)
    done(s, t_m)
    w, tw, s = load(D["ab_w_kv_up"].rearrange("(k p) n -> p k n", p=128),
                    lambda r: r[:, 0:2048].rearrange("p (k n) -> p k n", k=2))
    t_k = []
    for h0 in range(0, 8, 2):
        b = pick()
        jobs = []
        for j in range(2):
            jobs += chain(bank[b][0:64, j * 256:j * 256 + 256],
                          [(w[:, k, (h0 + j) * 128:(h0 + j) * 128 + 64], CK[:, k, :]) for k in range(2)])
        t = mms(jobs, tw, t_ck, read[b])
        t = act(KT[0:64, h0:h0 + 2, :], bank[b][0:64, :].rearrange("p (j t) -> p j t", j=2), ACT.Copy, t, qk_read)
        read[b] = (t,)
        t_k.append(t)
    t_k.append(vcopy(KT[64:96, :, :], wide(CR[64:96, :], 8), t_kr, qk_read))
    wv = w.rearrange("p k (h n) -> p k h n", h=8)
    ts = []
    for i in range(2):
        b = pick()
        t_m = mms(chain(bank[b][:, :], [(CK[:, k, i * 128:i * 128 + 128], wv[:, k, :, 64:128]) for k in range(2)]),
                  read[b])
        t = act(VV[:, i, 0:512], bank[b][:, :], ACT.Copy, t_m, qk_read)
        read[b] = (t,)
        ts.append(t)
    done(s, t_m)
    t_v = ts

    def first(u):
        b, t = pair_scores(u, QT[0:96, u, :], KT[0:96, u, :], None, t_q, t_k)
        return softmax(u, b, t, 2, 96 ** -0.5, E=E_[u % 2])

    staged(8, first, second, lambda u, t: third_half(u, t, 64 * u, 4 + u // 2))
    dump("MX", MX, t_mx)

    def into_t1(toks, first_c=0):
        def outer(c):
            def evac(m0, b, t):
                m = 4 * c + m0
                t = stt(T1[:, m:m + 2, :], XT[:, m:m + 2, :], ALPHA, bank[b][:, :].rearrange("p (j t) -> p j t", j=2),
                        ALU.mult, ALU.add, t)
                toks.append(t)
                return (t,)
            return evac
        return outer

    def layer_norm(gname, bname, i, toks):
        b = pick()
        t = ones_sum([T1[:, k, :] for k in range(8)], NT, b, toks)
        t = vts(SR[:, 256:512], bank[b][:, 0:NT], 1.0 / 1024, None, ALU.mult, None, t)
        read[b] = (t,)
        t_d = vtt(T1, T1, wide(SR[:, 256:512], 8), ALU.subtract, t)
        t = act(XT, T1, ACT.Square, t_d)
        b = pick()
        t = ones_sum([XT[:, k, :] for k in range(8)], NT, b, t)
        t_sq = t
        t_r, t = inv_root(bank[b][:, 0:NT], NT, 1024, 1e-5, SR[:, 0:NT], t)
        read[b] = (t_r,)
        t = vtt(T1, T1, wide(SR[:, 0:NT], 8), ALU.mult, t)
        ts = []
        for k in range(8):
            ts.append(vts(XT[:, k, :], T1[:, k, :], vcol(gname, 8 * i + k), vcol(bname, 8 * i + k),
                          ALU.mult, ALU.add, t, t_sq))
        return ts

    def mix_out(wname, toks_in):
        toks = []
        ev = into_t1(toks)
        for c in range(2):
            w, tw, s = col_block(D[wname], 512 * c, 512)
            done(s, project(w, tw, MX, 8, 4, 256, ev(c), toks_in, t_x))
        return toks

    def ffn(i, t_x):
        mark[0] = base
        A0 = mem(1024, 2)
        HF_ = mem(2816, 11)
        wg_, wu_, wd_ = D["ffn_w_gate"][i], D["ffn_w_up"][i], D["ffn_w_down"][i]
        a_free = {}
        h_free = {}
        t_h = {}
        ring_h = lambda m: HF_[:, m % 11, :]
        downs = []
        pieces = [(0, 512), (512, 512), (1024, 512), (1536, 512), (2048, 512), (2560, 256)]

        def hid(c):
            c0, n = pieces[c]
            wg, tg, s1 = col_block(wg_, c0, n)
            wu, tu, s2 = col_block(wu_, c0, n)
            for m0 in range(0, n // 128, 2):
                par = (c0 // 256 + m0 // 2) % 2
                bg, bu = 4 + 2 * par, 5 + 2 * par
                for w, tw, b in ((wg, tg, bg), (wu, tu, bu)):
                    jobs = []
                    for j in range(2):
                        jobs += chain(bank[b][:, j * 256:j * 256 + 256],
                                      [(w[:, k, (m0 + j) * 128:(m0 + j) * 128 + 128], XT[:, k, :]) for k in range(8)])
                    t = mms(jobs, tw, t_x, read[b])
                    if b == bg:
                        t1 = t
                    else:
                        t2 = t
                done(s1, t1)
                done(s2, t2)
                tc, ta = [], []
                v = 66 * i
                for j in range(2):
                    m = c0 // 128 + m0 + j
                    tc.append(act(A0[:, par, j * 256:j * 256 + 256], bank[bg][:, j * 256:j * 256 + 256], ACT.Identity,
                                  t1, a_free.get(par, ()), scale=vcol("ffn_conv_w_2", v + 22 + m),
                                  bias=vcol("ffn_conv_b_2", 22 * i + m)))
                for j in range(2):
                    m = c0 // 128 + m0 + j
                    src = bank[bg][:, j * 256:j * 256 + 256]
                    dst = A0[:, par, j * 256:j * 256 + 256]
                    t = stt(dst[:, 1:256], src[:, 0:255], vcol("ffn_conv_w_2", v + m), dst[:, 1:256],
                            ALU.mult, ALU.add, tc)
                    t = stt(dst[:, 0:255], src[:, 1:256], vcol("ffn_conv_w_2", v + 44 + m), dst[:, 0:255],
                            ALU.mult, ALU.add, t)
                    ta.append(t)
                read[bg] = tuple(ta)
                t = act(A0[:, par, :], A0[:, par, :], ACT.Gelu_apprx_tanh, ta)
                for j in range(2):
                    m = c0 // 128 + m0 + j
                    t3 = vtt(ring_h(m), A0[:, par, j * 256:j * 256 + 256], bank[bu][:, j * 256:j * 256 + 256],
                             ALU.mult, t, t2, h_free.get(m % 11, ()))
                    t_h[m] = t3
                read[bu] = (t3,)
                a_free[par] = t3

        def dn(c):
            c0, n = pieces[c]
            nk = n // 128
            w, tw, s = row_block(wd_, c0 // 128, nk)
            jobs = []
            for m in range(8):
                for k in range(nk):
                    kk_ = c0 // 128 + k
                    jobs.append((bank[m // 2][:, (m % 2) * 256:(m % 2) * 256 + 256], w[:, k, m * 128:m * 128 + 128],
                                 ring_h(kk_), kk_ == 0 and m % 2 == 0, kk_ == 21))
            t = mms(jobs, tw, [t_h[c0 // 128 + k] for k in range(nk)], read[0:4] if c == 0 else ())
            done(s, t)
            for k in range(nk):
                h_free[(c0 // 128 + k) % 11] = t
            return t

        for c in range(7):
            if c < 6:
                hid(c)
            if c >= 1:
                t = dn(c - 1)
        ts = []
        for j in range(4):
            t2 = stt(T1[:, 2 * j:2 * j + 2, :], XT[:, 2 * j:2 * j + 2, :], ALPHA,
                     bank[j][:, :].rearrange("p (a t) -> p a t", a=2), ALU.mult, ALU.add, t)
            read[j] = (t2,)
            ts.append(t2)
        return ts

    def ple(i, t_x):
        mark[0] = base
        SGT = mem(2048, 8)
        PJ = mem(512)
        t_sg = {}
        for c in range(2):
            w, tw, s = col_block(D["ple_w_gate"][i], 512 * c, 512)

            def evac(m0, b, t, c=c):
                m = 4 * c + m0
                t = act(SGT[:, m:m + 2, :], bank[b][:, :].rearrange("p (j t) -> p j t", j=2), ACT.Sigmoid, t)
                t_sg[m] = t
                return (t,)
            t_g = project(w, tw, XT, 8, 4, 256, evac, t_x)
            done(s, t_g)
        w, tw, s = row_block(D["ple_w_proj"][i], 0, 2)
        ts = []

        def evac(m0, b, t):
            g = SGT[:, m0:m0 + 2, :]
            t = vtt(g, g, bank[b][:, :].rearrange("p (j t) -> p j t", j=2), ALU.mult, t, t_sg[m0])
            ts.append(vtt(XT[:, m0:m0 + 2, :], XT[:, m0:m0 + 2, :], g, ALU.add, t, t_g))
            return (t,)
        done(s, project(w, tw, PP[:, 2 * i:2 * i + 2, :], 2, 8, 256, evac, t_pp))
        return ts

    toks = mix_out("ab_w_out", t_mx)
    t_x = layer_norm("ln_mix_g_2", "ln_mix_b_2", 0, toks)
    dump("X3", XT, t_x)
    handover()
    toks = ffn(0, t_x)
    t_x = layer_norm("ln_ffn_g_2", "ln_ffn_b_2", 0, toks)
    dump("X4", XT, t_x)
    handover()
    t_x = ple(0, t_x)
    dump("X5", XT, t_x)

    handover()
    mark[0] = base
    W = D["c_w_qkv"]
    t_q = rope_proj(QT[:, 0:4, :], 0, 4, cosA, sinA, C("Ra"), t_x)
    t_q += rope_proj(QT[:, 4:8, :], 512, 4, cosA, sinA, C("Ra"), t_x)
    t_k = rope_proj(KT[:, 0:4, :], 1024, 4, cosA, sinA, C("Ra"), t_x)
    t_k += rope_proj(KT[:, 4:8, :], 1536, 4, cosA, sinA, C("Ra"), t_x)
    t_v = []
    for c in range(2):
        w, tw, s = col_block(W, 2048 + 512 * c, 512)
        ts, t = values(w, tw, XT, 8, 512, lambda i, c=c: VV[:, i, 512 * c:512 * c + 512])
        done(s, t)
        t_v += ts
    LP = mem(256, 4)
    hand = [x.now() for x in lanes]
    s_lp = sem("s_lp")
    G.dma(lambda e: e.dma_start(LP.rearrange("p a b -> p (a b)"), D["c_lambda"].partition_broadcast(128)), s_lp, hand)
    LS = cols(2)
    NL = cols(2)
    t = vtt(LP[:, 0:3:2, :], LP[:, 0:3:2, :], LP[:, 1:4:2, :], ALU.mult, Tok(s_lp, 16))
    t = V(lambda e: e.tensor_reduce(LS, LP[:, 0:3:2, :], AX.X, ALU.add), t)
    t = act(LS, LS, ACT.Exp, t)
    t = vtt(NL[:, 0:1], LS[:, 1:2], LS[:, 0:1], ALU.subtract, t)
    t_nl = vts(NL[:, 0:1], NL[:, 0:1], LAMBDA_INIT, None, ALU.subtract, None, t)
    SLN = cols(1)
    t_sln = vts(SLN, vcol("c_subln_2"), 1.0 - LAMBDA_INIT, None, ALU.mult, None, t_vec)
    dump("NL", NL[:, 0:1], t_nl)
    t_mx = []

    def first(u):
        b, t = pair_scores(u, QT[0:64, u, :], KT[0:64, u, :], None, t_q, t_k)
        b2 = 2 + u % 2
        jobs = []
        for i in range(2):
            jobs += chain(bank[b2][:, i * 256:i * 256 + 256], [(QT[64:128, u, i * 128:i * 128 + 128], KT[64:128, u, :])])
        tb = mms(jobs, read[b2])
        t1 = softmax(u, b, t, 2, 0.125, E=E_[u % 2])
        t2 = softmax(u, b2, (tb, t_nl), 2, 0.125, E=E2_[u % 2], key="e2", factor=NL[:, 0:1])
        t3 = vtt(E_[u % 2], E_[u % 2], E2_[u % 2], ALU.add, t1, t2)
        at[("e2", u % 2)] = t3
        return t3

    def third(u, t):
        b = u % 2
        PT = PT_[u % 2]
        t = mms(chain(bank[b][:, 0:256], [(VV[:, j, 128 * u:128 * u + 128], PT[:, j * 256:j * 256 + 256])
                                          for j in range(2)]), t, t_v, read[b])
        at[("pt", u % 2)] = t
        t = act(MX[:, u, :], bank[b][:, 0:256], ACT.Copy, t)
        read[b] = (t,)
        t_mx.append(t)

    staged(8, first, second, third)
    dump("MXC0", MX, t_mx)
    t_mn = []
    for h in range(0, 8, 2):
        src = MX[:, h:h + 2, :].rearrange("p a t -> p (a t)")
        t = act(RQ, src, ACT.Square, t_mx, hn.get("rq", ()))
        b = pick()
        t = ones_sum([RQ], 512, b, t)
        hn["rq"] = t
        t_r, t = inv_root(bank[b][:, :], 512, 128, 1e-5, RR, t, hn.get("rr", ()))
        read[b] = (t_r,)
        t = stt(src, src, SLN, RR, ALU.mult, ALU.mult, t, t_sln)
        hn["rr"] = t
        t_mn.append(t)
    dump("MXC", MX, t_mn)
    toks = mix_out("c_w_out", t_mn)
    t_x = layer_norm("ln_mix_g_2", "ln_mix_b_2", 1, toks)
    dump("X6", XT, t_x)
    handover()
    toks = ffn(1, t_x)
    t_x = layer_norm("ln_ffn_g_2", "ln_ffn_b_2", 1, toks)
    handover()
    t_x = ple(1, t_x)
    s_out = sem("s_out")
    SP.dma(lambda e: e.dma_start(out, XT), s_out, t_x)
    SP.wait(Tok(s_out, 16))

    with ctx:
        block = ctx.enter_context(nc.Block())

        @block.tensor
        def _(e):
            PE.run(e)

        @block.vector
        def _(e):
            V.run(e)

        @block.scalar
        def _(e):
            A.run(e)

        @block.gpsimd
        def _(e):
            G.run(e)

        @block.sync
        def _(e):
            SP.run(e)


def arrays(x):
    a = {k: np.asarray(v) for k, v in x.items()}
    tile = lambda v: v.reshape(-1, 128).T
    fm = lambda v: v.reshape(NT, -1, 128).transpose(2, 1, 0)
    d = {n: a[n][0] for n in ("w_mod", "w_in", "w_br_hy", "w_br_gla", "w_br_att", "w_out", "moe_w_gate",
                              "moe_w_up", "moe_w_down", "hy_pos_w1", "hy_pos_w2", "hy_pos_w3")}
    d |= {"consts": CONSTS, "dft": DFT, "amask": AMASK, "sel": SEL, "posemb": POSEMB}
    d["vecs"] = np.concatenate([tile(a[n]) for n, _ in VECS], axis=1)
    d["cc"] = np.stack([tile(a["c"]), tile(a["c_ctx"])], axis=2).reshape(128, 16)
    d["xT"] = fm(a["x"])
    d["ctxT"] = fm(a["ctx"])
    d["hy_decay"] = a["hy_decay"].reshape(2048)
    d["hy64"] = np.stack([a["hy_pos_b1"][0], a["hy_sin_freq"][0], a["hy_pos_b2"][0]], axis=1)
    w2z = np.zeros((33, 512), np.float32)
    w2z[0:16, 0:256] = a["gla_wa2"][0, 0]
    w2z[16:32, 256:512] = a["gla_wa2"][0, 1]
    w2z[32] = a["gla_ba"].reshape(512)
    d["w2z"] = w2z
    d["router_w"], d["router_b"] = a["router_w"], a["router_b"]
    d["pT"] = a["p_2"].reshape(2, NT, 2, 128).transpose(3, 0, 2, 1).reshape(128, 4, NT)
    d["positions"] = a["positions_2"].reshape(NT)
    for n in ("ab_w_in", "ab_w_q_up", "ab_w_kv_up", "ab_w_out", "c_w_qkv", "c_w_out"):
        d[n] = a[n + "_2"][0]
    d["c_lambda"] = a["c_lambda_2"].reshape(256)
    for n in ("ffn_w_gate", "ffn_w_up", "ffn_w_down", "ple_w_gate", "ple_w_proj"):
        d[n] = a[n + "_2"]
    return {k: np.ascontiguousarray(v) for k, v in d.items()}


def kernel(**inputs):
    import concourse.bacc as bacc
    from concourse.bass_utils import run_bass_kernel_spmd

    nc = bacc.Bacc("TRN2", target_bir_lowering=False, num_devices=1)
    d = arrays(inputs)
    aps = {k: nc.dram_tensor(f"in_{k}", v.shape, mybir.dt.from_np(v.dtype), kind="ExternalInput").ap()
           for k, v in d.items()}
    out = nc.dram_tensor("out_0", (128, 8, NT), F32, kind="ExternalOutput").ap()
    build(nc, aps, out)
    r = run_bass_kernel_spmd(nc, [{f"in_{k}": v for k, v in d.items()}], core_ids=[0])
    return r.results[0]["out_0"].transpose(2, 1, 0).reshape(1, NT, 1024)
```

```python
from collections import namedtuple
from contextlib import ExitStack
import math

import numpy as np

import concourse.bass as bass
from concourse import mybir

F32 = mybir.dt.float32
I32 = mybir.dt.int32
F32R = mybir.dt.float32r
ALU = mybir.AluOpType
ACT = mybir.ActivationFunctionType
AX = mybir.AxisListType

Tok = namedtuple("Tok", "sem n")
Piece = namedtuple("Piece", "src k0 nk n raw")
Held = namedtuple("Held", "hi lo tok k0 nk free slot")

NT = 256
EPS = 1e-6
ALPHA = 4 ** 0.25
LAMBDA_INIT = 0.8 - 0.6 * math.exp(-0.3)
RAW = 5
WS = 3
AHEAD = 2
PIECE = 2048
ARENA = 24900
MAGIC = 12582912.0
TWO_PI = 2 * math.pi
C1 = 6.28125
C2 = float(np.float32(math.floor((TWO_PI - C1) * 2 ** 20) / 2 ** 20))
C3 = float(np.float32(TWO_PI - C1 - C2))
PI_F = float(np.nextafter(np.float32(math.pi), np.float32(0)))

VECS = [("b_mod", 48), ("norm1_g", 8), ("norm2_g", 8), ("q_norm_g", 1), ("k_norm_g", 1), ("gla_norm_g", 1),
        ("hy_conv_w", 36), ("hy_conv_b", 12), ("hy_skip", 8), ("ab_q_norm_2", 3), ("ab_kv_norm_2", 2),
        ("c_subln_2", 1), ("ln_mix_g_2", 16), ("ln_mix_b_2", 16), ("ffn_conv_w_2", 132),
        ("ffn_conv_b_2", 44), ("ln_ffn_g_2", 16), ("ln_ffn_b_2", 16)]
VOFF = {}
_n = 0
for _name, _k in VECS:
    VOFF[_name] = _n
    _n += _k
NV = _n


class Lane:

    def __init__(self, sem):
        self.sem, self.n, self.queue = sem, 0, []

    def __call__(self, emit, *after):
        self.queue.append((emit, after, self.sem, 1))
        self.n += 1
        return Tok(self.sem, self.n)

    def dma(self, emit, sem, *after):
        self.queue.append((emit, after, sem, 16))

    def wait(self, *after):
        self.queue.append((None, after, None, 0))

    def now(self):
        return Tok(self.sem, self.n)

    def run(self, eng):
        seen = {}

        def hold(t):
            if isinstance(t, Tok):
                if t.n > seen.get(id(t.sem), 0):
                    eng.wait_ge(t.sem, t.n)
                    seen[id(t.sem)] = t.n
            else:
                for u in t:
                    hold(u)

        for emit, after, sem, k in self.queue:
            hold(after)
            if emit is not None:
                emit(eng).then_inc(sem, k)


def shape_constants():
    f = np.float32
    i = np.arange(128)
    s, t = i[:, None], i[None, :]
    same = (s // 64) == (t // 64)
    out = {"ident": np.eye(128), "ones": np.ones((128, 128)),
           "Tf": (s <= t) & same, "Tb": (s >= t) & same,
           "SGf": (s > t) & same, "SGb": (s < t) & same, "SFf": s > t, "SFb": s < t}
    rax = np.zeros((128, 128))
    rax[i[1::2], i[0::2]] = -1
    rax[i[0::2], i[1::2]] = 1
    ra = np.zeros((128, 128))
    for b in (0, 64):
        for k in range(8):
            ra[b + 8 + k, b + k] = -1
            ra[b + k, b + 8 + k] = 1
    rb = np.zeros((128, 128))
    for k in range(16):
        rb[80 + k, 64 + k] = -1
        rb[64 + k, 80 + k] = 1
    out |= {"Rax": rax, "Ra": ra, "Rb": rb}
    tok = np.arange(NT)
    inv = np.power(f(10000.0), -np.arange(32, dtype=f) / f(32)).astype(f)
    ang = np.concatenate([(tok // 64).astype(f)[:, None] * inv, (tok % 64).astype(f)[:, None] * inv], axis=1)
    ang = np.repeat(ang, 2, axis=1).T.astype(np.float64)
    out |= {"cosx": np.cos(ang), "sinx": np.sin(ang)}
    fa = 1.0 / np.power(f(500000.0), np.arange(0, 16, 2, dtype=f) / f(16))
    fb = 1.0 / np.power(f(500000.0), np.arange(0, 32, 2, dtype=f) / f(32))
    fq = np.zeros((128, 2))
    for b in (0, 8, 64, 72):
        fq[b:b + 8, 0] = fa
    for b in (64, 80):
        fq[b:b + 16, 1] = fb
    tn = np.stack([-(i / 256.0), -((i + 128) / 256.0)], axis=1)
    out |= {"freq": fq, "negt": tn, "row0": (i > 0)[:, None] * 1.0,
            "rank": np.tile(16.0 - np.arange(16), (128, 1))}
    small = ["ident", "ones", "Tf", "Tb", "SGf", "SGb", "SFf", "SFb", "Rax", "Ra", "Rb", "cosx", "sinx",
             "freq", "negt", "row0", "rank"]
    at, n = {}, 0
    for k in small:
        at[k] = (n, out[k].shape[1])
        n += out[k].shape[1]
    consts = np.concatenate([np.asarray(out[k], f) for k in small], axis=1)

    m = np.arange(256)[:, None]
    k = np.arange(256)[None, :]
    w = 2 * np.pi * ((m * k) % 512) / 512
    cos, sin = np.cos(w), np.sin(w)
    alt = 1.0 - 2.0 * (m[:, 0] % 2)
    nyq_i = -sin[:, :128].copy()
    nyq_i[:, 0] = alt
    nyq_r = cos[:, :128].copy()
    nyq_r[:, 0] = alt
    fwd = np.concatenate([cos, -sin, nyq_i, nyq_r], axis=1)
    fwd = fwd.reshape(2, 128, 768).transpose(1, 0, 2).reshape(128, 1536)
    gr = 2 * cos.T / 512
    gr[0] /= 2
    gi = -2 * sin.T / 512
    gi[0] = alt / 512
    inv_t = np.concatenate([gr, gi], axis=0).reshape(4, 128, 256).transpose(1, 0, 2).reshape(128, 1024)
    dft = np.concatenate([fwd, inv_t], axis=1).astype(f)

    q = np.arange(128)[:, None, None] + 128 * np.arange(2)[None, :, None]
    d = np.abs(q - np.arange(256)[None, None, :])
    count = (d <= 64) * 1.0 + (d % 4 == 0) + (d % 16 == 0)
    neg = np.where(count > 0, 0.0, -1e30)
    mask = np.concatenate([count.reshape(128, 512), neg.reshape(128, 512)], axis=1).astype(f)
    sel = np.zeros((16, 16, 128), f)
    for e in range(16):
        sel[e, e] = 1
    t = np.arange(256, dtype=f)
    bands = np.linspace(1e-4, 15, 16, dtype=f)
    phase = f(2 * math.pi / 256) * t[:, None] * bands[None, :]
    z = np.concatenate([(t / f(256))[:, None], np.cos(phase), -np.sin(phase)], axis=-1)
    return consts, at, dft, mask, sel.reshape(16, 2048), np.ascontiguousarray(z.T.astype(f))


CONSTS, CAT, DFT, AMASK, SEL, POSEMB = shape_constants()


def build(nc, D, out, probe=()):
    with ExitStack() as ctx:
        known = {}

        def once(name, make):
            if name not in known:
                known[name] = make()
            return known[name]
        plan = []
        lay_out(nc, D, out, ctx, once, plan, False, ())
        lay_out(nc, D, out, ctx, once, plan, True, probe)


def lay_out(nc, D, out, ctx, once, plan, final, probe):
    sem = lambda name: once(name, lambda: ctx.enter_context(nc.semaphore(name)))
    PE, V, A, G, SP = (Lane(sem(n)) for n in ("s_pe", "s_dve", "s_act", "s_pool", "s_sp"))
    lanes = (PE, V, A, G)

    def sb(name, cols, dt=F32):
        return once(name, lambda: ctx.enter_context(nc.sbuf_tensor(name, [128, cols], dt)))

    raw = [sb(f"raw{i}", PIECE) for i in range(RAW)]
    cut = [sb(f"cut{i}", 2 * PIECE, F32R) for i in range(WS)]
    cst = sb("cst", CONSTS.shape[1])
    vec = sb("vec", NV)
    XT_ = sb("XT", 2048)
    modt = sb("mod", 96)
    stat = sb("stat", 1200)
    arena_at = once("arena_at", lambda: nc.sbuf_base)
    arena = sb("arena", ARENA)
    pairs_ = once("pairs", lambda: nc.alloc_sbuf_tensor_at("pairs", [128, ARENA], F32R, offset=arena_at))
    bank = [once(f"bank{i}", lambda: ctx.enter_context(nc.psum_tensor(f"bank{i}", [128, 512], F32))) for i in range(8)]
    XT = XT_[:, :].rearrange("p (k t) -> p k t", k=8)
    mark = [0]

    def mem(cols, split=None):
        o = mark[0]
        mark[0] += cols
        assert mark[0] <= ARENA, mark[0]
        ap = arena[:, o:o + cols]
        return ap if split is None else ap.rearrange("p (a b) -> p a b", a=split)

    def pair(k):
        o = mark[0]
        mark[0] += 512 * k
        assert mark[0] <= ARENA, mark[0]
        v = pairs_[:, o:o + 512 * k].rearrange("p (h k t) -> p h k t", h=2, k=k)
        return v[:, 0], v[:, 1]

    st_at = [0]

    def cols(n):
        o = st_at[0]
        st_at[0] += n
        assert st_at[0] <= 1200
        return stat[:, o:o + n]

    def C(name):
        o, n = CAT[name]
        return cst[:, o:o + n]

    def vcol(name, i=0, n=1):
        return vec[:, VOFF[name] + i:VOFF[name] + i + n]

    def wide(ap, n):
        return ap.unsqueeze(1).broadcast_to([ap.shape[0], n, ap.shape[1]])

    def long(ap, n):
        return ap.unsqueeze(2).broadcast_to([ap.shape[0], ap.shape[1], n])

    read = [()] * 8
    turn = [0]

    def pick(among=(4, 5, 6, 7)):
        turn[0] += 1
        return among[turn[0] % len(among)]

    raw_sem = [sem(f"s_raw{i}") for i in range(RAW)]
    raw_use = [0] * RAW
    raw_free = [[()] for i in range(RAW)]
    cut_free = [[()] for i in range(WS)]
    n_issued, n_cut, n_used = [0], [0], [0]
    held = []

    def issue(p):
        i = n_issued[0] % RAW
        n_issued[0] += 1
        assert raw_free[i][0] is not None
        raw_use[i] += 1
        cols_ = p.nk * p.n
        view = lambda t, o=0: t[:, o:o + cols_].rearrange("p (k n) -> p k n", k=p.nk)
        src = p.src.rearrange("(k p) n -> p k n", p=128)
        SP.dma(lambda e: e.dma_start(view(raw[i]), src), raw_sem[i], raw_free[i][0])
        t = Tok(raw_sem[i], 16 * raw_use[i])
        raw_free[i][0] = None
        if p.raw:
            held.append(Held(view(raw[i]), None, t, p.k0, p.nk, raw_free[i], i))
            return
        j = n_cut[0] % WS
        n_cut[0] += 1
        assert cut_free[j][0] is not None
        hi, lo = cut[j][:, 0:cols_], cut[j][:, PIECE:PIECE + cols_]
        ta = A(lambda e: e.activation(hi, raw[i][:, 0:cols_], ACT.Copy), t, cut_free[j][0])
        tv = V(lambda e: e.tensor_tensor(lo, raw[i][:, 0:cols_], hi.bitcast(F32), ALU.subtract), ta)
        raw_free[i][0] = (ta, tv)
        cut_free[j][0] = None
        held.append(Held(view(cut[j]), view(cut[j], PIECE), (ta, tv), p.k0, p.nk, cut_free[j], j))

    def need(p):
        n = n_used[0]
        n_used[0] += 1
        if not final:
            plan.append(p)
            issue(p)
        while final and n_issued[0] < min(n + AHEAD + 1, len(plan)):
            issue(plan[n_issued[0]])
        return held[n]

    def done(h, *toks):
        h.free[0] = toks

    def pieces(w, c0, n, nk, raw=False):
        per = max(1, PIECE // n)
        return [Piece(w[k0 * 128:min(k0 + per, nk) * 128, c0:c0 + n], k0, min(per, nk - k0), n, raw)
                for k0 in range(0, nk, per)]

    def fetch(dst, src, lane, name):
        s = sem(name)
        lane.dma(lambda e: e.dma_start(dst, src), s)
        return Tok(s, 16)

    def handover():
        t = [x.now() for x in lanes]
        for x in lanes:
            x.wait(t)
        return t

    out_sems = []

    def dump(name, ap, *after):
        if name in probe:
            s = sem("d_" + name)
            dst = probe[name](ap.shape)
            G.dma(lambda e: e.dma_start(dst, ap), s, *after)
            G.wait(Tok(s, 16))

    def vtt(o, a, b, op, *after):
        return V(lambda e: e.tensor_tensor(o, a, b, op), *after)

    def vts(o, a, s1, s2, op0, op1, *after):
        if s2 is None:
            return V(lambda e: e.tensor_scalar(o, a, s1, None, op0), *after)
        return V(lambda e: e.tensor_scalar(o, a, s1, s2, op0, op1), *after)

    def stt(o, a, s, b, op0, op1, *after):
        return V(lambda e: e.scalar_tensor_tensor(out=o, in0=a, scalar=s, in1=b, op0=op0, op1=op1), *after)

    def vcopy(o, a, *after):
        return V(lambda e: e.tensor_copy(o, a), *after)

    def act(o, a, f, *after, **kw):
        return A(lambda e: e.activation(o, a, f, **kw), *after)

    def mms(jobs, *after):
        def emit(e):
            for o, l, r, s0, s1 in jobs:
                last = e.matmul(o, l, r, start=s0, stop=s1, skip_group_check=True)
            return last
        return PE(emit, *after)

    def mm3(o, l, r, start, stop):
        return [(o, l[0], r[0], start, False), (o, l[0], r[1], False, False), (o, l[1], r[0], False, stop)]

    def cut_pair(dst, src, *after):
        hi, lo = dst
        n = src.shape[1]
        ts = []
        for k in range(0, n, 2):
            e_ = min(k + 2, n)
            ta = act(hi[:, k:e_, :], src[:, k:e_, :], ACT.Copy, *after)
            ts.append(vtt(lo[:, k:e_, :], src[:, k:e_, :], hi[:, k:e_, :].bitcast(F32), ALU.subtract, ta))
        return ts

    def chain(o, pairs):
        n = len(pairs)
        return [(o, l, r, i == 0, i == n - 1) for i, (l, r) in enumerate(pairs)]

    def turned(jobs, *after):
        def emit(e):
            for o, i in jobs:
                last = e.transpose(o, i, C("ident")[0:i.shape[0], 0:i.shape[0]])
            return last
        return PE(emit, *after)

    def inv_root(sums, n, d, eps, dst, *after):
        t = vts(dst, sums, 1.0 / d, eps, ALU.mult, ALU.add, *after)
        t2 = act(dst, dst, ACT.Sqrt, t)
        return t, V(lambda e: e.reciprocal(dst, dst), t2)

    def ones_sum(srcs, n, b, *after):
        return mms(chain(bank[b][:, 0:n], [(C("ones"), s) for s in srcs]), *after, read[b])

    t_cst = fetch(cst[:, :], D["consts"], A, "s_cst")
    t_vec = fetch(vec[:, :], D["vecs"], A, "s_vec")

    YHY = mem(1024, 4)
    HL = pair(8)
    keep_y = mark[0]
    cc = mem(16)
    sc = mem(16, 8)
    t_cc = fetch(cc, D["cc"], A, "s_cc")
    XC = mem(2048, 8)
    after_xc = mark[0]
    t_x = fetch(XT, D["xT"], A, "s_x")
    t_xc = fetch(XC, D["ctxT"], A, "s_xc")
    HF = mem(5120)
    DF = mem(2560)
    t_dft = fetch(DF, D["dft"], A, "s_dft")
    DFf = DF[:, 0:1536].rearrange("p (k n) -> p k n", k=2)
    DFi = DF[:, 1536:2560].rearrange("p (k n) -> p k n", k=4)
    keep_after_filters = mark[0]

    w3 = mem(2048)
    t_w3 = fetch(w3[0:64, :], D["hy_pos_w3"], A, "s_w3")
    dec = mem(4096, 2)
    dcy = mem(2048)
    t_dcy = fetch(dcy, D["hy_decay"].partition_broadcast(128), A, "s_dcy")
    w1 = mem(64)
    t_w1 = fetch(w1[0:33, :], D["hy_pos_w1"], A, "s_w1")
    w2 = mem(64)
    t_w2 = fetch(w2[0:64, :], D["hy_pos_w2"], A, "s_w2")
    h64 = mem(3)
    t_h64 = fetch(h64[0:64, :], D["hy64"], A, "s_h64")
    pemb = mem(256)
    t_pe = fetch(pemb[0:33, :], D["posemb"], A, "s_pemb")

    t_sc = act(sc.rearrange("p k c -> p (k c)"), cc, ACT.Silu, t_cc)

    def mod_chunk(c):
        for p in pieces(D["w_mod"], 512 * c, 512, 8, raw=True):
            w = need(p)
            jobs = []
            for m in range(4):
                o = 2 * (4 * c + m)
                jobs += [(bank[p.k0 // 4][:, o:o + 2], w.hi[:, k, m * 128:m * 128 + 128], sc[:, p.k0 + k, :],
                          k == 0, k == 3) for k in range(4)]
            t = mms(jobs, w.tok, t_sc)
            done(w, t)
        return t

    def reduce_angle(r, a, k, *after):
        t = vts(k, a, 1 / TWO_PI, MAGIC, ALU.mult, ALU.add, *after)
        t = vts(k, k, MAGIC, None, ALU.subtract, None, t)
        t = stt(r, k, -C1, a, ALU.mult, ALU.add, t)
        t = stt(r, k, -C2, r, ALU.mult, ALU.add, t)
        return stt(r, k, -C3, r, ALU.mult, ALU.add, t)

    ang = mem(256)
    kk = mem(256)
    hid = mem(256)
    for c in range(3):
        mod_chunk(c)
    t = mms(chain(bank[4][0:64, 0:256], [(w1[0:33, :], pemb[0:33, :])]), t_w1, t_pe)
    for layer in range(2):
        b = 4 + layer
        t = vts(ang[0:64, :], bank[b][0:64, 0:256], h64[0:64, 2 * layer:2 * layer + 1] if layer else h64[0:64, 0:1],
                h64[0:64, 1:2], ALU.add, ALU.mult, t, t_h64)
        t = reduce_angle(ang[0:64, :], ang[0:64, :], kk[0:64, :], t)
        t = vts(ang[0:64, :], ang[0:64, :], PI_F, -PI_F, ALU.min, ALU.max, t)
        t = act(hid[0:64, :], ang[0:64, :], ACT.Sin, t)
        if layer == 0:
            t = mms(chain(bank[5][0:64, 0:256], [(w2[0:64, :], hid[0:64, :])]), t, t_w2)
    dump("hid", hid[0:64, :], t)
    t_hid = t
    t = act(dcy, dcy, ACT.Abs, t_dcy)
    t_dec = []
    for i in range(2):
        t_dec.append(act(dec[:, i, :], dcy, ACT.Exp, t, t_cst, scale=C("negt")[:, i:i + 1]))
    F = arena[:, 1024:5120].rearrange("p (i n) -> p i n", i=2)
    t_f = []
    for i in range(2):
        for q in range(4):
            b = pick()
            if (i, q) in ((0, 0), (0, 2), (1, 0), (1, 2)):
                mod_chunk(3 + i * 2 + q // 2)
            t = mms(chain(bank[b][:, :], [(hid[0:64, i * 128:i * 128 + 128], w3[0:64, q * 512:q * 512 + 512])]),
                    t_hid, t_w3, read[b])
            dst, dd = F[:, i, q * 512:q * 512 + 512], dec[:, i, q * 512:q * 512 + 512]
            if i == 0 and q % 2 == 1:
                t = stt(dst, bank[b][:, :], C("row0"), dd, ALU.mult, ALU.mult, t, t_dec[i])
            else:
                t = vtt(dst, bank[b][:, :], dd, ALU.mult, t, t_dec[i])
            read[b] = (t,)
            t_f.append(t)
    last_filter = PE.now()
    PM = dec[:, :, :].rearrange("p i n -> p (i n)").rearrange("p (s i o n) -> p s i o n", s=2, i=2, o=2)
    AB = w3.rearrange("p (i d n) -> p i d n", i=2, d=2)
    recn = cols(1)
    rec = dcy[:, 0:512]
    t_abs_read = last_filter
    hf_off = {"A0": 0, "A1": 1, "B0": 2, "B1": 3, "D0": 4}

    def Hf(o, name):
        k = 5 * o + hf_off[name]
        return HF[:, 512 * k:512 * k + 512]

    t_hf = []
    t_rec_free = ()
    for o in range(2):
        fwd = [F[:, i, (2 * o) * 512:(2 * o) * 512 + 512] for i in range(2)]
        bwd = [F[:, i, (2 * o + 1) * 512:(2 * o + 1) * 512 + 512] for i in range(2)]
        t_ab = [act(AB[:, i, d, :], (fwd, bwd)[d][i], ACT.Abs, t_f, t_abs_read) for i in range(2) for d in range(2)]
        b = pick()
        t = ones_sum([AB[:, i, d, :] for i in range(2) for d in range(2)], 512, b, t_ab, t_cst)
        t_abs_read = t
        t = vts(rec, bank[b][:, :], EPS, None, ALU.add, None, t, t_rec_free, t_dec)
        read[b] = (t,)
        t_rec = V(lambda e: e.reciprocal(rec, rec), t)
        t_pm = []
        for i in range(2):
            for s, op in ((0, ALU.add), (1, ALU.subtract)):
                t = vtt(PM[:, s, i, o, :], fwd[i], bwd[i], op, t_f)
                t_pm.append(vtt(PM[:, s, i, o, :], PM[:, s, i, o, :], rec, ALU.mult, t, t_rec))
        t_rec_free = t_pm[-1]
        mod_chunk(7 + 2 * o)
        for name, c0, s in (("A0", 0, 0), ("A1", 128, 0), ("B0", 256, 1), ("B1", 384, 1), ("D0", 640, 0)):
            b = pick()
            t = mms(chain(bank[b][:, :], [(DFf[:, i, c0:c0 + 128], PM[:, s, i, o, :]) for i in range(2)]),
                    t_pm, t_dft, read[b])
            t = act(Hf(o, name), bank[b][:, :], ACT.Copy, t)
            read[b] = (t,)
            t_hf.append(t)
        mod_chunk(8 + 2 * o)
    dump("HF", HF[:, :], t_hf)
    t = mod_chunk(11)
    mod = modt[:, :].rearrange("p (m c) -> p m c", c=2)
    t_mod = vtt(mod, bank[0][:, 0:96].rearrange("p (m c) -> p m c", c=2), long(vcol("b_mod", 0, 48), 2), ALU.add,
                t, t_vec)
    read[0] = (t_mod,)
    t_mod = vtt(mod, bank[1][:, 0:96].rearrange("p (m c) -> p m c", c=2), mod, ALU.add, t_mod)
    read[1] = (t_mod,)
    dump("mod", modt[:, :], t_mod)

    handover()
    mark[0] = keep_after_filters

    T1 = mem(2048, 8)
    SR = mem(512)
    scl = cols(24)

    def modulated(X, n_x, scale_cols, gname, shift, dst, *after):
        t_s = stt(scale_cols, shift[1], 1.0, vcol(gname, 0, 8), ALU.add, ALU.mult, t_mod, *after)
        t = act(T1, X, ACT.Square, *after)
        b = pick()
        t = ones_sum([T1[:, k, :] for k in range(8)], NT, b, t, t_cst)
        t_r, t = inv_root(bank[b][:, 0:NT], NT, 1024, EPS, SR[:, n_x * NT:n_x * NT + NT], t)
        read[b] = (t_r,)
        t = vtt(T1, X, wide(SR[:, n_x * NT:n_x * NT + NT], 8), ALU.mult, t)
        for k in range(8):
            t_o = vts(T1[:, k, :], T1[:, k, :], scale_cols[:, k:k + 1], shift[0][:, k:k + 1], ALU.mult, ALU.add,
                      t, t_s)
        return cut_pair(dst, T1, t_o)

    t_h = modulated(XT, 0, scl[:, 0:8], "norm1_g", (mod[:, 0:8, 0], mod[:, 8:16, 0]), HL, t_x)

    def project(w, c0, tiles, Xs, nk, evac, *after, width=128, banks=(4, 5, 6, 7)):
        step = 4 // len(Xs) if width == 128 else tiles
        for t0 in range(0, tiles, step):
            nt = min(step, tiles - t0)
            units = [(j, X) for j in range(nt) for X in Xs]
            bs = [pick(banks) for _ in range(0, len(units), 2)]
            last = {}
            for p in pieces(w, c0 + t0 * width, nt * width, nk):
                h = need(p)
                for i, b in enumerate(bs):
                    jobs = []
                    for u, (j, X) in enumerate(units[2 * i:2 * i + 2]):
                        for k in range(p.nk):
                            c = slice(j * width, j * width + width)
                            jobs += mm3(bank[b][0:width, u * 256:u * 256 + 256], (h.hi[:, k, c], h.lo[:, k, c]),
                                        (X[0][:, p.k0 + k, :], X[1][:, p.k0 + k, :]),
                                        p.k0 + k == 0 and u == 0, p.k0 + k == nk - 1)
                    last[i] = t = mms(jobs, h.tok, after, read[b])
                done(h, t)
            for i, b in enumerate(bs):
                read[b] = evac(t0 + 2 * i // len(Xs), b, last[i])
        return t

    def token_major(w, c0, n, Xs, nk, dst, *after):
        per = 512 // n
        bs = [pick() for _ in range(0, len(Xs), per)]
        for p in pieces(w, c0, n, nk):
            h = need(p)
            jobs = []
            for i, X in enumerate(Xs):
                o = bank[bs[i // per]][:, (i % per) * n:(i % per) * n + n]
                for k in range(p.nk):
                    jobs += mm3(o, X(p.k0 + k), (h.hi[:, k, :], h.lo[:, k, :]),
                                p.k0 + k == 0 and i % per == 0, p.k0 + k == nk - 1)
            t = mms(jobs, h.tok, after, [read[b] for b in bs])
            done(h, t)
        ts = []
        for i, b in enumerate(bs):
            t = act(dst(i * per), bank[b][:, 0:per * n].rearrange("p (i n) -> p i n", i=per), ACT.Copy, t)
            read[b] = (t,)
            ts.append(t)
        return ts

    def tokens_of(X, i):
        return lambda k: tuple(x[:, k, i * 128:i * 128 + 128] for x in X)

    W = D["w_in"]

    UV = mem(3072, 12)
    t_uv = []

    def conv_evac(base):
        def evac(m0, b, t):
            ts, t1 = [], []
            for j in range(2):
                m = base + m0 + j
                t1.append(act(UV[:, m, :], bank[b][:, j * 256:j * 256 + 256], ACT.Identity, t,
                              scale=vcol("hy_conv_w", 12 + m), bias=vcol("hy_conv_b", m)))
            for j in range(2):
                m = base + m0 + j
                src = bank[b][:, j * 256:j * 256 + 256]
                dst = UV[:, m, :]
                t2 = stt(dst[:, 1:256], src[:, 0:255], vcol("hy_conv_w", m), dst[:, 1:256], ALU.mult, ALU.add, t1)
                t3 = stt(dst[:, 0:255], src[:, 1:256], vcol("hy_conv_w", 24 + m), dst[:, 0:255], ALU.mult, ALU.add, t2)
                ts.append(t3)
            t_uv.extend(ts)
            return tuple(ts)
        return evac

    for c in (2, 0, 1):
        project(W, 3104 + 512 * c, 4, (HL,), 8, conv_evac(4 * c), t_h, t_vec)
    dump("UV", UV, t_uv)

    ZT = mem(1024, 2)
    XF = T1.rearrange("p (j a) t -> p j (a t)", j=4)
    YF = mem(2048, 4)
    TP = mem(512)
    hy = {}

    def hyena_spectrum(o, z, *after):
        tz = []
        for i in range(2):
            b = pick()
            t = turned([(bank[b][:, c * 128:c * 128 + 128], z[:, c, i * 128:i * 128 + 128]) for c in range(4)],
                       *after, t_cst, read[b])
            t = act(ZT[:, i, :], bank[b][:, :], ACT.Copy, t, hy.get("zt", ()))
            read[b] = (t,)
            tz.append(t)
        tx = []
        for j, c0 in enumerate((0, 128, 512, 384)):
            b = pick()
            t = mms(chain(bank[b][:, :], [(DFf[:, i, c0:c0 + 128], ZT[:, i, :]) for i in range(2)]), tz, read[b])
            hy["zt"] = t
            t = act(XF[:, j, :], bank[b][:, :], ACT.Copy, t, hy.get("xf", ()))
            read[b] = (t,)
            tx.append(t)
        ty = []
        for j in range(2):
            R, I = XF[:, j, :], XF[:, 2 + j, :]
            a, bb = Hf(o, f"A{j}"), Hf(o, f"B{j}")
            d = Hf(o, "D0") if j == 0 else a
            t = vtt(YF[:, j, :], R, a, ALU.mult, tx, hy.get("yf", ()))
            t2 = vtt(TP, I, bb, ALU.mult, t)
            t = vtt(YF[:, j, :], YF[:, j, :], TP, ALU.subtract, t2)
            t2 = vtt(YF[:, 2 + j, :], R, bb, ALU.mult, t)
            t3 = vtt(TP, I, d, ALU.mult, t2)
            t4 = vtt(YF[:, 2 + j, :], YF[:, 2 + j, :], TP, ALU.add, t3)
            ty += [t, t4]
        hy["xf"] = t4
        return ty

    def hyena_back(o, z, gate, dst, ty):
        res = []
        for c0 in (0, 2):
            b = pick()
            jobs = []
            for c in (c0, c0 + 1):
                jobs += chain(bank[b][:, (c - c0) * 256:(c - c0) * 256 + 256],
                              [(YF[:, j, c * 128:c * 128 + 128], DFi[:, j, :]) for j in range(4)])
            t = mms(jobs, ty, read[b])
            hy["yf"] = t
            rs = []
            for c in (c0, c0 + 1):
                t1 = stt(z[:, c, :], z[:, c, :], vcol("hy_skip", 4 * o + c),
                         bank[b][:, (c - c0) * 256:(c - c0) * 256 + 256], ALU.mult, ALU.add, t)
                rs.append(t1)
                res.append(vtt(dst[:, c, :], z[:, c, :], gate[:, c, :], ALU.mult, t1))
            read[b] = tuple(rs)
        return res

    z = UV[:, 8:12, :]
    ty = hyena_spectrum(0, z, t_uv)
    tz1 = hyena_back(0, z, UV[:, 0:4, :], z, ty)
    ty = hyena_spectrum(1, z, tz1)
    t_yhy = hyena_back(1, z, UV[:, 4:8, :], YHY, ty)
    dump("YHY", YHY, t_yhy)

    handover()
    mark[0] = after_xc
    T1 = mem(2048, 8)
    after_t1 = mark[0]
    SR = mem(512)
    HR = pair(8)
    keep_hr = mark[0]
    YATT = T1
    t_hc = modulated(XC, 1, scl[:, 8:16], "norm1_g", (mod[:, 0:8, 1], mod[:, 8:16, 1]), HR, t_xc)
    TOK4 = [tokens_of(X, i) for X in (HL, HR) for i in range(2)]
    KT = mem(1024, 2)
    VV = mem(1024, 4)
    QT = mem(2048, 8)
    RQ = mem(512)
    RR = mem(512)
    RN = mem(512)
    RC = mem(512)

    hn = {"free": ()}

    def rope(src, n, R, cos, sin, dst, parts, *after, rows=None):
        lo, hi = rows or (0, parts)
        b = pick((0, 1, 2, 3))
        t = mms(chain(bank[b][0:parts, 0:n * 256], [(R, src)]), *after, read[b])
        s3 = src.rearrange("p (n t) -> p n t", n=n)
        c3 = RC[:, 0:n * 256].rearrange("p (n t) -> p n t", n=n)
        b3 = bank[b][:, 0:n * 256].rearrange("p (n t) -> p n t", n=n)
        t1 = vtt(c3[lo:hi], b3[lo:hi], wide(sin[lo:hi, :], n), ALU.mult, t, hn.get("rc", ()))
        read[b] = (t1,)
        t2 = vtt(dst[lo:hi], s3[lo:hi], wide(cos[lo:hi, :], n), ALU.mult, t1, *after)
        t3 = vtt(dst[lo:hi], dst[lo:hi], c3[lo:hi], ALU.add, t2)
        hn["rc"] = t3
        return t3, t

    def head_norm(b, tok, gcol, dst, n, d=128, eps=EPS, among=(0, 1, 2, 3)):
        t1 = act(RQ[:, 0:n], bank[b][:, 0:n], ACT.Square, tok, hn.get("rq", ()))
        b2 = pick(among)
        t = ones_sum([RQ[:, 0:n]], n, b2, t1, t_cst)
        hn["rq"] = t
        t_r, t = inv_root(bank[b2][:, 0:n], n, d, eps, RR[:, 0:n], t, hn.get("rr", ()))
        read[b2] = (t_r,)
        t = stt(dst, bank[b][:, 0:n], gcol, RR[:, 0:n], ALU.mult, ALU.mult, t, hn.get("rn", ()))
        hn["rr"] = t
        return t

    t_k = []

    def evac(h, b, t):
        t = head_norm(b, t, vcol("k_norm_g"), RN, 512)
        t1, t2 = rope(RN[:, 0:256], 1, C("Rax"), C("cosx"), C("sinx"), KT[:, h:h + 1, 0:256], 128, t)
        t3 = vcopy(KT[:, h, 256:512], RN[:, 256:512], t)
        hn["rn"] = (t1, t2, t3)
        t_k.extend([t1, t3])
        return (t,)
    project(W, 0, 2, (HL, HR), 8, evac, t_h, t_hc)
    t_v = token_major(W, 256, 256, TOK4, 8, lambda i: VV[:, i:i + 2, :])
    t_q = []

    def evac(m, b, t):
        t = head_norm(b, t, vcol("q_norm_g"), RN, 512)
        t1, t2 = rope(RN, 2, C("Rax"), C("cosx"), C("sinx"), QT[:, m:m + 2, :], 128, t)
        hn["rn"] = (t1, t2)
        t_q.append(t1)
        return (t,)
    project(W, 1312, 8, (HL,), 8, evac)
    dump("KT", KT, t_k)
    dump("QT", QT, t_q)

    E_ = [mem(512), mem(512)]
    PT_ = [mem(512), mem(512)]
    at = {}

    def softmax(u, b, tok, g, scale, masked=False, E=None, key="e", factor=None):
        n = 512 // g
        c = cols(4 * g)
        mx, nm, l, r = (c[:, g * i:g * i + g] for i in range(4))
        src = bank[b][:, :].rearrange("p (g n) -> p g n", g=g)
        e3 = E.rearrange("p (g n) -> p g n", g=g)
        held = at.get((key, u % 2), ())
        if masked:
            tok = stt(E, bank[b][:, :], scale, AM[:, 512:1024], ALU.mult, ALU.add, tok, held)
            read[b] = (tok,)
            src, scale = e3, 1.0
        t = V(lambda e: e.tensor_reduce(mx, src, AX.X, ALU.max), tok)
        t = vts(nm, mx, -scale, None, ALU.mult, None, t)
        te = []
        for i in range(g):
            kw = {} if masked else {"accum_out": l[:, i:i + 1]}
            te.append(A(lambda e, i=i, kw=kw: e.activation(e3[:, i, :], src[:, i, :], ACT.Exp, bias=nm[:, i:i + 1],
                                                         scale=scale, **kw), t, held))
        if not masked:
            read[b] = (te[-1], t)
        if masked:
            t = vtt(E, E, AM[:, 0:512], ALU.mult, te)
            t = V(lambda e: e.tensor_reduce(l, e3, AX.X, ALU.add), t)
        else:
            t = te
        t = V(lambda e: e.reciprocal(r, l), t)
        if factor is not None:
            t = vts(r, r, factor, None, ALU.mult, None, t)
        for i in range(g):
            t2 = vts(e3[:, i, :], e3[:, i, :], r[:, i:i + 1], None, ALU.mult, None, t)
        return t2

    def flip(u, E, tok, order):
        b = 6 + u % 2
        t = turned([(bank[b][:, j * 128:j * 128 + 128], E[:, o * 128:o * 128 + 128]) for j, o in enumerate(order)],
                   tok, t_cst, read[b])
        at[("e", u % 2)] = t
        t = act(PT_[u % 2], bank[b][:, :], ACT.Copy, t, at.get(("pt", u % 2), ()))
        read[b] = (t,)
        return t

    def staged(n, first, second, third):
        a, b = {}, {}
        for i in range(n + 2):
            if i < n:
                a[i] = first(i)
            if 1 <= i <= n:
                b[i - 1] = second(i - 1, a[i - 1])
            if i >= 2:
                third(i - 2, b[i - 2])

    t_yatt = []

    def first(u):
        h, i = u // 2, u % 2
        b = 4 + u % 2
        t = mms(chain(bank[b][:, :], [(QT[:, h, i * 128:i * 128 + 128], KT[:, h // 4, :])]), t_q, t_k, read[b])
        return softmax(u, b, t, 1, 128 ** -0.5, E=E_[u % 2])

    def second(u, t):
        return flip(u, E_[u % 2], t, (0, 1, 2, 3))

    def third(u, t):
        h, i = u // 2, u % 2
        b = u % 4
        PT = PT_[u % 2]
        t = mms(chain(bank[b][:, 0:128], [(VV[:, j, (h // 4) * 128:(h // 4) * 128 + 128], PT[:, j * 128:j * 128 + 128])
                                          for j in range(4)]), t, t_v, read[b])
        at[("pt", u % 2)] = t
        t = act(YATT[:, h, i * 128:i * 128 + 128], bank[b][:, 0:128], ACT.Copy, t)
        read[b] = (t,)
        t_yatt.append(t)

    staged(16, first, second, third)
    dump("YATT", YATT, t_yatt)

    handover()
    mark[0] = keep_hr
    YGLA = XC[:, 0:4, :]
    OG = XC[:, 4:8, :]
    GKT = mem(1024, 2)
    GKK = mem(1024, 4)
    GV = mem(2048, 4)
    GA = mem(512)
    GQ = mem(512, 2)
    LA = mem(2048, 4)
    W2 = mem(512)
    W2B = mem(512)
    EP = mem(1024).rearrange("p (d j t) -> p d j t", d=2, j=2)
    EN = mem(1024).rearrange("p (d j t) -> p d j t", d=2, j=2)
    o_hr = keep_hr - 4096
    KE = arena[:, o_hr:o_hr + 2048].rearrange("p (i d f) -> p i d f", i=4, d=2)
    SS = arena[:, o_hr + 2048:o_hr + 4096].rearrange("p (d j c v) -> p d j c v", d=2, j=2, c=4)
    LAf = LA.rearrange("p i n -> p (i n)")
    AT = [LAf[:, 0:512], LAf[:, 512:1024]]
    hn = {}
    hand = [x.now() for x in lanes]
    s_w2 = sem("s_w2z")
    G.dma(lambda e: e.dma_start(W2[96:128, :], D["w2z"][0:32, :]), s_w2, hand)
    G.dma(lambda e: e.dma_start(W2B[96:97, :], D["w2z"][32:33, :]), s_w2, hand)
    t_w2z = Tok(s_w2, 32)

    t_gk, t_ga = [], []

    def evac(j, b, t):
        t = act(GKT[:, j, :], bank[b][:, :], ACT.Copy, t)
        t_gk.append(t)
        return (t,)
    project(W, 512, 2, (HL, HR), 8, evac)

    def evac(j, b, t):
        t = act(GA[96:128, :], bank[b][96:128, :], ACT.Copy, t)
        t_ga.append(t)
        return (t,)
    project(W, 1184, 1, (HL, HR), 8, evac)
    t_gv = token_major(W, 768, 512, TOK4, 8, lambda i: GV[:, i:i + 1, :])
    hr_read = PE.now()
    t_la = []
    for i in range(4):
        b = pick()
        t = mms(chain(bank[b][:, :], [(GA[96:128, i * 128:i * 128 + 128], W2[96:128, :]),
                                      (C("ones")[96:97, :], W2B[96:97, :])]), t_ga, t_w2z, read[b])
        lw = EP.rearrange("p d j t -> p (d j t)")[:, (i % 2) * 512:(i % 2) * 512 + 512]
        t2 = act(lw, bank[b][:, :], ACT.Abs, t, hn.get(("lw", i % 2), ()))
        t1 = vts(LA[:, i, :], bank[b][:, :], 0.0, None, ALU.min, None, t2)
        read[b] = (t1, t2)
        t = act(lw, lw, ACT.Exp, t2, scale=-1.0)
        t = act(lw, lw, ACT.Ln, t, bias=1.0)
        t = vtt(LA[:, i, :], LA[:, i, :], lw, ALU.subtract, t, t1)
        hn[("lw", i % 2)] = t
        t_la.append(t)
    dump("LA", LA, t_la)
    t_kk = []
    for i0 in (0, 2):
        b = pick()
        t = turned([(bank[b][:, (i - i0) * 256 + j * 128:(i - i0) * 256 + j * 128 + 128],
                     GKT[:, j, i * 128:i * 128 + 128]) for i in (i0, i0 + 1) for j in range(2)],
                   t_gk, t_cst, read[b])
        t = act(GKK[:, i0:i0 + 2, :], bank[b][:, :].rearrange("p (i n) -> p i n", i=2), ACT.Copy, t)
        read[b] = (t,)
        t_kk.append(t)
    t_gq = []

    def evac(m0, b, t):
        t = act(GQ, bank[b][:, :].rearrange("p (j t) -> p j t", j=2), ACT.Copy, t)
        t_gq.append(t)
        return (t,)
    project(W, 2336, 2, (HL,), 8, evac)
    t_ep, t_en = [], []
    for d, name in enumerate(("Tf", "Tb")):
        b = pick()
        jobs = []
        for j in range(2):
            for i in range(2):
                o = j * 256 + i * 128
                jobs += chain(bank[b][:, o:o + 128], [(LA[:, i, d * 256 + j * 128:d * 256 + j * 128 + 128], C(name))])
        t = mms(jobs, t_la, t_cst, read[b])
        src = bank[b][:, :].rearrange("p (j t) -> p j t", j=2)
        t1 = act(EP[:, d, :, :], src, ACT.Exp, t, t_la, scale=1 / 16)
        t2 = act(EN[:, d, :, :], src, ACT.Exp, t, scale=-1 / 16)
        read[b] = (t1, t2)
        t_ep.append(t1)
        t_en.append(t2)
    t_ke = []
    for i in range(4):
        b = pick()
        jobs = []
        for d in range(2):
            name = ("SG" if i < 2 else "SF") + "fb"[d]
            pairs = [(C(name), LA[:, i, d * 256:d * 256 + 256])]
            if (i, d) == (2, 0):
                pairs.append((C("ones"), LA[:, 3, 0:256]))
            if (i, d) == (3, 1):
                pairs.append((C("ones"), LA[:, 2, 256:512]))
            jobs += chain(bank[b][:, d * 256:d * 256 + 256], pairs)
        t = mms(jobs, read[b])
        t = act(KE[:, i, :, :], bank[b][:, :].rearrange("p (d f) -> p d f", d=2), ACT.Exp, t, hr_read, scale=1 / 16)
        read[b] = (t,)
        t_ke.append(vtt(KE[:, i, :, :], KE[:, i, :, :], wide(GKK[:, i, :], 2), ALU.mult, t, t_kk))
    DC = cols(16).rearrange("p (d j c) -> p d j c", d=2, j=2)
    t_dc = [vcopy(DC[:, d, :, :], EP[:, d, :, (63 if d == 0 else 0)::64], t_ep) for d in range(2)]
    t_qd = [stt(EP[:, d, :, :], GQ, 0.125, EP[:, d, :, :], ALU.mult, ALU.mult, t_gq, t_dc) for d in range(2)]
    t_ki = [vtt(EN[:, d, :, :], GKT[:, :, 0:256], EN[:, d, :, :], ALU.mult, t_gk, t_en) for d in range(2)]
    t_ss = {}
    for d in range(2):
        c0 = 0 if d == 0 else 3
        b = pick()
        jobs = []
        for j in range(2):
            jobs += chain(bank[b][:, j * 256:j * 256 + 256],
                          [(KE[:, 2 + i, d, j * 128:j * 128 + 128], GV[:, 2 + i, j * 256:j * 256 + 256]) for i in range(2)])
        t = mms(jobs, t_ke, t_gv, read[b])
        b4 = bank[b][:, :].rearrange("p (j h v) -> p j h v", j=2, h=2)
        ts = [vcopy(SS[64 * h:64 * h + 64, d, :, c0, :], b4[64 * h:64 * h + 64, :, h, :], t, hr_read)
              for h in range(2)]
        read[b] = tuple(ts)
        t_ss[d] = ts
    for n in range(3):
        for d in range(2):
            c = n if d == 0 else 3 - n
            nx = c + 1 if d == 0 else c - 1
            b = pick()
            r0 = 64 * (c % 2)
            jobs = []
            for j in range(2):
                jobs += chain(bank[b][:, j * 256:j * 256 + 256],
                              [(KE[r0:r0 + 64, c // 2, d, j * 128:j * 128 + 128],
                                GV[r0:r0 + 64, c // 2, j * 256:j * 256 + 256])])
            t = mms(jobs, t_ke, t_gv, read[b])
            ts = []
            for j in range(2):
                for h in range(2):
                    p = slice(64 * h, 64 * h + 64)
                    ts.append(stt(SS[p, d, j, nx, :], SS[p, d, j, c, :], DC[p, d, j, c:c + 1],
                                  bank[b][p, j * 256 + h * 128:j * 256 + h * 128 + 128], ALU.mult, ALU.add,
                                  t, t_ss[d], t_dc))
            read[b] = tuple(ts)
            t_ss[d] = ts
    dump("SS", SS, t_ss[0], t_ss[1])
    la_read = PE.now()
    t_og = []

    def evac(m0, b, t):
        t = act(OG[:, m0:m0 + 2, :], bank[b][:, :].rearrange("p (j t) -> p j t", j=2), ACT.Silu, t)
        t_og.append(t)
        return (t,)
    project(W, 2592, 4, (HL,), 8, evac)
    t_at = {0: la_read, 1: la_read}
    maskv = cst[:, CAT["Tf"][0]:CAT["Tf"][0] + 256].rearrange("p (d t) -> p d t", d=2)
    t_ygla = []
    RQ, RR = LAf[:, 1024:1536], LAf[:, 1536:2048]
    hn = {"rq": la_read, "rr": la_read}
    for h in range(4):
        j, hh = h // 2, h % 2
        p = slice(64 * hh, 64 * hh + 64)
        b = 4 + h % 2
        jobs = []
        for d in range(2):
            for i in range(2):
                o = (d * 2 + i) * 128
                jobs += chain(bank[b][:, o:o + 128], [(EN[p, d, j, i * 128:i * 128 + 128],
                                                       EP[p, d, j, i * 128:i * 128 + 128])])
        t = mms(jobs, t_qd, t_ki, read[b])
        am = AT[h % 2].rearrange("p (d i t) -> p d i t", d=2, i=2)
        t = vtt(am, bank[b][:, :].rearrange("p (d i t) -> p d i t", d=2, i=2),
                maskv.unsqueeze(2).broadcast_to([128, 2, 2, 128]), ALU.mult, t, t_at.get(h % 2, ()))
        read[b] = (t,)
        bo = 2 * (h // 2)
        o0 = 256 * (h % 2)
        jobs = []
        for i in range(2):
            for d in range(2):
                jobs.append((bank[bo][:, o0 + i * 128:o0 + i * 128 + 128], GV[:, i, h * 128:h * 128 + 128],
                             am[:, d, i, :], i == 0 and d == 0, False))
        for d in range(2):
            for c in range(4):
                jobs.append((bank[bo][:, o0 + c * 64:o0 + c * 64 + 64], SS[p, d, j, c, :],
                             EP[p, d, j, c * 64:c * 64 + 64], False, (d, c) == (1, 3)))
        t = mms(jobs, t, t_ss[0], t_ss[1], t_gv, read[bo])
        t_at[h % 2] = t
        if h % 2 == 1:
            t = head_norm(bo, t, vcol("gla_norm_g"), YGLA[:, h - 1:h + 1, :].rearrange("p a t -> p (a t)"), 512,
                          among=(6, 7))
            read[bo] = (t,)
            t_ygla.append(vtt(YGLA[:, h - 1:h + 1, :], YGLA[:, h - 1:h + 1, :], OG[:, h - 1:h + 1, :], ALU.mult,
                              t, t_og))
    dump("YGLA", YGLA, t_ygla)

    handover()
    mark[0] = after_t1
    BG = mem(6144, 24)
    MT = mem(2048, 8)
    TM = [mem(512), mem(512)]
    YS = pair(8)
    YH_, YG_ = (YS[0][:, 0:4], YS[1][:, 0:4]), (YS[0][:, 4:8], YS[1][:, 4:8])
    t_yc = {0: cut_pair(YH_, YHY, t_yhy), 1: cut_pair(YG_, YGLA, t_ygla)}
    t_bg = {}

    def evac(m, b, t):
        t = act(BG[:, m:m + 2, :], bank[b][:, :].rearrange("p (j t) -> p j t", j=2), ACT.Sigmoid, t)
        t_bg[m] = t
        return (t,)
    project(W, 4640, 24, (HL,), 8, evac)
    t_m = {}
    for br, (name, Y, nk) in enumerate((("w_br_hy", YH_, 4), ("w_br_gla", YG_, 4), ("w_br_att", YS, 8))):
        if br == 2:
            t_yc[2] = cut_pair(YS, YATT, t_yatt, PE.now())

        def evac(m, b, t):
            src = bank[b][:, :].rearrange("p (j t) -> p j t", j=2)
            g = BG[:, 8 * br + m:8 * br + m + 2, :]
            if br == 0:
                t_m[m] = vtt(MT[:, m:m + 2, :], src, g, ALU.mult, t, t_bg[8 * br + m])
                return (t_m[m],)
            x = TM[(m // 2) % 2].rearrange("p (j t) -> p j t", j=2)
            t1 = vtt(x, src, g, ALU.mult, t, t_bg[8 * br + m])
            t_m[m] = vtt(MT[:, m:m + 2, :], MT[:, m:m + 2, :], x, ALU.add, t1, t_m[m])
            return (t1,)
        project(D[name], 0, 8, (Y,), nk, evac, t_yc[br])
    dump("MT", MT, list(t_m.values()))
    t_x1 = []

    def residual(gate0, toks):
        def evac(m0, b, t):
            ts = []
            for j in range(2):
                m = m0 + j
                ts.append(stt(XT[:, m, :], bank[b][:, j * 256:j * 256 + 256], mod[:, gate0 + m, 0:1], XT[:, m, :],
                              ALU.mult, ALU.add, t, t_mod))
            toks.extend(ts)
            return tuple(ts)
        return evac

    t_ms = cut_pair(HL, MT, list(t_m.values()), PE.now())
    project(D["w_out"], 0, 8, (HL,), 8, residual(16, t_x1), t_ms)
    dump("X1", XT, t_x1)

    handover()
    mark[0] = 0
    T1 = mem(2048, 8)
    SR = mem(512)
    H2S = pair(8)
    H2 = T1
    t_h2 = modulated(XT, 0, scl[:, 16:24], "norm2_g", (mod[:, 24:32, 0], mod[:, 32:40, 0]), H2S, t_x1)
    dump("H2", H2, t_h2)
    RWT = mem(128, 8)
    RB = mem(16)
    SL = mem(2048)
    hand = [x.now() for x in lanes]
    s_rw = sem("s_rw")
    for dst, src in ((RWT, D["router_w"].rearrange("(k p) e -> p k e", p=128)),
                     (RB, D["router_b"].partition_broadcast(128)), (SL[0:16, :], D["sel"])):
        G.dma(lambda e, dst=dst, src=src: e.dma_start(dst, src), s_rw, hand)
    t_rw = Tok(s_rw, 48)
    b = pick()
    jobs = []
    for i in range(2):
        jobs += chain(bank[b][:, i * 16:i * 16 + 16], [(H2[:, k, i * 128:i * 128 + 128], RWT[:, k, :]) for k in range(8)])
    t = mms(jobs, t_h2, t_rw, read[b])
    S3 = mem(32, 2)
    SEL3 = mem(32, 2)
    t_s = act(S3, bank[b][:, 0:32].rearrange("p (i e) -> p i e", i=2), ACT.Sigmoid, t)
    read[b] = (t_s,)
    t = vtt(SEL3, S3, wide(RB, 2), ALU.add, t_s)
    q4 = SEL3.rearrange("p i (g e) -> p (i g) e", g=4)
    PR = mem(48, 8)
    t1 = vtt(PR[:, :, 0:3], q4[:, :, 0:3], q4[:, :, 1:4], ALU.add, t)
    t2 = vtt(PR[:, :, 3:5], q4[:, :, 0:2], q4[:, :, 2:4], ALU.add, t)
    t3 = vtt(PR[:, :, 5:6], q4[:, :, 0:1], q4[:, :, 3:4], ALU.add, t)
    GS = mem(8, 2)
    t = V(lambda e: e.tensor_reduce(GS.rearrange("p i g -> p (i g)"), PR, AX.X, ALU.max), t1, t2, t3)

    def first_of_largest(x, n, hot, rank, *after):
        mx = cols(2)
        t = V(lambda e: e.tensor_reduce(mx, x, AX.X, ALU.max), *after)
        t = vtt(hot, x, long(mx, n), ALU.is_equal, t)
        t = vtt(hot, hot, wide(rank, 2), ALU.mult, t, t_cst)
        t = V(lambda e: e.tensor_reduce(mx, hot, AX.X, ALU.max), t)
        return vtt(hot, hot, long(mx, n), ALU.is_equal, t)

    GH = mem(8, 2)
    t = first_of_largest(GS, 4, GH, C("rank")[:, 0:4], t)
    KG = mem(8, 2)
    t1 = vts(KG, GH, 1.0, 1e30, ALU.subtract, ALU.mult, t)
    sm = SEL3.rearrange("p i (g e) -> p (i g) e", g=4)
    gh2 = long(GH.rearrange("p i g -> p (i g)"), 4)
    kg2 = long(KG.rearrange("p i g -> p (i g)"), 4)
    t = vtt(sm, sm, gh2, ALU.mult, t)
    t = vtt(sm, sm, kg2, ALU.add, t, t1)
    O1 = mem(32, 2)
    O2 = mem(32, 2)
    t_o1 = first_of_largest(SEL3, 16, O1, C("rank"), t)
    t = stt(SEL3, O1, -1e30, SEL3, ALU.mult, ALU.add, t_o1)
    t = first_of_largest(SEL3, 16, O2, C("rank"), t)
    t = vtt(O1, O1, O2, ALU.add, t)
    t = vtt(O1, O1, S3, ALU.mult, t)
    ws = cols(2)
    t = V(lambda e: e.tensor_reduce(ws, O1, AX.X, ALU.add), t)
    t = V(lambda e: e.reciprocal(ws, ws), t)
    t = vtt(O1, O1, long(ws, 16), ALU.mult, t)
    dump("gates", O1, t)
    b = pick()
    t = turned([(bank[b][0:16, i * 128:i * 128 + 128], O1[:, i, :]) for i in range(2)], t, read[b])
    GT = mem(256)
    t_gt = vcopy(GT[0:16, :], bank[b][0:16, 0:256], t)
    read[b] = (t_gt,)
    GB = mem(4096, 16)
    t_gb = []
    for e0 in range(0, 16, 2):
        b = pick()
        jobs = []
        for j in range(2):
            jobs += chain(bank[b][:, j * 256:j * 256 + 256], [(SL[0:16, (e0 + j) * 128:(e0 + j) * 128 + 128], GT[0:16, :])])
        t = mms(jobs, t_gt, t_rw, read[b])
        t = act(GB[:, e0:e0 + 2, :], bank[b][:, :].rearrange("p (j t) -> p j t", j=2), ACT.Copy, t)
        read[b] = (t,)
        t_gb.append(t)
    HD = [pair(4), pair(4)]
    SG = [mem(512), mem(512)]
    t_hd = {}
    hd_free = {}
    sg_free = {}

    def hidden(e):
        wg = pieces(D["moe_w_gate"][e], 0, 512, 8)
        wu = pieces(D["moe_w_up"][e], 0, 512, 8)
        par = 4
        t_b = {}
        for w, bs in ((wg, (4, 6)), (wu, (5, 7))):
            for p in w:
                h = need(p)
                for half, b in enumerate(bs):
                    jobs = []
                    for j in range(2):
                        c = slice((2 * half + j) * 128, (2 * half + j) * 128 + 128)
                        for k in range(p.nk):
                            jobs += mm3(bank[b][:, j * 256:j * 256 + 256], (h.hi[:, k, c], h.lo[:, k, c]),
                                        (H2S[0][:, p.k0 + k, :], H2S[1][:, p.k0 + k, :]),
                                        p.k0 + k == 0 and j == 0, p.k0 + k == 7)
                    t_b[b] = mms(jobs, h.tok, t_h2, read[b])
                done(h, t_b[bs[1]])
        ts = []
        for half in range(2):
            bg, bu = 4 + 2 * half, 5 + 2 * half
            t3 = act(SG[half], bank[bg][:, :], ACT.Silu, t_b[bg], sg_free.get(half, ()))
            read[bg] = (t3,)
            sl = slice(2 * half, 2 * half + 2)
            s3 = SG[half].rearrange("p (j t) -> p j t", j=2)
            t4 = vtt(SG[half], SG[half], bank[bu][:, :], ALU.mult, t3, t_b[bu])
            read[bu] = (t4,)
            t5 = vtt(s3, s3, wide(GB[:, e, :], 2), ALU.mult, t4, t_gb)
            t6 = cut_pair((HD[e % 2][0][:, sl, :], HD[e % 2][1][:, sl, :]), s3, t5, hd_free.get(e % 2, ()))
            sg_free[half] = t6
            ts += t6
        t_hd[e] = ts

    def accumulate(w, X, nk, r0, k_of, first, last, *after):
        for p in pieces(w[r0 * 128:(r0 + nk) * 128, :], 0, 1024, nk):
            h = need(p)
            jobs = []
            for m in range(8):
                for k in range(p.nk):
                    x = k_of(p.k0 + k)
                    jobs += mm3(bank[m // 2][:, (m % 2) * 256:(m % 2) * 256 + 256],
                                (h.hi[:, k, m * 128:m * 128 + 128], h.lo[:, k, m * 128:m * 128 + 128]),
                                (X[0][:, x, :], X[1][:, x, :]),
                                first and p.k0 + k == 0 and m % 2 == 0, last and p.k0 + k == nk - 1)
            t = mms(jobs, h.tok, *after)
            done(h, t)
        return t

    def down(e):
        t = accumulate(D["moe_w_down"][e], HD[e % 2], 4, 0, lambda k: k, e == 0, e == 15, t_hd[e],
                       read[0:4] if e == 0 else ())
        hd_free[e % 2] = t
        return t

    for e in range(17):
        if e < 16:
            hidden(e)
        if e >= 1:
            t_y = down(e - 1)
    t_x = []
    for m in range(8):
        t = stt(XT[:, m, :], bank[m // 2][:, (m % 2) * 256:(m % 2) * 256 + 256], mod[:, 40 + m, 0:1], XT[:, m, :],
                ALU.mult, ALU.add, t_y)
        read[m // 2] = (t,)
        t_x.append(t)
    dump("X2", XT, t_x)

    handover()
    mark[0] = 0
    hand = [x.now() for x in lanes]
    T1 = mem(2048, 8)
    XS = pair(8)
    SR = mem(512)
    RC = mem(512)
    ROT = mem(1024, 4)
    PP = pair(4)
    s_pp = sem("s_pp")
    G.dma(lambda e: e.dma_start(T1[:, 0:4, :], D["pT"]), s_pp, hand)
    t_pp = cut_pair(PP, T1[:, 0:4, :], Tok(s_pp, 16))
    t_xs = cut_pair(XS, XT, t_x)
    POS, POSI, K1, K2 = (T1[:, 4 + i, :] for i in range(4))
    s_pos = sem("s_pos")
    G.dma(lambda e: e.dma_start(POSI.bitcast(I32), D["positions"].partition_broadcast(128)), s_pos, hand)
    t = vcopy(POS, POSI.bitcast(I32), Tok(s_pos, 16))
    t_rot = []
    tk = ()
    for n in range(2):
        cosn, sinn = ROT[:, 2 * n, :], ROT[:, 2 * n + 1, :]
        t1 = vts(sinn, POS, C("freq")[:, n:n + 1], None, ALU.mult, None, t, t_cst)
        t1 = reduce_angle(sinn, sinn, K1, t1)
        t1 = vts(cosn, sinn, math.pi / 2, None, ALU.add, None, t1)
        t2 = vts(K2, cosn, math.pi, -TWO_PI, ALU.is_gt, ALU.mult, t1)
        t2 = vtt(cosn, cosn, K2, ALU.add, t2)
        t3 = vts(cosn, cosn, PI_F, -PI_F, ALU.min, ALU.max, t2)
        t4 = vts(sinn, sinn, PI_F, -PI_F, ALU.min, ALU.max, t2)
        t_rot.append(act(ROT[:, 2 * n:2 * n + 2, :], ROT[:, 2 * n:2 * n + 2, :], ACT.Sin, t3, t4))
    dump("ROT", ROT, t_rot)
    cosA, sinA, cosB, sinB = (ROT[:, i, :] for i in range(4))
    MX = mem(2048, 8)
    AM = mem(1024)
    s_am = sem("s_am")
    G.dma(lambda e: e.dma_start(AM, D["amask"]), s_am, hand)
    t_am = Tok(s_am, 16)
    base = mark[0]
    QT = mem(2048, 8)
    KT = mem(2048, 8)
    VV = mem(2048, 2)
    o_e = mark[0]
    E_ = [mem(512), mem(512)]
    E2_ = [mem(512), mem(512)]
    o_ck = mark[0]
    PT_ = [mem(512), mem(512)]
    RN = mem(512)
    RQ, RR = mem(512), mem(512)
    hn = {}
    at = {}

    W = D["ab_w_in"]

    def rope_proj(dst, c0, nm, cos, sin, R, *after):
        ts = []

        def evac(m0, b, t):
            t = act(RN, bank[b][:, :], ACT.Copy, t, hn.get("rn", ()))
            t1, t2 = rope(RN, 2, R, cos, sin, dst[:, m0:m0 + 2, :], 128, t, t_rot)
            hn["rn"] = (t1, t2)
            ts.append(t1)
            return (t,)
        project(W, c0, nm, (XS,), 8, evac, *after)
        return ts

    t_q = rope_proj(QT, 0, 4, cosA, sinA, C("Ra"), t_xs)
    t_k = rope_proj(KT, 512, 4, cosA, sinA, C("Ra"), t_xs)
    TOK2 = [tokens_of(XS, i) for i in range(2)]
    t_v = token_major(W, 1024, 512, TOK2, 8, lambda i: VV[:, i:i + 1, 0:512])
    t_mx = []

    def pair_scores(u, q, k, p, *after):
        b = 4 + u % 2
        jobs = []
        for i in range(2):
            jobs += chain(bank[b][:, i * 256:i * 256 + 256], [(q[:, i * 128:i * 128 + 128], k)])
        return b, mms(jobs, *after, read[b])

    def first(u):
        p = slice(64 * (u % 2), 64 * (u % 2) + 64)
        b, t = pair_scores(u, QT[p, u // 2, :], KT[p, u // 2, :], p, t_q, t_k)
        return softmax(u, b, (t, t_am), 2, 0.125, masked=True, E=E_[u % 2])

    def second(u, t):
        return flip(u, E_[u % 2], t, (0, 2, 1, 3))

    def third_half(u, t, col, tile):
        b = u % 4
        p = slice(64 * (u % 2), 64 * (u % 2) + 64)
        PT = PT_[u % 2]
        t = mms(chain(bank[b][p, 0:256], [(VV[:, j, col:col + 64], PT[:, j * 256:j * 256 + 256]) for j in range(2)]),
                t, t_v, read[b])
        at[("pt", u % 2)] = t
        t = act(MX[p, tile, :], bank[b][p, 0:256], ACT.Copy, t)
        read[b] = (t,)
        t_mx.append(t)

    staged(8, first, second, lambda u, t: third_half(u, t, 64 * u, u // 2))
    dump("MXA", MX[:, 0:4, :], t_mx)
    qk_read = PE.now()

    T1f = T1.rearrange("p k t -> p (k t)")
    CQ, CSQ = (T1f[:, o:o + 768].rearrange("p (k t) -> p k t", k=3) for o in (0, 768))
    CK = T1f[:, 1536:2048].rearrange("p (k t) -> p k t", k=2)
    CR = mem(256)
    CS = CSQ
    t_c = []
    CQK = [CQ[:, 0, :], CQ[:, 1, :], CQ[:, 2, :], CK[:, 0, :], CK[:, 1, :]]

    def evac(m0, b, t):
        for j in range(min(2, 5 - m0)):
            t = act(CQK[m0 + j], bank[b][:, j * 256:j * 256 + 256], ACT.Copy, t)
            t_c.append(t)
        return (t,)
    project(W, 1536, 5, (XS,), 8, evac)
    h = need(pieces(W, 1952, 256, 8, raw=True)[0])
    b = pick()
    t_m = mms(chain(bank[b][64:96, 0:256], [(h.hi[:, k, 224:256], XT[:, k, :]) for k in range(8)]),
              h.tok, t_x, read[b])
    done(h, t_m)
    t_z = V(lambda e: e.memset(CR[0:64, :], 0.0))
    t_cr = act(CR[64:96, :], bank[b][64:96, 0:256], ACT.Copy, t_m)
    read[b] = (t_cr,)

    def plain_norm(X, nk, d, eps, gname, *after):
        t = act(CS[:, 0:nk, :], X, ACT.Square, *after, hn.get("cs", ()))
        b = pick()
        t = ones_sum([CS[:, k, :] for k in range(nk)], NT, b, t)
        hn["cs"] = t
        t_r, t = inv_root(bank[b][:, 0:NT], NT, d, eps, SR[:, 0:NT], t, hn.get("sr", ()))
        read[b] = (t_r,)
        ts = [stt(X[:, k, :], X[:, k, :], vcol(gname, k), SR[:, 0:NT], ALU.mult, ALU.mult, t) for k in range(nk)]
        hn["sr"] = ts
        return ts

    e_at = o_e
    CQS = tuple(pairs_[:, e_at + 768 * i:e_at + 768 * i + 768].rearrange("p (k t) -> p k t", k=3) for i in range(2))
    CKS = tuple(pairs_[:, o_ck + 512 * i:o_ck + 512 * i + 512].rearrange("p (k t) -> p k t", k=2) for i in range(2))
    t_cq = plain_norm(CQ, 3, 384, EPS, "ab_q_norm_2", t_c)
    t_cq = cut_pair(CQS, CQ, t_cq, qk_read)
    t_ck = plain_norm(CK, 2, 256, EPS, "ab_kv_norm_2", t_c)
    t_ck = cut_pair(CKS, CK, t_ck, qk_read)
    t_kr, _ = rope(CR[0:96, :], 1, C("Rb")[0:96, 0:96], cosB, sinB, CR.unsqueeze(1), 96, t_z, t_cr, t_rot, rows=(64, 96))
    t_q = []

    def evac(h0, b, t):
        t = act(RN[0:96, :], bank[b][0:96, :], ACT.Copy, t, hn.get("rn", ()))
        t1, t2 = rope(RN[0:96, :], 2, C("Rb")[0:96, 0:96], cosB, sinB, QT[:, h0:h0 + 2, :], 96, t, qk_read)
        hn["rn"] = (t1, t2)
        t_q.append(t1)
        return (t,)
    project(D["ab_w_q_up"], 0, 8, (CQS,), 3, evac, t_cq, width=96)
    t_k = []
    h = need(pieces(D["ab_w_kv_up"], 0, 1024, 2)[0])
    for h0 in range(0, 8, 2):
        b = pick()
        jobs = []
        for j in range(2):
            for k in range(2):
                c = slice((h0 + j) * 128, (h0 + j) * 128 + 128)
                jobs += mm3(bank[b][:, j * 256:j * 256 + 256], (h.hi[:, k, c], h.lo[:, k, c]),
                            (CKS[0][:, k, :], CKS[1][:, k, :]), k == 0, k == 1)
        t = mms(jobs, h.tok, t_ck, read[b])
        t = act(KT[0:64, h0:h0 + 2, :], bank[b][0:64, :].rearrange("p (j t) -> p j t", j=2), ACT.Copy, t, qk_read)
        read[b] = (t,)
        t_k.append(t)
    t_k.append(vcopy(KT[64:96, :, :], wide(CR[64:96, :], 8), t_kr, qk_read))
    wv = [x.rearrange("p k (h n) -> p k h n", h=8) for x in (h.hi, h.lo)]
    t_v = []
    for i in range(2):
        b = pick()
        jobs = []
        for k in range(2):
            jobs += mm3(bank[b][:, :], tuple(x[:, k, i * 128:i * 128 + 128] for x in CKS),
                        tuple(x[:, k, :, 64:128] for x in wv), k == 0, k == 1)
        t_m = mms(jobs, read[b])
        t = act(VV[:, i, 0:512], bank[b][:, :], ACT.Copy, t_m, qk_read)
        read[b] = (t,)
        t_v.append(t)
    done(h, t_m)

    def first(u):
        b, t = pair_scores(u, QT[0:96, u, :], KT[0:96, u, :], None, t_q, t_k)
        return softmax(u, b, t, 2, 96 ** -0.5, E=E_[u % 2])

    staged(8, first, second, lambda u, t: third_half(u, t, 64 * u, 4 + u // 2))
    dump("MX", MX, t_mx)

    def into_t1(toks):
        def evac(m, b, t):
            t = stt(T1[:, m:m + 2, :], XT[:, m:m + 2, :], ALPHA, bank[b][:, :].rearrange("p (j t) -> p j t", j=2),
                    ALU.mult, ALU.add, t)
            toks.append(t)
            return (t,)
        return evac

    def layer_norm(gname, bname, i, toks):
        b = pick()
        t = ones_sum([T1[:, k, :] for k in range(8)], NT, b, toks)
        t = vts(SR[:, 256:512], bank[b][:, 0:NT], 1.0 / 1024, None, ALU.mult, None, t)
        read[b] = (t,)
        t_d = vtt(T1, T1, wide(SR[:, 256:512], 8), ALU.subtract, t)
        t = act(XT, T1, ACT.Square, t_d)
        b = pick()
        t = ones_sum([XT[:, k, :] for k in range(8)], NT, b, t)
        t_sq = t
        t_r, t = inv_root(bank[b][:, 0:NT], NT, 1024, 1e-5, SR[:, 0:NT], t)
        read[b] = (t_r,)
        t = vtt(T1, T1, wide(SR[:, 0:NT], 8), ALU.mult, t)
        ts = []
        for k in range(8):
            ts.append(vts(XT[:, k, :], T1[:, k, :], vcol(gname, 8 * i + k), vcol(bname, 8 * i + k),
                          ALU.mult, ALU.add, t, t_sq))
        return ts, cut_pair(XS, XT, ts)

    def mix_out(wname, toks_in):
        toks = []
        mark[0] = base
        MXS = pair(8)
        t_ = cut_pair(MXS, MX, toks_in, PE.now())
        project(D[wname], 0, 8, (MXS,), 8, into_t1(toks), t_, t_x)
        return toks

    def ffn(i, t_x):
        mark[0] = base
        A0 = mem(1024, 2)
        HF_ = pair(11)
        wg_, wu_, wd_ = D["ffn_w_gate"][i], D["ffn_w_up"][i], D["ffn_w_down"][i]
        a_free = {}
        h_free = {}
        t_h = {}
        blocks = [(0, 512), (512, 512), (1024, 512), (1536, 512), (2048, 512), (2560, 256)]

        def hid(c):
            c0, n = blocks[c]
            nb = n // 256
            par0 = c0 // 256
            t_b = {}
            for w, o in ((wg_, 0), (wu_, 1)):
                for p in pieces(w, c0, n, 8):
                    h = need(p)
                    for q in range(nb):
                        b = 4 + 2 * ((par0 + q) % 2) + o
                        jobs = []
                        for j in range(2):
                            c_ = slice((2 * q + j) * 128, (2 * q + j) * 128 + 128)
                            for k in range(p.nk):
                                jobs += mm3(bank[b][:, j * 256:j * 256 + 256], (h.hi[:, k, c_], h.lo[:, k, c_]),
                                            (XS[0][:, p.k0 + k, :], XS[1][:, p.k0 + k, :]),
                                            p.k0 + k == 0 and j == 0, p.k0 + k == 7)
                        t_b[b] = t = mms(jobs, h.tok, t_x, read[b])
                    done(h, t)
            for q in range(nb):
                m0 = 2 * q
                par = (par0 + q) % 2
                bg, bu = 4 + 2 * par, 5 + 2 * par
                t1, t2 = t_b[bg], t_b[bu]
                tc, ta = [], []
                v = 66 * i
                for j in range(2):
                    m = c0 // 128 + m0 + j
                    tc.append(act(A0[:, par, j * 256:j * 256 + 256], bank[bg][:, j * 256:j * 256 + 256], ACT.Identity,
                                  t1, a_free.get(par, ()), scale=vcol("ffn_conv_w_2", v + 22 + m),
                                  bias=vcol("ffn_conv_b_2", 22 * i + m)))
                for j in range(2):
                    m = c0 // 128 + m0 + j
                    src = bank[bg][:, j * 256:j * 256 + 256]
                    dst = A0[:, par, j * 256:j * 256 + 256]
                    t = stt(dst[:, 1:256], src[:, 0:255], vcol("ffn_conv_w_2", v + m), dst[:, 1:256],
                            ALU.mult, ALU.add, tc)
                    t = stt(dst[:, 0:255], src[:, 1:256], vcol("ffn_conv_w_2", v + 44 + m), dst[:, 0:255],
                            ALU.mult, ALU.add, t)
                    ta.append(t)
                read[bg] = tuple(ta)
                t = act(A0[:, par, :], A0[:, par, :], ACT.Gelu_apprx_tanh, ta)
                t3 = vtt(A0[:, par, :], A0[:, par, :], bank[bu][:, :], ALU.mult, t, t2)
                read[bu] = (t3,)
                ts = []
                for j in range(2):
                    m = c0 // 128 + m0 + j
                    sl = slice(m % 11, m % 11 + 1)
                    tc = cut_pair((HF_[0][:, sl, :], HF_[1][:, sl, :]),
                                  A0[:, par, j * 256:j * 256 + 256].unsqueeze(1), t3, h_free.get(m % 11, ()))
                    t_h[m] = tc
                    ts += tc
                a_free[par] = ts

        def dn(c):
            c0, n = blocks[c]
            nk = n // 128
            t = accumulate(wd_, HF_, nk, c0 // 128, lambda k: (c0 // 128 + k) % 11, c == 0, c == 5,
                           [t_h[c0 // 128 + k] for k in range(nk)], read[0:4] if c == 0 else ())
            for k in range(nk):
                h_free[(c0 // 128 + k) % 11] = t
            return t

        for c in range(7):
            if c < 6:
                hid(c)
            if c >= 1:
                t = dn(c - 1)
        ts = []
        for j in range(4):
            t2 = stt(T1[:, 2 * j:2 * j + 2, :], XT[:, 2 * j:2 * j + 2, :], ALPHA,
                     bank[j][:, :].rearrange("p (a t) -> p a t", a=2), ALU.mult, ALU.add, t)
            read[j] = (t2,)
            ts.append(t2)
        return ts

    def ple(i, t_x, t_xs):
        mark[0] = base
        SGT = mem(2048, 8)
        t_sg = {}

        def evac(m, b, t):
            t = act(SGT[:, m:m + 2, :], bank[b][:, :].rearrange("p (j t) -> p j t", j=2), ACT.Sigmoid, t)
            t_sg[m] = t
            return (t,)
        project(D["ple_w_gate"][i], 0, 8, (XS,), 8, evac, t_xs)
        ts = []

        def evac(m0, b, t):
            g = SGT[:, m0:m0 + 2, :]
            t = vtt(g, g, bank[b][:, :].rearrange("p (j t) -> p j t", j=2), ALU.mult, t, t_sg[m0])
            ts.append(vtt(XT[:, m0:m0 + 2, :], XT[:, m0:m0 + 2, :], g, ALU.add, t))
            return (t,)
        P_ = (PP[0][:, 2 * i:2 * i + 2], PP[1][:, 2 * i:2 * i + 2])
        project(D["ple_w_proj"][i], 0, 8, (P_,), 2, evac, t_pp, t_x)
        return ts

    toks = mix_out("ab_w_out", t_mx)
    t_x, t_xs = layer_norm("ln_mix_g_2", "ln_mix_b_2", 0, toks)
    dump("X3", XT, t_x)
    handover()
    toks = ffn(0, t_xs)
    t_x, t_xs = layer_norm("ln_ffn_g_2", "ln_ffn_b_2", 0, toks)
    dump("X4", XT, t_x)
    handover()
    t_x = ple(0, t_x, t_xs)
    t_xs = cut_pair(XS, XT, t_x, PE.now())
    dump("X5", XT, t_x)

    handover()
    mark[0] = base
    W = D["c_w_qkv"]
    QT = mem(2048, 8)
    KT = mem(2048, 8)
    VV = mem(2048, 2)
    E_ = [mem(512), mem(512)]
    E2_ = [mem(512), mem(512)]
    PT_ = [mem(512), mem(512)]
    RN = mem(512)
    RQ, RR = mem(512), mem(512)
    t_q = rope_proj(QT, 0, 8, cosA, sinA, C("Ra"), t_xs)
    t_k = rope_proj(KT, 1024, 8, cosA, sinA, C("Ra"), t_xs)
    t_v = []
    for c in range(2):
        t_v += token_major(W, 2048 + 512 * c, 512, TOK2, 8, lambda i, c=c: VV[:, i:i + 1, 512 * c:512 * c + 512])
    LP = mem(256, 4)
    hand = [x.now() for x in lanes]
    s_lp = sem("s_lp")
    G.dma(lambda e: e.dma_start(LP.rearrange("p a b -> p (a b)"), D["c_lambda"].partition_broadcast(128)), s_lp, hand)
    LS = cols(2)
    NL = cols(2)
    t = vtt(LP[:, 0:3:2, :], LP[:, 0:3:2, :], LP[:, 1:4:2, :], ALU.mult, Tok(s_lp, 16))
    t = V(lambda e: e.tensor_reduce(LS, LP[:, 0:3:2, :], AX.X, ALU.add), t)
    t = act(LS, LS, ACT.Exp, t)
    t = vtt(NL[:, 0:1], LS[:, 1:2], LS[:, 0:1], ALU.subtract, t)
    t_nl = vts(NL[:, 0:1], NL[:, 0:1], LAMBDA_INIT, None, ALU.subtract, None, t)
    SLN = cols(1)
    t_sln = vts(SLN, vcol("c_subln_2"), 1.0 - LAMBDA_INIT, None, ALU.mult, None, t_vec)
    dump("NL", NL[:, 0:1], t_nl)
    t_mx = []

    def first(u):
        b, t = pair_scores(u, QT[0:64, u, :], KT[0:64, u, :], None, t_q, t_k)
        b2 = 2 + u % 2
        jobs = []
        for i in range(2):
            jobs += chain(bank[b2][:, i * 256:i * 256 + 256], [(QT[64:128, u, i * 128:i * 128 + 128], KT[64:128, u, :])])
        tb = mms(jobs, read[b2])
        t1 = softmax(u, b, t, 2, 0.125, E=E_[u % 2])
        t2 = softmax(u, b2, (tb, t_nl), 2, 0.125, E=E2_[u % 2], key="e2", factor=NL[:, 0:1])
        t3 = vtt(E_[u % 2], E_[u % 2], E2_[u % 2], ALU.add, t1, t2)
        at[("e2", u % 2)] = t3
        return t3

    def third(u, t):
        b = u % 2
        PT = PT_[u % 2]
        t = mms(chain(bank[b][:, 0:256], [(VV[:, j, 128 * u:128 * u + 128], PT[:, j * 256:j * 256 + 256])
                                          for j in range(2)]), t, t_v, read[b])
        at[("pt", u % 2)] = t
        t = act(MX[:, u, :], bank[b][:, 0:256], ACT.Copy, t)
        read[b] = (t,)
        t_mx.append(t)

    staged(8, first, second, third)
    dump("MXC0", MX, t_mx)
    t_mn = []
    for h in range(0, 8, 2):
        src = MX[:, h:h + 2, :].rearrange("p a t -> p (a t)")
        t = act(RQ, src, ACT.Square, t_mx, hn.get("rq", ()))
        b = pick()
        t = ones_sum([RQ], 512, b, t)
        hn["rq"] = t
        t_r, t = inv_root(bank[b][:, :], 512, 128, 1e-5, RR, t, hn.get("rr", ()))
        read[b] = (t_r,)
        t = stt(src, src, SLN, RR, ALU.mult, ALU.mult, t, t_sln)
        hn["rr"] = t
        t_mn.append(t)
    dump("MXC", MX, t_mn)
    toks = mix_out("c_w_out", t_mn)
    t_x, t_xs = layer_norm("ln_mix_g_2", "ln_mix_b_2", 1, toks)
    dump("X6", XT, t_x)
    handover()
    toks = ffn(1, t_xs)
    t_x, t_xs = layer_norm("ln_ffn_g_2", "ln_ffn_b_2", 1, toks)
    handover()
    t_x = ple(1, t_x, t_xs)
    s_out = sem("s_out")
    SP.dma(lambda e: e.dma_start(out, XT), s_out, t_x)
    SP.wait(Tok(s_out, 16))

    if not final:
        return
    with nc.Block() as block:

        @block.tensor
        def _(e):
            PE.run(e)

        @block.vector
        def _(e):
            V.run(e)

        @block.scalar
        def _(e):
            A.run(e)

        @block.gpsimd
        def _(e):
            G.run(e)

        @block.sync
        def _(e):
            SP.run(e)


def arrays(x):
    a = {k: np.asarray(v) for k, v in x.items()}
    tile = lambda v: v.reshape(-1, 128).T
    fm = lambda v: v.reshape(NT, -1, 128).transpose(2, 1, 0)
    d = {n: a[n][0] for n in ("w_mod", "w_in", "w_br_hy", "w_br_gla", "w_br_att", "w_out", "moe_w_gate",
                              "moe_w_up", "moe_w_down", "hy_pos_w1", "hy_pos_w2", "hy_pos_w3")}
    d |= {"consts": CONSTS, "dft": DFT, "amask": AMASK, "sel": SEL, "posemb": POSEMB}
    d["vecs"] = np.concatenate([tile(a[n]) for n, _ in VECS], axis=1)
    d["cc"] = np.stack([tile(a["c"]), tile(a["c_ctx"])], axis=2).reshape(128, 16)
    d["xT"] = fm(a["x"])
    d["ctxT"] = fm(a["ctx"])
    d["hy_decay"] = a["hy_decay"].reshape(2048)
    d["hy64"] = np.stack([a["hy_pos_b1"][0], a["hy_sin_freq"][0], a["hy_pos_b2"][0]], axis=1)
    w2z = np.zeros((33, 512), np.float32)
    w2z[0:16, 0:256] = a["gla_wa2"][0, 0]
    w2z[16:32, 256:512] = a["gla_wa2"][0, 1]
    w2z[32] = a["gla_ba"].reshape(512)
    d["w2z"] = w2z
    d["router_w"], d["router_b"] = a["router_w"], a["router_b"]
    d["pT"] = a["p_2"].reshape(2, NT, 2, 128).transpose(3, 0, 2, 1).reshape(128, 4, NT)
    d["positions"] = a["positions_2"].reshape(NT)
    for n in ("ab_w_in", "ab_w_q_up", "ab_w_kv_up", "ab_w_out", "c_w_qkv", "c_w_out"):
        d[n] = a[n + "_2"][0]
    d["c_lambda"] = a["c_lambda_2"].reshape(256)
    for n in ("ffn_w_gate", "ffn_w_up", "ffn_w_down", "ple_w_gate", "ple_w_proj"):
        d[n] = a[n + "_2"]
    return {k: np.ascontiguousarray(v) for k, v in d.items()}


def kernel(**inputs):
    import concourse.bacc as bacc
    from concourse.bass_utils import run_bass_kernel_spmd

    nc = bacc.Bacc("TRN2", target_bir_lowering=False, num_devices=1)
    d = arrays(inputs)
    aps = {k: nc.dram_tensor(f"in_{k}", v.shape, mybir.dt.from_np(v.dtype), kind="ExternalInput").ap()
           for k, v in d.items()}
    out = nc.dram_tensor("out_0", (128, 8, NT), F32, kind="ExternalOutput").ap()
    build(nc, aps, out)
    r = run_bass_kernel_spmd(nc, [{f"in_{k}": v for k, v in d.items()}], core_ids=[0])
    return r.results[0]["out_0"].transpose(2, 1, 0).reshape(1, NT, 1024)
```

```python
from collections import namedtuple
from contextlib import ExitStack
import math

import numpy as np

import concourse.bass as bass
from concourse import mybir

F32 = mybir.dt.float32
I32 = mybir.dt.int32
F32R = mybir.dt.float32r
ALU = mybir.AluOpType
ACT = mybir.ActivationFunctionType
AX = mybir.AxisListType

Tok = namedtuple("Tok", "sem n")
Piece = namedtuple("Piece", "src k0 nk n raw")
Cut = namedtuple("Cut", "hi lo toks")
Held = namedtuple("Held", "hi lo tok k0 nk free slot")

NT = 256
EPS = 1e-6
EPSILONS = [1e-6, 1e-5]
ALPHA = 4 ** 0.25
LAMBDA_INIT = 0.8 - 0.6 * math.exp(-0.3)
RAW = 5
WS = 3
AHEAD = 2
PIECE = 2048
ARENA = 24320
MAGIC = 12582912.0
TWO_PI = 2 * math.pi
C1 = 6.28125
C2 = float(np.float32(math.floor((TWO_PI - C1) * 2 ** 20) / 2 ** 20))
C3 = float(np.float32(TWO_PI - C1 - C2))
PI_F = float(np.nextafter(np.float32(math.pi), np.float32(0)))

VECS = [("b_mod", 48), ("norm1_g", 8), ("norm2_g", 8), ("q_norm_g", 1), ("k_norm_g", 1), ("gla_norm_g", 1),
        ("hy_conv_w", 36), ("hy_conv_b", 12), ("hy_skip", 8), ("ab_q_norm_2", 3), ("ab_kv_norm_2", 2),
        ("c_subln_2", 1), ("ln_mix_g_2", 16), ("ln_mix_b_2", 16), ("ffn_conv_w_2", 132),
        ("ffn_conv_b_2", 44), ("ln_ffn_g_2", 16), ("ln_ffn_b_2", 16)]
VOFF = {}
_n = 0
for _name, _k in VECS:
    VOFF[_name] = _n
    _n += _k
NV = _n


def flat(after):
    out = []
    for t in after:
        if isinstance(t, Tok):
            out.append(t)
        else:
            out += flat(t)
    return out


class Lane:

    def __init__(self, sem):
        self.sem, self.n, self.queue = sem, 0, []

    def __call__(self, emit, *after):
        self.queue.append((emit, flat(after), self.sem, 1))
        self.n += 1
        return Tok(self.sem, self.n)

    def dma(self, emit, sem, *after):
        self.queue.append((emit, flat(after), sem, 16))

    def wait(self, *after):
        self.queue.append((None, flat(after), None, 0))

    def now(self):
        return Tok(self.sem, self.n)

    def run(self, eng):
        seen = {}
        for emit, after, sem, k in self.queue:
            for t in after:
                if t.n > seen.get(id(t.sem), 0):
                    eng.wait_ge(t.sem, t.n)
                    seen[id(t.sem)] = t.n
            if emit is not None:
                emit(eng).then_inc(sem, k)


def shape_constants():
    f = np.float32
    i = np.arange(128)
    s, t = i[:, None], i[None, :]
    same = (s // 64) == (t // 64)
    out = {"ident": np.eye(128), "ones": np.ones((128, 128)),
           "Tf": (s <= t) & same, "Tb": (s >= t) & same,
           "SGf": (s > t) & same, "SGb": (s < t) & same, "SFf": s > t, "SFb": s < t}
    rax = np.zeros((128, 128))
    rax[i[1::2], i[0::2]] = -1
    rax[i[0::2], i[1::2]] = 1
    ra = np.zeros((128, 128))
    for b in (0, 64):
        for k in range(8):
            ra[b + 8 + k, b + k] = -1
            ra[b + k, b + 8 + k] = 1
    rb = np.zeros((128, 128))
    for k in range(16):
        rb[80 + k, 64 + k] = -1
        rb[64 + k, 80 + k] = 1
    out |= {"Rax": rax, "Ra": ra, "Rb": rb}
    tok = np.arange(NT)
    inv = np.power(f(10000.0), -np.arange(32, dtype=f) / f(32)).astype(f)
    ang = np.concatenate([(tok // 64).astype(f)[:, None] * inv, (tok % 64).astype(f)[:, None] * inv], axis=1)
    ang = np.repeat(ang, 2, axis=1).T.astype(np.float64)
    out |= {"cosx": np.cos(ang), "sinx": np.sin(ang)}
    fa = 1.0 / np.power(f(500000.0), np.arange(0, 16, 2, dtype=f) / f(16))
    fb = 1.0 / np.power(f(500000.0), np.arange(0, 32, 2, dtype=f) / f(32))
    fq = np.zeros((128, 2))
    for b in (0, 8, 64, 72):
        fq[b:b + 8, 0] = fa
    for b in (64, 80):
        fq[b:b + 16, 1] = fb
    tn = np.stack([-(i / 256.0), -((i + 128) / 256.0)], axis=1)
    out |= {"freq": fq, "negt": tn, "row0": (i > 0)[:, None] * 1.0,
            "rank": np.tile(16.0 - np.arange(16), (128, 1)),
            "fold": (s % 2 == i[None, :2]) * 1.0, "eps": np.tile([EPSILONS], (128, 1))}
    small = ["ident", "ones", "Tf", "Tb", "SGf", "SGb", "SFf", "SFb", "Rax", "Ra", "Rb", "cosx", "sinx",
             "freq", "negt", "row0", "rank", "fold", "eps"]
    at, n = {}, 0
    for k in small:
        at[k] = (n, out[k].shape[1])
        n += out[k].shape[1]
    consts = np.concatenate([np.asarray(out[k], f) for k in small], axis=1)

    m = np.arange(256)[:, None]
    k = np.arange(256)[None, :]
    w = 2 * np.pi * ((m * k) % 512) / 512
    cos, sin = np.cos(w), np.sin(w)
    alt = 1.0 - 2.0 * (m[:, 0] % 2)
    nyq_i = -sin[:, :128].copy()
    nyq_i[:, 0] = alt
    nyq_r = cos[:, :128].copy()
    nyq_r[:, 0] = alt
    fwd = np.concatenate([cos, -sin, nyq_i, nyq_r], axis=1)
    fwd = fwd.reshape(2, 128, 768).transpose(1, 0, 2).reshape(128, 1536)
    gr = 2 * cos.T / 512
    gr[0] /= 2
    gi = -2 * sin.T / 512
    gi[0] = alt / 512
    inv_t = np.concatenate([gr, gi], axis=0).reshape(4, 128, 256).transpose(1, 0, 2).reshape(128, 1024)
    dft = np.concatenate([fwd, inv_t], axis=1).astype(f)

    q = np.arange(128)[:, None, None] + 128 * np.arange(2)[None, :, None]
    d = np.abs(q - np.arange(256)[None, None, :])
    count = (d <= 64) * 1.0 + (d % 4 == 0) + (d % 16 == 0)
    neg = np.where(count > 0, 0.0, -1e30)
    mask = np.concatenate([count.reshape(128, 512), neg.reshape(128, 512)], axis=1).astype(f)
    t = np.arange(256, dtype=f)
    bands = np.linspace(1e-4, 15, 16, dtype=f)
    phase = f(2 * math.pi / 256) * t[:, None] * bands[None, :]
    z = np.concatenate([(t / f(256))[:, None], np.cos(phase), -np.sin(phase)], axis=-1)
    return consts, at, dft, mask, np.ascontiguousarray(z.T.astype(f))


CONSTS, CAT, DFT, AMASK, POSEMB = shape_constants()


def build(nc, D, out):
    with ExitStack() as ctx:
        known = {}

        def once(name, make):
            if name not in known:
                known[name] = make()
            return known[name]
        plan = []
        lay_out(nc, D, out, ctx, once, plan, False)
        lay_out(nc, D, out, ctx, once, plan, True)


def lay_out(nc, D, out, ctx, once, plan, final):
    sem = lambda name: once(name, lambda: ctx.enter_context(nc.semaphore(name)))
    PE, V, A, G, SP = (Lane(sem(n)) for n in ("s_pe", "s_dve", "s_act", "s_pool", "s_sp"))
    lanes = (PE, V, A, G)

    def sb(name, cols, dt=F32):
        return once(name, lambda: ctx.enter_context(nc.sbuf_tensor(name, [128, cols], dt)))

    raw = [sb(f"raw{i}", PIECE) for i in range(RAW)]
    cut = [sb(f"cut{i}", 2 * PIECE, F32R) for i in range(WS)]
    cst = sb("cst", CONSTS.shape[1])
    vec = sb("vec", NV)
    XT_ = sb("XT", 2048)
    modt = sb("mod", 96)
    stat = sb("stat", 400)
    sct = sb("sct", 156, F32R)
    mrow = sb("mrow", 1024)
    arena_at = once("arena_at", lambda: nc.sbuf_base)
    arena = sb("arena", ARENA)
    pairs_ = once("pairs", lambda: nc.alloc_sbuf_tensor_at("pairs", [128, ARENA], F32R, offset=arena_at))
    bank = [once(f"bank{i}", lambda: ctx.enter_context(nc.psum_tensor(f"bank{i}", [128, 512], F32))) for i in range(8)]
    XT = XT_[:, :].rearrange("p (k t) -> p k t", k=8)
    mark = [0]

    def mem(cols, split=None):
        o = mark[0]
        mark[0] += cols
        assert mark[0] <= ARENA, mark[0]
        ap = arena[:, o:o + cols]
        return ap if split is None else ap.rearrange("p (a b) -> p a b", a=split)

    def pair(k):
        o = mark[0]
        mark[0] += 512 * k
        assert mark[0] <= ARENA, mark[0]
        v = pairs_[:, o:o + 512 * k].rearrange("p (h k t) -> p h k t", h=2, k=k)
        return Cut(v[:, 0], v[:, 1], [()] * k)

    def part(X, a, b):
        return Cut(X.hi[:, a:b], X.lo[:, a:b], [()] * (b - a))

    st_at = [0]

    def cols(n):
        o = st_at[0]
        st_at[0] += n
        assert st_at[0] <= 400
        return stat[:, o:o + n]

    def C(name):
        o, n = CAT[name]
        return cst[:, o:o + n]

    def vcol(name, i=0, n=1):
        return vec[:, VOFF[name] + i:VOFF[name] + i + n]

    def wide(ap, n):
        return ap.unsqueeze(1).broadcast_to([ap.shape[0], n, ap.shape[1]])

    def long(ap, n):
        return ap.unsqueeze(2).broadcast_to([ap.shape[0], ap.shape[1], n])

    read = [()] * 8
    turn = {}

    def pick(among=(4, 5, 6, 7)):
        turn[among] = turn.get(among, 0) + 1
        return among[turn[among] % len(among)]

    raw_sem = [sem(f"s_raw{i}") for i in range(RAW)]
    raw_use = [0] * RAW
    raw_free = [[()] for i in range(RAW)]
    cut_free = [[()] for i in range(WS)]
    n_issued, n_cut, n_used = [0], [0], [0]
    held = []

    def issue(p):
        i = n_issued[0] % RAW
        n_issued[0] += 1
        assert raw_free[i][0] is not None
        raw_use[i] += 1
        cols_ = p.nk * p.n
        view = lambda t, o=0: t[:, o:o + cols_].rearrange("p (k n) -> p k n", k=p.nk)
        src = p.src.rearrange("(k p) n -> p k n", p=128)
        SP.dma(lambda e: e.dma_start(view(raw[i]), src), raw_sem[i], raw_free[i][0])
        t = Tok(raw_sem[i], 16 * raw_use[i])
        raw_free[i][0] = None
        if p.raw:
            held.append(Held(view(raw[i]), None, t, p.k0, p.nk, raw_free[i], i))
            return
        j = n_cut[0] % WS
        n_cut[0] += 1
        assert cut_free[j][0] is not None
        hi, lo = cut[j][:, 0:cols_], cut[j][:, PIECE:PIECE + cols_]
        ta = A(lambda e: e.activation(hi, raw[i][:, 0:cols_], ACT.Copy), t, cut_free[j][0])
        tv = V(lambda e: e.tensor_tensor(lo, raw[i][:, 0:cols_], hi.bitcast(F32), ALU.subtract), ta)
        raw_free[i][0] = (ta, tv)
        cut_free[j][0] = None
        held.append(Held(view(cut[j]), view(cut[j], PIECE), (ta, tv), p.k0, p.nk, cut_free[j], j))

    def need(p):
        n = n_used[0]
        n_used[0] += 1
        if not final:
            plan.append(p)
            issue(p)
        while final and n_issued[0] < min(n + AHEAD + 1, len(plan)):
            issue(plan[n_issued[0]])
        return held[n]

    def done(h, *toks):
        h.free[0] = toks

    def pieces(w, c0, n, nk, raw=False):
        per = max(1, PIECE // n)
        return [Piece(w[k0 * 128:min(k0 + per, nk) * 128, c0:c0 + n], k0, min(per, nk - k0), n, raw)
                for k0 in range(0, nk, per)]

    def fetch(dst, src, lane, name):
        s = sem(name)
        lane.dma(lambda e: e.dma_start(dst, src), s)
        return Tok(s, 16)

    def handover():
        t = [x.now() for x in lanes]
        for x in lanes:
            x.wait(t)
        return t

    def vtt(o, a, b, op, *after):
        return V(lambda e: e.tensor_tensor(o, a, b, op), *after)

    def vts(o, a, s1, s2, op0, op1, *after):
        if s2 is None:
            return V(lambda e: e.tensor_scalar(o, a, s1, None, op0), *after)
        return V(lambda e: e.tensor_scalar(o, a, s1, s2, op0, op1), *after)

    def stt(o, a, s, b, op0, op1, *after):
        return V(lambda e: e.scalar_tensor_tensor(out=o, in0=a, scalar=s, in1=b, op0=op0, op1=op1), *after)

    def vcopy(o, a, *after):
        return V(lambda e: e.tensor_copy(o, a), *after)

    def act(o, a, f, *after, **kw):
        return A(lambda e: e.activation(o, a, f, **kw), *after)

    def mms(jobs, *after):
        def emit(e):
            for o, l, r, s0, s1 in jobs:
                last = e.matmul(o, l, r, start=s0, stop=s1, skip_group_check=True)
            return last
        return PE(emit, *after)

    waited = set()

    def sweep(steps, *after):
        jobs, toks = [], list(after)
        for need_, more in steps:
            new = [t for t in flat([need_]) if t not in waited]
            if new and jobs:
                mms(jobs, toks)
                jobs, toks = [], []
            waited.update(new)
            toks += new
            jobs += more
        return mms(jobs, toks)

    def in_turn(front, back, n=4):
        for i in range(n + 1):
            if i < n:
                front(i)
            if i >= 1:
                back(i - 1)

    def mm3(o, l, r, start, stop):
        return [(o, l[0], r[0], start, False), (o, l[0], r[1], False, False), (o, l[1], r[0], False, stop)]

    def cut_pair(dst, src, *after):
        hi, lo = dst.hi, dst.lo
        n = src.shape[1]
        ts = []
        for k in range(0, n, 2):
            e_ = min(k + 2, n)
            ta = act(hi[:, k:e_, :], src[:, k:e_, :], ACT.Copy, *after)
            ts.append(vtt(lo[:, k:e_, :], src[:, k:e_, :], hi[:, k:e_, :].bitcast(F32), ALU.subtract, ta))
            dst.toks[k:e_] = [ts[-1]] * (e_ - k)
        return ts

    def chain(o, pairs):
        n = len(pairs)
        return [(o, l, r, i == 0, i == n - 1) for i, (l, r) in enumerate(pairs)]

    def turned(jobs, *after):
        def emit(e):
            for o, i in jobs:
                last = e.transpose(o, i, C("ident")[0:i.shape[0], 0:i.shape[0]])
            return last
        return PE(emit, *after)

    def inv_root(sums, n, d, eps, dst, *after):
        t = act(dst, sums, ACT.Sqrt, *after, t_cst, scale=1.0 / d, bias=C("eps")[:, EPSILONS.index(eps):EPSILONS.index(eps) + 1])
        return t, V(lambda e: e.reciprocal(dst, dst), t)

    def ones_sum(srcs, n, b, *after):
        return mms(chain(bank[b][:, 0:n], [(C("ones"), s) for s in srcs]), *after, read[b])

    YHY = mem(1024, 4)
    HL = pair(8)
    RS = mem(512)
    cc = mem(16)
    sc = mem(16, 8)
    t_cc = fetch(cc, D["cc"], A, "s_cc")
    XC = mem(2048, 8)
    after_xc = mark[0]
    HF = mem(5120)
    DF = mem(2560)
    DFf = DF[:, 0:1536].rearrange("p (k n) -> p k n", k=2)
    DFi = DF[:, 1536:2560].rearrange("p (k n) -> p k n", k=4)
    keep_after_filters = mark[0]

    w3 = mem(2048)
    dec = mem(4096, 2)
    dcy = mem(2048)
    take = lambda o, n: arena[:, o:o + n]
    w1, w2, h64, pemb = take(0, 64), take(64, 64), take(128, 3), take(256, 256)
    ang, kk = take(512, 256), take(768, 256)
    hid = mem(256)
    t_w1 = fetch(w1[0:33, :], D["hy_pos_w1"], A, "s_w1")
    t_pe = fetch(pemb[0:33, :], D["posemb"], A, "s_pemb")
    t_h64 = fetch(h64[0:64, :], D["hy64"], A, "s_h64")
    t_w2 = fetch(w2[0:64, :], D["hy_pos_w2"], A, "s_w2")
    t_cst = fetch(cst[:, :], D["consts"], SP, "s_cst")
    t_dcy = fetch(dcy, D["hy_decay"].partition_broadcast(128), SP, "s_dcy")
    t_w3 = fetch(w3[0:64, :], D["hy_pos_w3"], SP, "s_w3")
    t_vec = fetch(vec[:, :], D["vecs"], A, "s_vec")
    t_dft = fetch(DF, D["dft"], A, "s_dft")
    t_x = fetch(XT, D["xT"], A, "s_x")
    t_xc = fetch(XC, D["ctxT"], A, "s_xc")

    t = act(sc.rearrange("p k c -> p (k c)"), cc, ACT.Silu, t_cc)
    sc4 = sct[:, 0:32].rearrange("p (k h c) -> p k h c", k=8, h=2)
    t_sc = [vcopy(sc4[:, :, 0, :], sc, t)]
    t_sc.append(vtt(sc4[:, :, 1, :], sc, sc4[:, :, 0, :].bitcast(F32), ALU.subtract, t_sc))
    t_sc.append(vcopy(sct[:, 32:156], sc[:, 0, 0:1].broadcast_to([128, 124]), t))

    mod_row, row_read, late = {}, {0: (), 1: ()}, []

    def mod_columns():
        while late:
            c = late.pop(0)
            t = mms([(bank[0][:, 2 * (4 * c + m):2 * (4 * c + m) + 2], mrow[0:4, 512 * (c % 2) + 128 * m:512 * (c % 2) + 128 * m + 128],
                      C("fold")[0:4, :], True, True) for m in range(4)], mod_row[c], t_cst, read[0])
            row_read[c % 2] = t

    def mod_chunk(c):
        jobs = []
        for p in pieces(D["w_mod"], 512 * c, 512, 8):
            w = need(p)
            t = mms([(bank[1][:, :], sct[:, 4 * (p.k0 + k):4 * (p.k0 + k) + 128], x[:, k, :], p.k0 + k == 0 and i == 0,
                      p.k0 + k == 7 and i == 1) for k in range(p.nk) for i, x in enumerate((w.hi, w.lo))],
                    w.tok, t_sc, read[1])
            done(w, t)
        mod_columns()
        mod_row[c] = act(mrow[0:4, 512 * (c % 2):512 * (c % 2) + 512], bank[1][0:4, :], ACT.Copy, t, row_read[c % 2])
        read[1] = (mod_row[c],)
        late.append(c)

    def reduce_angle(r, a, k, *after):
        t = vts(k, a, 1 / TWO_PI, MAGIC, ALU.mult, ALU.add, *after)
        t = vts(k, k, MAGIC, None, ALU.subtract, None, t)
        t = stt(r, k, -C1, a, ALU.mult, ALU.add, t)
        t = stt(r, k, -C2, r, ALU.mult, ALU.add, t)
        return stt(r, k, -C3, r, ALU.mult, ALU.add, t)

    mod_chunk(0)
    t = mms(chain(bank[4][0:64, 0:256], [(w1[0:33, :], pemb[0:33, :])]), t_w1, t_pe)
    for layer in range(2):
        b = 4 + layer
        t = vts(ang[0:64, :], bank[b][0:64, 0:256], h64[0:64, 2 * layer:2 * layer + 1] if layer else h64[0:64, 0:1],
                h64[0:64, 1:2], ALU.add, ALU.mult, t, t_h64)
        t = reduce_angle(ang[0:64, :], ang[0:64, :], kk[0:64, :], t)
        t = vts(ang[0:64, :], ang[0:64, :], PI_F, -PI_F, ALU.min, ALU.max, t)
        t = act(hid[0:64, :], ang[0:64, :], ACT.Sin, t)
        if layer == 0:
            t = mms(chain(bank[5][0:64, 0:256], [(w2[0:64, :], hid[0:64, :])]), t, t_w2)
    t_hid = t
    t = act(dcy, dcy, ACT.Abs, t_dcy)
    t_dec = []
    for i in range(2):
        t_dec.append(act(dec[:, i, :], dcy, ACT.Exp, t, t_cst, scale=C("negt")[:, i:i + 1]))
    F = arena[:, 1024:5120].rearrange("p (i n) -> p i n", i=2)
    t_f = []
    for i in range(2):
        for q in range(4):
            b = pick()
            t = mms(chain(bank[b][:, :], [(hid[0:64, i * 128:i * 128 + 128], w3[0:64, q * 512:q * 512 + 512])]),
                    t_hid, t_w3, read[b])
            dst, dd = F[:, i, q * 512:q * 512 + 512], dec[:, i, q * 512:q * 512 + 512]
            if i == 0 and q % 2 == 1:
                t = stt(dst, bank[b][:, :], C("row0"), dd, ALU.mult, ALU.mult, t, t_dec[i])
            else:
                t = vtt(dst, bank[b][:, :], dd, ALU.mult, t, t_dec[i])
            read[b] = (t,)
            t_f.append(t)
    last_filter = PE.now()
    PM = dec[:, :, :].rearrange("p i n -> p (i n)").rearrange("p (s i o n) -> p s i o n", s=2, i=2, o=2)
    AB = w3.rearrange("p (i d n) -> p i d n", i=2, d=2)
    recn = cols(1)
    rec = dcy[:, 0:512]
    t_abs_read = last_filter
    hf_off = {"A0": 0, "A1": 1, "B0": 2, "B1": 3, "D0": 4}

    def Hf(o, name):
        k = 5 * o + hf_off[name]
        return HF[:, 512 * k:512 * k + 512]

    t_pm = {0: [], 1: []}
    t_abs = {}

    def taps(o):
        return [[F[:, i, (2 * o + d) * 512:(2 * o + d) * 512 + 512] for i in range(2)] for d in range(2)]

    def absolute(o):
        t_abs[o] = [act(AB[:, i, d, :], taps(o)[d][i], ACT.Abs, t_f, t_abs_read) for i in range(2) for d in range(2)]

    absolute(0)
    for o in range(2):
        for i in range(2):
            for s, op in ((0, ALU.add), (1, ALU.subtract)):
                t_pm[o].append(vtt(PM[:, s, i, o, :], taps(o)[0][i], taps(o)[1][i], op, t_f))
    mod_chunk(1)
    mod_chunk(2)
    t_hf = []
    for o in range(2):
        rec = dcy[:, 512 * o:512 * o + 512]
        b = pick((2, 3))
        t = ones_sum([AB[:, i, d, :] for i in range(2) for d in range(2)], 512, b, t_abs[o], t_cst)
        t_abs_read = t
        t = vts(rec, bank[b][:, :], EPS, None, ALU.add, None, t, t_dec)
        read[b] = (t,)
        t_rec = V(lambda e, rec=rec: e.reciprocal(rec, rec), t)
        if o == 0:
            absolute(1)
        for name, c0, s in (("A0", 0, 0), ("A1", 128, 0), ("B0", 256, 1), ("B1", 384, 1), ("D0", 640, 0)):
            b = pick()
            t = mms(chain(bank[b][:, :], [(DFf[:, i, c0:c0 + 128], PM[:, s, i, o, :]) for i in range(2)]),
                    t_pm[o], t_dft, read[b])
            t = vtt(Hf(o, name), bank[b][:, :], rec, ALU.mult, t, t_rec)
            read[b] = (t,)
            t_hf.append(t)

    def sum_by_parts(b, X, toks):
        for j in range(4):
            t = mms([(bank[b][:, 0:NT], C("ones"), X[:, k, :], k == 0, k == 7) for k in (2 * j, 2 * j + 1)],
                    toks[j], t_cst, read[b])
        return t

    def inverse_rms(X, SQ, rs, *after):
        ts = [act(SQ[:, j:j + 2, :], X[:, j:j + 2, :], ACT.Square, *after) for j in range(0, 8, 2)]
        b = pick()
        t = sum_by_parts(b, SQ, ts)
        t_r, t = inv_root(bank[b][:, 0:NT], NT, 1024, EPS, rs, t)
        read[b] = (t_r,)
        return t

    rms_x, rms_c = RS[:, 0:NT], RS[:, NT:2 * NT]
    t_rx = inverse_rms(XT, arena[:, 2048:4096].rearrange("p (k t) -> p k t", k=8), rms_x, t_x, t_pm[0], t_pm[1], t_abs[1])
    mod_chunk(3)
    t_rc = inverse_rms(XC, arena[:, 2048:4096].rearrange("p (k t) -> p k t", k=8), rms_c, t_xc, t_rx)
    mod = modt[:, :].rearrange("p (m c) -> p m c", c=2)

    def mod_ready(c0, c1):
        a, z = 4 * c0, 4 * c1
        mod_columns()
        t = vtt(mod[:, a:z, :], bank[0][:, 2 * a:2 * z].rearrange("p (m c) -> p m c", c=2),
                long(vcol("b_mod", a, z - a), 2), ALU.add, PE.now(), t_vec)
        read[0] = (t,)
        return t

    t_mod = mod_ready(0, 4)

    handover()
    mark[0] = keep_after_filters

    T1 = mem(2048, 8)
    scl = cols(24)

    def modulated(X, rs, t_rs, scale_cols, gname, shift, dst, *after):
        t_s = stt(scale_cols, shift[1], 1.0, vcol(gname, 0, 8), ALU.add, ALU.mult, t_mod)
        t1 = {}

        def front(i):
            t1[i] = vtt(T1[:, 2 * i:2 * i + 2, :], X[:, 2 * i:2 * i + 2, :], wide(rs, 2), ALU.mult, t_rs, *after)

        def back(i):
            j = 2 * i
            t2 = [act(T1[:, k, :], T1[:, k, :], ACT.Identity, t1[i], t_s, scale=scale_cols[:, k:k + 1],
                      bias=shift[0][:, k:k + 1]) for k in (j, j + 1)]
            dst.toks[j:j + 2] = cut_pair(part(dst, j, j + 2), T1[:, j:j + 2, :], t2) * 2

        in_turn(front, back)
        return tuple(dst.toks)

    t_h = modulated(XT, rms_x, t_rx, scl[:, 0:8], "norm1_g", (mod[:, 0:8, 0], mod[:, 8:16, 0]), HL, t_x)

    def project(w, c0, tiles, Xs, nk, evac, *after, width=128, banks=(4, 5, 6, 7),
                lag=None, beside=None):
        per = 4 // len(Xs) if width == 128 else tiles
        for t0 in range(0, tiles, per):
            nt = min(per, tiles - t0)
            units = [(j, X) for j in range(nt) for X in Xs]
            bs = [pick(banks) for _ in range(0, len(units), 2)]
            last = {}
            for p in pieces(w, c0 + t0 * width, nt * width, nk):
                h = need(p)
                for i, b in enumerate(bs):
                    steps = []
                    for u, (j, X) in enumerate(units[2 * i:2 * i + 2]):
                        for k in range(p.nk):
                            c = slice(j * width, j * width + width)
                            steps.append((X.toks[p.k0 + k],
                                          mm3(bank[b][0:width, u * 256:u * 256 + 256], (h.hi[:, k, c], h.lo[:, k, c]),
                                              (X[0][:, p.k0 + k, :], X[1][:, p.k0 + k, :]),
                                              p.k0 + k == 0 and u == 0, p.k0 + k == nk - 1)))
                    last[i] = t = sweep(steps, h.tok, after, read[b])
                done(h, t)
                step()
            flush()
            for i, b in enumerate(bs):
                if lag:
                    lagging.append(lagged(evac, t0 + 2 * i // len(Xs), b, last[i]))
                else:
                    read[b] = evac(t0 + 2 * i // len(Xs), b, last[i])
            step()
            if beside:
                beside.pop(0)()
        if lag != "on":
            flush()
        return t

    lagging = []

    def lagged(evac, m, b, t):
        read[b] = yield from evac(m, b, t)

    def step():
        for g in lagging[:2]:
            if next(g, g) is g:
                lagging.remove(g)

    def flush():
        while lagging:
            step()

    def whole(g):
        while True:
            try:
                next(g)
            except StopIteration as end:
                return end.value

    def token_major(w, c0, n, Xs, nk, dst, *after, wait=()):
        per = 512 // n
        bs = [pick() for _ in range(0, len(Xs), per)]
        for p in pieces(w, c0, n, nk):
            h = need(p)
            jobs = []
            for i, X in enumerate(Xs):
                o = bank[bs[i // per]][:, (i % per) * n:(i % per) * n + n]
                for k in range(p.nk):
                    jobs += mm3(o, X(p.k0 + k), (h.hi[:, k, :], h.lo[:, k, :]),
                                p.k0 + k == 0 and i % per == 0, p.k0 + k == nk - 1)
            t = mms(jobs, h.tok, [X.toks for X in wait], after, [read[b] for b in bs])
            done(h, t)
            step()
        flush()
        ts = []
        for i, b in enumerate(bs):
            t = act(dst(i * per), bank[b][:, 0:per * n].rearrange("p (i n) -> p i n", i=per), ACT.Copy, t)
            read[b] = (t,)
            ts.append(t)
        return ts

    def tokens_of(X, i):
        return lambda k: tuple(x[:, k, i * 128:i * 128 + 128] for x in X[:2])

    W = D["w_in"]

    UV = mem(3072, 12)
    t_uv = []

    def conv_evac(base):
        def evac(m0, b, t):
            ts, t1 = [], []
            for j in range(2):
                m = base + m0 + j
                t1.append(act(UV[:, m, :], bank[b][:, j * 256:j * 256 + 256], ACT.Identity, t,
                              scale=vcol("hy_conv_w", 12 + m), bias=vcol("hy_conv_b", m)))
            for j in range(2):
                m = base + m0 + j
                src = bank[b][:, j * 256:j * 256 + 256]
                dst = UV[:, m, :]
                t2 = stt(dst[:, 1:256], src[:, 0:255], vcol("hy_conv_w", m), dst[:, 1:256], ALU.mult, ALU.add, t1)
                t3 = stt(dst[:, 0:255], src[:, 1:256], vcol("hy_conv_w", 24 + m), dst[:, 0:255], ALU.mult, ALU.add, t2)
                ts.append(t3)
            t_uv.extend(ts)
            return tuple(ts)
        return evac

    for c in (2, 0, 1):
        project(W, 3104 + 512 * c, 4, (HL,), 8, conv_evac(4 * c), t_vec)

    ZT = mem(1024, 2)
    XF = T1.rearrange("p (j a) t -> p j (a t)", j=4)
    YF = mem(2048, 4)
    TP = mem(512)
    hy = {}

    def hyena_spectrum(o, z, *after):
        tz = []
        for i in range(2):
            b = pick()
            t = turned([(bank[b][:, c * 128:c * 128 + 128], z[:, c, i * 128:i * 128 + 128]) for c in range(4)],
                       *after, t_cst, read[b])
            t = act(ZT[:, i, :], bank[b][:, :], ACT.Copy, t, hy.get("zt", ()))
            read[b] = (t,)
            tz.append(t)
        tx = []
        for j, c0 in enumerate((0, 128, 512, 384)):
            b = pick()
            t = mms(chain(bank[b][:, :], [(DFf[:, i, c0:c0 + 128], ZT[:, i, :]) for i in range(2)]), tz, read[b])
            hy["zt"] = t
            t = act(XF[:, j, :], bank[b][:, :], ACT.Copy, t, hy.get("xf", ()))
            read[b] = (t,)
            tx.append(t)
        ty = []
        for j in range(2):
            R, I = XF[:, j, :], XF[:, 2 + j, :]
            a, bb = Hf(o, f"A{j}"), Hf(o, f"B{j}")
            d = Hf(o, "D0") if j == 0 else a
            t = vtt(YF[:, j, :], R, a, ALU.mult, tx, hy.get("yf", ()))
            t2 = vtt(TP, I, bb, ALU.mult, t)
            t = vtt(YF[:, j, :], YF[:, j, :], TP, ALU.subtract, t2)
            t2 = vtt(YF[:, 2 + j, :], R, bb, ALU.mult, t)
            t3 = vtt(TP, I, d, ALU.mult, t2)
            t4 = vtt(YF[:, 2 + j, :], YF[:, 2 + j, :], TP, ALU.add, t3)
            ty += [t, t4]
        hy["xf"] = t4
        mod_chunk(5 + o)
        return ty

    def hyena_back(o, z, gate, dst, ty):
        res = []
        for c0 in (0, 2):
            b = pick()
            jobs = []
            for c in (c0, c0 + 1):
                jobs += chain(bank[b][:, (c - c0) * 256:(c - c0) * 256 + 256],
                              [(YF[:, j, c * 128:c * 128 + 128], DFi[:, j, :]) for j in range(4)])
            t = mms(jobs, ty, read[b])
            hy["yf"] = t
            if c0 == 2 and o == 0:
                mod_chunk(4)
            rs = []
            for c in (c0, c0 + 1):
                t1 = stt(z[:, c, :], z[:, c, :], vcol("hy_skip", 4 * o + c),
                         bank[b][:, (c - c0) * 256:(c - c0) * 256 + 256], ALU.mult, ALU.add, t)
                rs.append(t1)
                res.append(vtt(dst[:, c, :], z[:, c, :], gate[:, c, :], ALU.mult, t1))
            read[b] = tuple(rs)
        return res

    z = UV[:, 8:12, :]
    ty = hyena_spectrum(0, z, t_uv)
    tz1 = hyena_back(0, z, UV[:, 0:4, :], z, ty)
    ty = hyena_spectrum(1, z, tz1)
    t_yhy = hyena_back(1, z, UV[:, 4:8, :], YHY, ty)

    handover()
    mark[0] = after_xc
    T1 = mem(2048, 8)
    after_t1 = mark[0]
    HR = pair(8)
    keep_hr = mark[0]
    YATT = T1
    t_hc = modulated(XC, rms_c, t_rc, scl[:, 8:16], "norm1_g", (mod[:, 0:8, 1], mod[:, 8:16, 1]), HR, t_xc)
    mod_chunk(7)
    TOK4 = [tokens_of(X, i) for X in (HL, HR) for i in range(2)]
    KT = mem(1024, 2)
    VV = mem(1024, 4)
    QT = mem(2048, 8)
    RQ = mem(512)
    RR = mem(512)
    RN = mem(512)
    RC = mem(512)

    hn = {}
    roots = [cols(4), cols(4)]
    spare = [(2, 3)]

    def rope(src, n, R, cos, sin, dst, parts, *after, rows=None, slot=0):
        lo, hi = rows or (0, parts)
        b = pick(spare[0])
        t = mms(chain(bank[b][0:parts, 0:n * 256], [(R, src)]), *after, read[b])
        s3 = src.rearrange("p (n t) -> p n t", n=n)
        c3 = RC_[slot][:, 0:n * 256].rearrange("p (n t) -> p n t", n=n)
        b3 = bank[b][:, 0:n * 256].rearrange("p (n t) -> p n t", n=n)
        t2 = vtt(dst[lo:hi], s3[lo:hi], wide(cos[lo:hi, :], n), ALU.mult, *after)
        yield
        t1 = vtt(c3[lo:hi], b3[lo:hi], wide(sin[lo:hi, :], n), ALU.mult, t, hn.get(("rc", slot), ()))
        read[b] = (t1,)
        t3 = vtt(dst[lo:hi], dst[lo:hi], c3[lo:hi], ALU.add, t2, t1)
        hn[("rc", slot)] = t3
        return t3, t

    def head_norm(b, tok, gcol, dst, n, d=128, eps=EPS, among=None, slot=0):
        rq, rr, rt = RQ_[slot][:, 0:n], RR_[slot][:, 0:n], roots[slot]
        m = n // 128
        t0 = act(dst, bank[b][:, 0:n], ACT.Copy, tok, hn.get(("rn", slot), ()))
        read[b] = (t0,)
        t1 = act(rq, dst, ACT.Square, t0, hn.get(("rq", slot), ()))
        yield
        b2 = pick(among or spare[0])
        t = mms([(bank[b2][:, i:i + 1], rq[:, 128 * i:128 * i + 128], C("ones")[:, 0:1], True, True) for i in range(m)],
                t1, t_cst, read[b2])
        hn[("rq", slot)] = t
        t_r, t = inv_root(bank[b2][:, 0:m], m, d, eps, rt, t, hn.get(("rr", slot), ()))
        r3 = rr.rearrange("p (m t) -> p m t", m=m)
        t = vtt(r3, wide(C("ident"), m), long(rt, 128), ALU.mult, t)
        yield
        t2 = mms([(bank[b2][:, 0:n], C("ones"), rr, True, True)], t, t_r)
        t = stt(dst, dst, gcol, bank[b2][:, 0:n], ALU.mult, ALU.mult, t2)
        read[b2] = (t,)
        hn[("rr", slot)] = t
        return t

    RQ_, RR_, RN_, RC_ = ([a, T1[:, 2 * i:2 * i + 2, :].rearrange("p a t -> p (a t)")]
                          for i, a in enumerate((RQ, RR, RN, RC)))
    for name in ("rq", "rr", "rn", "rc"):
        hn[(name, 1)] = t_hc
    t_k = []

    def evac(h, b, t):
        rn = RN_[h]
        t = yield from head_norm(b, t, vcol("k_norm_g"), rn, 512, slot=h)
        t3 = vcopy(KT[:, h, 256:512], rn[:, 256:512], t)
        t1, t2 = yield from rope(rn[:, 0:256], 1, C("Rax"), C("cosx"), C("sinx"), KT[:, h:h + 1, 0:256], 128, t, slot=h)
        hn[("rn", h)] = (t1, t2, t3)
        t_k.extend([t1, t3])
        return read[b]
    project(W, 0, 2, (HL, HR), 8, evac, lag="on")
    t_v = token_major(W, 256, 256, TOK4, 8, lambda i: VV[:, i:i + 2, :], wait=(HL, HR))
    t_q = []

    def evac(m, b, t):
        i = m // 2 % 2
        t = yield from head_norm(b, t, vcol("q_norm_g"), RN_[i], 512, slot=i)
        t1, t2 = yield from rope(RN_[i], 2, C("Rax"), C("cosx"), C("sinx"), QT[:, m:m + 2, :], 128, t, slot=i)
        hn[("rn", i)] = (t1, t2)
        t_q.append(t1)
        return read[b]
    project(W, 1312, 8, (HL,), 8, evac, lag=True)

    E_ = [mem(512), mem(512), mem(512)]
    PT_ = [mem(512), mem(512)]
    at = {}

    def softmax(u, b, tok, g, scale, masked=False, E=None, key="e", factor=None,
                plus=None):
        n = 512 // g
        c = cols(4 * g)
        mx, nm, l, r = (c[:, g * i:g * i + g] for i in range(4))
        src = bank[b][:, :].rearrange("p (g n) -> p g n", g=g)
        e3 = E.rearrange("p (g n) -> p g n", g=g)
        held = at.get((key, u % 3), ())
        if masked:
            tok = stt(E, bank[b][:, :], scale, AM[:, 512:1024], ALU.mult, ALU.add, tok, held)
            read[b] = (tok,)
            src, scale = e3, 1.0
        t = V(lambda e: e.tensor_reduce(mx, src, AX.X, ALU.max), tok)
        t = vts(nm, mx, -scale, None, ALU.mult, None, t)
        te = []
        for i in range(g):
            kw = {} if masked else {"accum_out": l[:, i:i + 1]}
            te.append(A(lambda e, i=i, kw=kw: e.activation(e3[:, i, :], src[:, i, :], ACT.Exp, bias=nm[:, i:i + 1],
                                                         scale=scale, **kw), t, held))
        if not masked:
            read[b] = (te[-1], t)

        def tail(*after):
            t = te
            if masked:
                t = vtt(E, E, AM[:, 0:512], ALU.mult, te)
                t = V(lambda e: e.tensor_reduce(l, e3, AX.X, ALU.add), t)
            t = V(lambda e: e.reciprocal(r, l), t)
            if factor is not None:
                t = vts(r, r, factor, None, ALU.mult, None, t)
            for i in range(g):
                if plus is not None:
                    t2 = stt(e3[:, i, :], e3[:, i, :], r[:, i:i + 1], plus[:, i * n:i * n + n], ALU.mult, ALU.add,
                             t, *after)
                else:
                    t2 = vts(e3[:, i, :], e3[:, i, :], r[:, i:i + 1], None, ALU.mult, None, t)
            return t2
        return tail

    def flip(u, E, tok, order):
        b = 6 + u % 2
        t = turned([(bank[b][:, j * 128:j * 128 + 128], E[:, o * 128:o * 128 + 128]) for j, o in enumerate(order)],
                   tok, t_cst, read[b])
        at[("e", u % 3)] = t
        t = act(PT_[u % 2], bank[b][:, :], ACT.Copy, t, at.get(("pt", u % 2), ()))
        read[b] = (t,)
        return t

    def staged(n, first, second, third):
        a, b = {}, {}
        for i in range(n + 3):
            if i < n:
                a[i] = first(i)
            if 1 <= i <= n:
                a[i - 1] = a[i - 1]()
            if 2 <= i <= n + 1:
                b[i - 2] = second(i - 2, a[i - 2])
            if i >= 3:
                third(i - 3, b[i - 3])
            step()
        flush()

    t_yatt = []

    def first(u):
        h, i = u // 2, u % 2
        b = 4 + u % 2
        t = mms(chain(bank[b][:, :], [(QT[:, h, i * 128:i * 128 + 128], KT[:, h // 4, :])]), t_q, t_k, read[b])
        return softmax(u, b, t, 1, 128 ** -0.5, E=E_[u % 3])

    def second(u, t):
        return flip(u, E_[u % 3], t, (0, 1, 2, 3))

    def third(u, t):
        h, i = u // 2, u % 2
        b = 2 + u % 2
        PT = PT_[u % 2]
        t = mms(chain(bank[b][:, 0:128], [(VV[:, j, (h // 4) * 128:(h // 4) * 128 + 128], PT[:, j * 128:j * 128 + 128])
                                          for j in range(4)]), t, t_v, read[b])
        at[("pt", u % 2)] = t
        t = act(YATT[:, h, i * 128:i * 128 + 128], bank[b][:, 0:128], ACT.Copy, t)
        read[b] = (t,)
        t_yatt.append(t)

    staged(16, first, second, third)

    handover()
    mark[0] = keep_hr
    YGLA = XC[:, 0:4, :]
    OG = XC[:, 4:8, :]
    GKT = mem(1024, 2)
    GKK = mem(1024, 4)
    GV = mem(2048, 4)
    GA = mem(512)
    GQ = mem(512, 2)
    LA = mem(2048, 4)
    W2 = mem(512)
    W2B = mem(512)
    EP = mem(1024).rearrange("p (d j t) -> p d j t", d=2, j=2)
    EN = mem(1024).rearrange("p (d j t) -> p d j t", d=2, j=2)
    o_hr = keep_hr - 4096
    KE = arena[:, o_hr:o_hr + 2048].rearrange("p (i d f) -> p i d f", i=4, d=2)
    SS = arena[:, o_hr + 2048:o_hr + 4096].rearrange("p (d j c v) -> p d j c v", d=2, j=2, c=4)
    LAf = LA.rearrange("p i n -> p (i n)")
    AT = [LAf[:, 0:512], LAf[:, 512:1024]]
    hn = {}
    hand = [x.now() for x in lanes]
    s_w2 = sem("s_w2z")
    G.dma(lambda e: e.dma_start(W2[96:128, :], D["w2z"][0:32, :]), s_w2, hand)
    G.dma(lambda e: e.dma_start(W2B[96:97, :], D["w2z"][32:33, :]), s_w2, hand)
    t_w2z = Tok(s_w2, 32)

    t_gk, t_ga = [], []

    def evac(j, b, t):
        t = act(GKT[:, j, :], bank[b][:, :], ACT.Copy, t)
        t_gk.append(t)
        return (t,)
    project(W, 512, 2, (HL, HR), 8, evac)

    def evac(j, b, t):
        t = act(GA[96:128, :], bank[b][96:128, :], ACT.Copy, t)
        t_ga.append(t)
        return (t,)
    project(W, 1184, 1, (HL, HR), 8, evac)
    t_gv = token_major(W, 768, 512, TOK4, 8, lambda i: GV[:, i:i + 1, :], wait=(HL, HR))
    hr_read = PE.now()
    t_la = []
    for i in range(4):
        b = pick()
        t = mms(chain(bank[b][:, :], [(GA[96:128, i * 128:i * 128 + 128], W2[96:128, :]),
                                      (C("ones")[96:97, :], W2B[96:97, :])]), t_ga, t_w2z, read[b])
        lw = EP.rearrange("p d j t -> p (d j t)")[:, (i % 2) * 512:(i % 2) * 512 + 512]
        t2 = act(lw, bank[b][:, :], ACT.Abs, t, hn.get(("lw", i % 2), ()))
        t1 = vts(LA[:, i, :], bank[b][:, :], 0.0, None, ALU.min, None, t2)
        read[b] = (t1, t2)
        t = act(lw, lw, ACT.Exp, t2, scale=-1.0)
        t = act(lw, lw, ACT.Ln, t, bias=1.0)
        t = vtt(LA[:, i, :], LA[:, i, :], lw, ALU.subtract, t, t1)
        hn[("lw", i % 2)] = t
        t_la.append(t)
    t_kk = []
    for i0 in (0, 2):
        b = pick()
        t = turned([(bank[b][:, (i - i0) * 256 + j * 128:(i - i0) * 256 + j * 128 + 128],
                     GKT[:, j, i * 128:i * 128 + 128]) for i in (i0, i0 + 1) for j in range(2)],
                   t_gk, t_cst, read[b])
        t = act(GKK[:, i0:i0 + 2, :], bank[b][:, :].rearrange("p (i n) -> p i n", i=2), ACT.Copy, t)
        read[b] = (t,)
        t_kk.append(t)
    t_gq = []

    def evac(m0, b, t):
        t = act(GQ, bank[b][:, :].rearrange("p (j t) -> p j t", j=2), ACT.Copy, t)
        t_gq.append(t)
        return (t,)
    project(W, 2336, 2, (HL,), 8, evac)
    t_ep, t_en = [], []
    for d, name in enumerate(("Tf", "Tb")):
        b = pick()
        jobs = []
        for j in range(2):
            for i in range(2):
                o = j * 256 + i * 128
                jobs += chain(bank[b][:, o:o + 128], [(LA[:, i, d * 256 + j * 128:d * 256 + j * 128 + 128], C(name))])
        t = mms(jobs, t_la, t_cst, read[b])
        src = bank[b][:, :].rearrange("p (j t) -> p j t", j=2)
        t1 = act(EP[:, d, :, :], src, ACT.Exp, t, t_la, scale=1 / 16)
        t2 = act(EN[:, d, :, :], src, ACT.Exp, t, scale=-1 / 16)
        read[b] = (t1, t2)
        t_ep.append(t1)
        t_en.append(t2)
    t_ke = []
    for i in range(4):
        b = pick()
        jobs = []
        for d in range(2):
            name = ("SG" if i < 2 else "SF") + "fb"[d]
            pairs = [(C(name), LA[:, i, d * 256:d * 256 + 256])]
            if (i, d) == (2, 0):
                pairs.append((C("ones"), LA[:, 3, 0:256]))
            if (i, d) == (3, 1):
                pairs.append((C("ones"), LA[:, 2, 256:512]))
            jobs += chain(bank[b][:, d * 256:d * 256 + 256], pairs)
        t = mms(jobs, read[b])
        t = act(KE[:, i, :, :], bank[b][:, :].rearrange("p (d f) -> p d f", d=2), ACT.Exp, t, hr_read, scale=1 / 16)
        read[b] = (t,)
        t_ke.append(vtt(KE[:, i, :, :], KE[:, i, :, :], wide(GKK[:, i, :], 2), ALU.mult, t, t_kk))
    DC = cols(16).rearrange("p (d j c) -> p d j c", d=2, j=2)
    t_dc = [vcopy(DC[:, d, :, :], EP[:, d, :, (63 if d == 0 else 0)::64], t_ep) for d in range(2)]
    t_qd = [stt(EP[:, d, :, :], GQ, 0.125, EP[:, d, :, :], ALU.mult, ALU.mult, t_gq, t_dc) for d in range(2)]
    t_ki = [vtt(EN[:, d, :, :], GKT[:, :, 0:256], EN[:, d, :, :], ALU.mult, t_gk, t_en) for d in range(2)]
    t_ss = {}
    for d in range(2):
        c0 = 0 if d == 0 else 3
        b = pick()
        jobs = []
        for j in range(2):
            jobs += chain(bank[b][:, j * 256:j * 256 + 256],
                          [(KE[:, 2 + i, d, j * 128:j * 128 + 128], GV[:, 2 + i, j * 256:j * 256 + 256]) for i in range(2)])
        t = mms(jobs, t_ke, t_gv, read[b])
        b4 = bank[b][:, :].rearrange("p (j h v) -> p j h v", j=2, h=2)
        ts = [vcopy(SS[64 * h:64 * h + 64, d, :, c0, :], b4[64 * h:64 * h + 64, :, h, :], t, hr_read)
              for h in range(2)]
        read[b] = tuple(ts)
        t_ss[d] = ts
    for n in range(3):
        for d in range(2):
            c = n if d == 0 else 3 - n
            nx = c + 1 if d == 0 else c - 1
            b = pick()
            r0 = 64 * (c % 2)
            jobs = []
            for j in range(2):
                jobs += chain(bank[b][:, j * 256:j * 256 + 256],
                              [(KE[r0:r0 + 64, c // 2, d, j * 128:j * 128 + 128],
                                GV[r0:r0 + 64, c // 2, j * 256:j * 256 + 256])])
            t = mms(jobs, t_ke, t_gv, read[b])
            ts = []
            for j in range(2):
                for h in range(2):
                    p = slice(64 * h, 64 * h + 64)
                    ts.append(stt(SS[p, d, j, nx, :], SS[p, d, j, c, :], DC[p, d, j, c:c + 1],
                                  bank[b][p, j * 256 + h * 128:j * 256 + h * 128 + 128], ALU.mult, ALU.add,
                                  t, t_ss[d], t_dc))
            read[b] = tuple(ts)
            t_ss[d] = ts
    la_read = PE.now()
    t_og = []

    def evac(m0, b, t):
        t = act(OG[:, m0:m0 + 2, :], bank[b][:, :].rearrange("p (j t) -> p j t", j=2), ACT.Silu, t)
        t_og.append(t)
        return (t,)
    project(W, 2592, 4, (HL,), 8, evac)
    t_at = {0: la_read, 1: la_read}
    maskv = cst[:, CAT["Tf"][0]:CAT["Tf"][0] + 256].rearrange("p (d t) -> p d t", d=2)
    t_ygla = []
    RQ_, RR_ = [LAf[:, 1024:1536]], [LAf[:, 1536:2048]]
    hn = {("rq", 0): la_read, ("rr", 0): la_read}
    for h in range(4):
        j, hh = h // 2, h % 2
        p = slice(64 * hh, 64 * hh + 64)
        b = 4 + h % 2
        jobs = []
        for d in range(2):
            for i in range(2):
                o = (d * 2 + i) * 128
                jobs += chain(bank[b][:, o:o + 128], [(EN[p, d, j, i * 128:i * 128 + 128],
                                                       EP[p, d, j, i * 128:i * 128 + 128])])
        t = mms(jobs, t_qd, t_ki, read[b])
        am = AT[h % 2].rearrange("p (d i t) -> p d i t", d=2, i=2)
        t = vtt(am, bank[b][:, :].rearrange("p (d i t) -> p d i t", d=2, i=2),
                maskv.unsqueeze(2).broadcast_to([128, 2, 2, 128]), ALU.mult, t, t_at.get(h % 2, ()))
        read[b] = (t,)
        bo = 2 + h // 2
        o0 = 256 * (h % 2)
        jobs = []
        for i in range(2):
            for d in range(2):
                jobs.append((bank[bo][:, o0 + i * 128:o0 + i * 128 + 128], GV[:, i, h * 128:h * 128 + 128],
                             am[:, d, i, :], i == 0 and d == 0, False))
        for d in range(2):
            for c in range(4):
                jobs.append((bank[bo][:, o0 + c * 64:o0 + c * 64 + 64], SS[p, d, j, c, :],
                             EP[p, d, j, c * 64:c * 64 + 64], False, (d, c) == (1, 3)))
        t = mms(jobs, t, t_ss[0], t_ss[1], t_gv, read[bo])
        t_at[h % 2] = t
        if h % 2 == 1:
            t = whole(head_norm(bo, t, vcol("gla_norm_g"),
                                YGLA[:, h - 1:h + 1, :].rearrange("p a t -> p (a t)"), 512, among=(6, 7)))
            t_ygla.append(vtt(YGLA[:, h - 1:h + 1, :], YGLA[:, h - 1:h + 1, :], OG[:, h - 1:h + 1, :], ALU.mult,
                              t, t_og))

    hand = handover()
    mark[0] = after_t1
    RWT = arena[:, ARENA - 144:ARENA - 16].rearrange("p (k e) -> p k e", k=8)
    RB = arena[:, ARENA - 16:ARENA]
    s_rw = sem("s_rw")
    for dst, src in ((RWT, D["router_w"].rearrange("(k p) e -> p k e", p=128)),
                     (RB, D["router_b"].partition_broadcast(128))):
        G.dma(lambda e, dst=dst, src=src: e.dma_start(dst, src), s_rw, hand)
    t_rw = Tok(s_rw, 32)
    BG = mem(6144, 24)
    MT = mem(2048, 8)
    TM = [mem(512), mem(512)]
    YS = pair(8)
    YH_, YG_ = part(YS, 0, 4), part(YS, 4, 8)
    cut_pair(YH_, YHY, t_yhy)
    cut_pair(YG_, YGLA, t_ygla)
    t_bg = {}

    def evac(m, b, t):
        t = act(BG[:, m:m + 2, :], bank[b][:, :].rearrange("p (j t) -> p j t", j=2), ACT.Sigmoid, t)
        t_bg[m] = t
        return (t,)
    project(W, 4640, 24, (HL,), 8, evac, beside=[lambda c=c: mod_chunk(c) for c in range(8, 12)])
    t_m = {}
    for br, (name, Y, nk) in enumerate((("w_br_hy", YH_, 4), ("w_br_gla", YG_, 4), ("w_br_att", YS, 8))):
        if br == 2:
            cut_pair(YS, YATT, t_yatt, PE.now())

        def evac(m, b, t):
            src = bank[b][:, :].rearrange("p (j t) -> p j t", j=2)
            g = BG[:, 8 * br + m:8 * br + m + 2, :]
            if br == 0:
                t_m[m] = vtt(MT[:, m:m + 2, :], src, g, ALU.mult, t, t_bg[8 * br + m])
                return (t_m[m],)
            x = TM[(m // 2) % 2].rearrange("p (j t) -> p j t", j=2)
            t1 = vtt(x, src, g, ALU.mult, t, t_bg[8 * br + m])
            t_m[m] = vtt(MT[:, m:m + 2, :], MT[:, m:m + 2, :], x, ALU.add, t1, t_m[m])
            return (t1,)
        project(D[name], 0, 8, (Y,), nk, evac)
    t_x1 = []

    def residual(gate0, toks):
        def evac(m0, b, t):
            ts = []
            for j in range(2):
                m = m0 + j
                ts.append(stt(XT[:, m, :], bank[b][:, j * 256:j * 256 + 256], mod[:, gate0 + m, 0:1], XT[:, m, :],
                              ALU.mult, ALU.add, t, t_mod))
            toks.extend(ts)
            return tuple(ts)
        return evac

    for j in range(0, 8, 2):
        HL.toks[j:j + 2] = cut_pair(part(HL, j, j + 2), MT[:, j:j + 2, :], t_m[j], PE.now()) * 2
    t_mod = mod_ready(4, 12)
    project(D["w_out"], 0, 8, (HL,), 8, residual(16, t_x1))

    handover()
    mark[0] = 0
    T1 = mem(2048, 8)
    SR = mem(512)
    H2S = pair(8)
    H2 = T1
    t_r2 = inverse_rms(XT, T1, SR[:, 0:NT], t_x1)
    t_h2 = modulated(XT, SR[:, 0:NT], t_r2, scl[:, 16:24], "norm2_g", (mod[:, 24:32, 0], mod[:, 32:40, 0]), H2S, t_x1)
    t_b = {}

    def hidden(e, between=None):
        wg = pieces(D["moe_w_gate"][e], 0, 512, 8)
        wu = pieces(D["moe_w_up"][e], 0, 512, 8)
        for w, bs in ((wg, (4, 6)), (wu, (5, 7))):
            for p in w:
                h = need(p)
                for half, b in enumerate(bs):
                    steps = []
                    for j in range(2):
                        c = slice((2 * half + j) * 128, (2 * half + j) * 128 + 128)
                        for k in range(p.nk):
                            steps.append((H2S.toks[p.k0 + k],
                                          mm3(bank[b][:, j * 256:j * 256 + 256], (h.hi[:, k, c], h.lo[:, k, c]),
                                              (H2S[0][:, p.k0 + k, :], H2S[1][:, p.k0 + k, :]),
                                              p.k0 + k == 0 and j == 0, p.k0 + k == 7)))
                    t_b[b] = sweep(steps, h.tok, read[b])
                done(h, t_b[bs[1]])
                if between and w is wg and p.k0 == 0:
                    between()

    def activate(e):
        ts = []
        for half in range(2):
            bg, bu = 4 + 2 * half, 5 + 2 * half
            t3 = act(SG[half], bank[bg][:, :], ACT.Silu, t_b[bg], sg_free.get(half, ()))
            read[bg] = (t3,)
            s3 = SG[half].rearrange("p (j t) -> p j t", j=2)
            t4 = vtt(SG[half], SG[half], bank[bu][:, :], ALU.mult, t3, t_b[bu])
            read[bu] = (t4,)
            t5 = vtt(s3, s3, wide(GB[:, e, :], 2), ALU.mult, t4, t_gb)
            t6 = cut_pair(part(HD[e % 2], 2 * half, 2 * half + 2), s3, t5, hd_free.get(e % 2, ()))
            sg_free[half] = t6
            ts += t6
        t_hd[e] = ts

    def gates():
        b = pick((0, 1, 2, 3))
        jobs = []
        for i in range(2):
            jobs += chain(bank[b][:, i * 16:i * 16 + 16], [(H2[:, k, i * 128:i * 128 + 128], RWT[:, k, :]) for k in range(8)])
        t = mms(jobs, t_h2, t_rw, read[b])
        S3 = mem(32, 2)
        SEL3 = mem(32, 2)
        t_s = act(S3, bank[b][:, 0:32].rearrange("p (i e) -> p i e", i=2), ACT.Sigmoid, t)
        read[b] = (t_s,)
        t = vtt(SEL3, S3, wide(RB, 2), ALU.add, t_s)
        q4 = SEL3.rearrange("p i (g e) -> p (i g) e", g=4)
        PR = mem(48, 8)
        t1 = vtt(PR[:, :, 0:3], q4[:, :, 0:3], q4[:, :, 1:4], ALU.add, t)
        t2 = vtt(PR[:, :, 3:5], q4[:, :, 0:2], q4[:, :, 2:4], ALU.add, t)
        t3 = vtt(PR[:, :, 5:6], q4[:, :, 0:1], q4[:, :, 3:4], ALU.add, t)
        GS = mem(8, 2)
        t = V(lambda e: e.tensor_reduce(GS.rearrange("p i g -> p (i g)"), PR, AX.X, ALU.max), t1, t2, t3)

        def first_of_largest(x, n, hot, rank, *after):
            mx = cols(2)
            t = V(lambda e: e.tensor_reduce(mx, x, AX.X, ALU.max), *after)
            t = vtt(hot, x, long(mx, n), ALU.is_equal, t)
            t = vtt(hot, hot, wide(rank, 2), ALU.mult, t, t_cst)
            t = V(lambda e: e.tensor_reduce(mx, hot, AX.X, ALU.max), t)
            return vtt(hot, hot, long(mx, n), ALU.is_equal, t)

        GH = mem(8, 2)
        t = first_of_largest(GS, 4, GH, C("rank")[:, 0:4], t)
        KG = mem(8, 2)
        t1 = vts(KG, GH, 1.0, 1e30, ALU.subtract, ALU.mult, t)
        sm = SEL3.rearrange("p i (g e) -> p (i g) e", g=4)
        gh2 = long(GH.rearrange("p i g -> p (i g)"), 4)
        kg2 = long(KG.rearrange("p i g -> p (i g)"), 4)
        t = vtt(sm, sm, gh2, ALU.mult, t)
        t = vtt(sm, sm, kg2, ALU.add, t, t1)
        O1 = mem(32, 2)
        O2 = mem(32, 2)
        t_o1 = first_of_largest(SEL3, 16, O1, C("rank"), t)
        t = stt(SEL3, O1, -1e30, SEL3, ALU.mult, ALU.add, t_o1)
        t = first_of_largest(SEL3, 16, O2, C("rank"), t)
        t = vtt(O1, O1, O2, ALU.add, t)
        t = vtt(O1, O1, S3, ALU.mult, t)
        ws = cols(2)
        t = V(lambda e: e.tensor_reduce(ws, O1, AX.X, ALU.add), t)
        t = V(lambda e: e.reciprocal(ws, ws), t)
        t = vtt(O1, O1, long(ws, 16), ALU.mult, t)
        return O1, t

    router = []
    hidden(0, between=lambda: router.append(gates()))
    O1, t = router[0]
    b = pick((0, 1, 2, 3))
    t = turned([(bank[b][0:16, i * 128:i * 128 + 128], O1[:, i, :]) for i in range(2)], t, read[b])
    GT = mem(256)
    t_gt = vcopy(GT[0:16, :], bank[b][0:16, 0:256], t)
    read[b] = (t_gt,)
    GB = mem(4096, 16)
    t_gb = []
    for e0 in range(0, 16, 2):
        b = pick((0, 1, 2, 3))
        jobs = []
        for j in range(2):
            jobs += chain(bank[b][:, j * 256:j * 256 + 256],
                          [(C("ident")[0:16, e0 + j:e0 + j + 1].broadcast_to([16, 128]), GT[0:16, :])])
        t = mms(jobs, t_gt, t_rw, read[b])
        t = act(GB[:, e0:e0 + 2, :], bank[b][:, :].rearrange("p (j t) -> p j t", j=2), ACT.Copy, t)
        read[b] = (t,)
        t_gb.append(t)
    HD = [pair(4), pair(4)]
    SG = [mem(512), mem(512)]
    t_hd = {}
    hd_free = {}
    sg_free = {}

    def accumulate(w, X, nk, r0, k_of, first, last, *after, between=None):
        for p in pieces(w[r0 * 128:(r0 + nk) * 128, :], 0, 1024, nk):
            h = need(p)
            jobs = []
            for m in range(8):
                for k in range(p.nk):
                    x = k_of(p.k0 + k)
                    jobs += mm3(bank[m // 2][:, (m % 2) * 256:(m % 2) * 256 + 256],
                                (h.hi[:, k, m * 128:m * 128 + 128], h.lo[:, k, m * 128:m * 128 + 128]),
                                (X[0][:, x, :], X[1][:, x, :]),
                                first and p.k0 + k == 0 and m % 2 == 0, last and p.k0 + k == nk - 1)
            t = mms(jobs, h.tok, *after)
            done(h, t)
            if between and p.k0 == 0:
                between()
        return t

    def down(e, between=None):
        t = accumulate(D["moe_w_down"][e], HD[e % 2], 4, 0, lambda k: k, e == 0, e == 15, t_hd[e],
                       read[0:4] if e == 0 else (), between=between)
        hd_free[e % 2] = t
        return t

    mark_, mark[0] = mark[0], ARENA - 4352
    ROT = mem(1024, 4)
    PP = pair(4)
    AM = mem(1024)
    LP = mem(256, 4)
    mark[0] = 17408
    PT0 = mem(1024, 4)
    POS, POSI, K1, K2 = (mem(256) for _ in range(4))
    mark[0] = mark_
    cosA, sinA, cosB, sinB = (ROT[:, i, :] for i in range(4))
    loads = [("s_pp", PT0, D["pT"]), ("s_pos", POSI.bitcast(I32), D["positions"].partition_broadcast(128)),
             ("s_am", AM, D["amask"]), ("s_lp", LP.rearrange("p a b -> p (a b)"), D["c_lambda"].partition_broadcast(128))]
    G.wait([x.now() for x in lanes])
    t_pp_in, t_pos, t_am, t_lp = (fetch(dst, src, G, name) for name, dst, src in loads)
    NL = cols(2)
    SLN = cols(1)
    t_rot, t_nl, t_sln, t_pp = [], [], [], []

    def rotations(n):
        cosn, sinn = ROT[:, 2 * n, :], ROT[:, 2 * n + 1, :]
        t = vcopy(POS, POSI.bitcast(I32), t_pos) if n == 0 else ()
        t1 = vts(sinn, POS, C("freq")[:, n:n + 1], None, ALU.mult, None, t, t_cst)
        t1 = reduce_angle(sinn, sinn, K1, t1)
        t1 = vts(cosn, sinn, math.pi / 2, None, ALU.add, None, t1)
        t2 = vts(K2, cosn, math.pi, -TWO_PI, ALU.is_gt, ALU.mult, t1)
        t2 = vtt(cosn, cosn, K2, ALU.add, t2)
        t3 = vts(cosn, cosn, PI_F, -PI_F, ALU.min, ALU.max, t2)
        t4 = vts(sinn, sinn, PI_F, -PI_F, ALU.min, ALU.max, t2)
        t_rot.append(act(ROT[:, 2 * n:2 * n + 2, :], ROT[:, 2 * n:2 * n + 2, :], ACT.Sin, t3, t4))

    def small_operands():
        LS = cols(2)
        t = vtt(LP[:, 0:3:2, :], LP[:, 0:3:2, :], LP[:, 1:4:2, :], ALU.mult, t_lp)
        t = V(lambda e: e.tensor_reduce(LS, LP[:, 0:3:2, :], AX.X, ALU.add), t)
        t = act(LS, LS, ACT.Exp, t)
        t = vtt(NL[:, 0:1], LS[:, 1:2], LS[:, 0:1], ALU.subtract, t)
        t_nl.append(vts(NL[:, 0:1], NL[:, 0:1], LAMBDA_INIT, None, ALU.subtract, None, t))
        t_sln.append(vts(SLN, vcol("c_subln_2"), 1.0 - LAMBDA_INIT, None, ALU.mult, None, t_vec))
        t_pp.extend(cut_pair(PP, PT0, t_pp_in))

    beside = {3: lambda: rotations(0), 4: lambda: rotations(1), 5: small_operands}
    for e in range(17):
        if 1 <= e < 16:
            hidden(e)
        if e == 0:
            activate(e)
        if e >= 1:
            t_y = down(e - 1, (lambda: activate(e)) if e < 16 else None)
        if e in beside:
            beside[e]()
    t_x = []
    mark[0] = 0
    T1 = mem(2048, 8)
    XS = pair(8)

    def front(i):
        ts = [stt(XT[:, m, :], bank[i][:, (m % 2) * 256:(m % 2) * 256 + 256], mod[:, 40 + m, 0:1], XT[:, m, :],
                  ALU.mult, ALU.add, t_y) for m in (2 * i, 2 * i + 1)]
        read[i] = tuple(ts)
        t_x.extend(ts)

    def back(i):
        j = 2 * i
        XS.toks[j:j + 2] = cut_pair(part(XS, j, j + 2), XT[:, j:j + 2, :], t_x[j:j + 2]) * 2

    in_turn(front, back)
    spare[0] = (0, 1, 2, 3)

    SR = mem(512)
    RC = mem(512)
    MX = mem(2048, 8)
    base = mark[0]
    QT = mem(2048, 8)
    KT = mem(2048, 8)
    VV = mem(2048, 2)
    o_e = mark[0]
    E_ = [mem(512), mem(512)]
    E2_ = [mem(512), mem(512)]
    o_ck = mark[0]
    PT_ = [mem(512), mem(512)]
    RN = mem(512)
    RQ, RR = mem(512), mem(512)
    hn = {}
    at = {}
    E_.append(E2_[0])
    RN_, RC_ = [RN, RQ], [RC, RR]

    W = D["ab_w_in"]

    def rope_proj(dst, c0, nm, cos, sin, R, *after):
        ts = []

        def evac(m0, b, t):
            i = m0 // 2 % 2
            tc = act(RN_[i], bank[b][:, :], ACT.Copy, t, hn.get(("rn", i), ()))
            read[b] = (tc,)
            yield
            t1, t2 = yield from rope(RN_[i], 2, R, cos, sin, dst[:, m0:m0 + 2, :], 128, tc, t_rot, slot=i)
            hn[("rn", i)] = (t1, t2)
            ts.append(t1)
            return (tc,)
        project(W, c0, nm, (XS,), 8, evac, *after, lag="on")
        return ts

    t_q = rope_proj(QT, 0, 4, cosA, sinA, C("Ra"))
    t_k = rope_proj(KT, 512, 4, cosA, sinA, C("Ra"))
    TOK2 = [tokens_of(XS, i) for i in range(2)]
    t_v = token_major(W, 1024, 512, TOK2, 8, lambda i: VV[:, i:i + 1, 0:512], wait=(XS,))
    t_mx = []

    def pair_scores(u, q, k, p, *after):
        b = 4 + u % 2
        jobs = []
        for i in range(2):
            jobs += chain(bank[b][:, i * 256:i * 256 + 256], [(q[:, i * 128:i * 128 + 128], k)])
        return b, mms(jobs, *after, read[b])

    def first(u):
        p = slice(64 * (u % 2), 64 * (u % 2) + 64)
        b, t = pair_scores(u, QT[p, u // 2, :], KT[p, u // 2, :], p, t_q, t_k)
        return softmax(u, b, (t, t_am), 2, 0.125, masked=True, E=E_[u % 3])

    def second(u, t):
        return flip(u, E_[u % 3], t, (0, 2, 1, 3))

    def third_half(u, t, col, tile):
        b = u % 4
        p = slice(64 * (u % 2), 64 * (u % 2) + 64)
        PT = PT_[u % 2]
        t = mms(chain(bank[b][p, 0:256], [(VV[:, j, col:col + 64], PT[:, j * 256:j * 256 + 256]) for j in range(2)]),
                t, t_v, read[b])
        at[("pt", u % 2)] = t
        t = act(MX[p, tile, :], bank[b][p, 0:256], ACT.Copy, t)
        read[b] = (t,)
        t_mx.append(t)
        if tile >= 4 and u % 2 == 1:
            XS.toks[tile:tile + 1] = cut_pair(part(XS, tile, tile + 1), MX[:, tile:tile + 1, :], t_mx[-2:])

    staged(8, first, second, lambda u, t: third_half(u, t, 64 * u, u // 2))
    qk_read = PE.now()

    T1f = T1.rearrange("p k t -> p (k t)")
    CQ, CSQ = (T1f[:, o:o + 768].rearrange("p (k t) -> p k t", k=3) for o in (0, 768))
    CK = T1f[:, 1536:2048].rearrange("p (k t) -> p k t", k=2)
    CR, CRR = E2_[1][:, 0:256], E2_[1][:, 256:512]
    CS = CSQ
    t_c = []
    CQK = [CQ[:, 0, :], CQ[:, 1, :], CQ[:, 2, :], CK[:, 0, :], CK[:, 1, :]]

    def evac(m0, b, t):
        for j in range(min(2, 5 - m0)):
            t = act(CQK[m0 + j], bank[b][:, j * 256:j * 256 + 256], ACT.Copy, t)
            t_c.append(t)
        return (t,)
    t = project(W, 1536, 5, (XS,), 8, evac)
    for j in range(0, 4, 2):
        XS.toks[j:j + 2] = cut_pair(part(XS, j, j + 2), MX[:, j:j + 2, :], t_mx, t) * 2
    h = need(pieces(W, 1952, 256, 8, raw=True)[0])
    b = pick()
    t_m = mms(chain(bank[b][64:96, 0:256], [(h.hi[:, k, 224:256], XT[:, k, :]) for k in range(8)]),
              h.tok, t_x, read[b])
    done(h, t_m)
    t_z = V(lambda e: e.memset(CR[0:64, :], 0.0))
    t_cr = act(CR[64:96, :], bank[b][64:96, 0:256], ACT.Copy, t_m)
    read[b] = (t_cr,)

    def plain_norm(X, nk, d, eps, gname, *after):
        t = act(CS[:, 0:nk, :], X, ACT.Square, *after, hn.get("cs", ()))
        b = pick()
        t = ones_sum([CS[:, k, :] for k in range(nk)], NT, b, t)
        hn["cs"] = t
        t_r, t = inv_root(bank[b][:, 0:NT], NT, d, eps, SR[:, 0:NT], t, hn.get("sr", ()))
        read[b] = (t_r,)
        ts = [stt(X[:, k, :], X[:, k, :], vcol(gname, k), SR[:, 0:NT], ALU.mult, ALU.mult, t) for k in range(nk)]
        hn["sr"] = ts
        return ts

    e_at = o_e
    def pair_at(o, k):
        v = pairs_[:, o:o + 512 * k].rearrange("p (h k t) -> p h k t", h=2, k=k)
        return Cut(v[:, 0], v[:, 1], [()] * k)

    CQS, CKS = pair_at(e_at, 3), pair_at(o_ck, 2)
    t_cq = plain_norm(CQ, 3, 384, EPS, "ab_q_norm_2", t_c)
    t_cq = cut_pair(CQS, CQ, t_cq, qk_read)
    t_ck = plain_norm(CK, 2, 256, EPS, "ab_kv_norm_2", t_c)
    t_ck = cut_pair(CKS, CK, t_ck, qk_read)
    t_kr, _ = whole(rope(CR[0:96, :], 1, C("Rb")[0:96, 0:96], cosB, sinB, CRR.unsqueeze(1), 96, t_z, t_cr, t_rot,
                         rows=(64, 96)))
    t_q = []

    def evac(h0, b, t):
        i = h0 // 2 % 2
        rn = RN_[i][0:96, :]
        t = act(rn, bank[b][0:96, :], ACT.Copy, t, hn.get(("rn", i), ()))
        yield
        t1, t2 = yield from rope(rn, 2, C("Rb")[0:96, 0:96], cosB, sinB, QT[:, h0:h0 + 2, :], 96, t, qk_read, slot=i)
        hn[("rn", i)] = (t1, t2)
        t_q.append(t1)
        return (t,)
    project(D["ab_w_q_up"], 0, 8, (CQS,), 3, evac, width=96, lag=True)
    t_k = []
    h = need(pieces(D["ab_w_kv_up"], 0, 1024, 2)[0])
    for h0 in range(0, 8, 2):
        b = pick()
        jobs = []
        for j in range(2):
            for k in range(2):
                c = slice((h0 + j) * 128, (h0 + j) * 128 + 128)
                jobs += mm3(bank[b][:, j * 256:j * 256 + 256], (h.hi[:, k, c], h.lo[:, k, c]),
                            (CKS[0][:, k, :], CKS[1][:, k, :]), k == 0, k == 1)
        t = mms(jobs, h.tok, t_ck, read[b])
        t = act(KT[0:64, h0:h0 + 2, :], bank[b][0:64, :].rearrange("p (j t) -> p j t", j=2), ACT.Copy, t, qk_read)
        read[b] = (t,)
        t_k.append(t)
    t_k.append(vcopy(KT[64:96, :, :], wide(CRR[64:96, :], 8), t_kr, qk_read))
    wv = [x.rearrange("p k (h n) -> p k h n", h=8) for x in (h.hi, h.lo)]
    t_v = []
    for i in range(2):
        b = pick()
        jobs = []
        for k in range(2):
            jobs += mm3(bank[b][:, :], tuple(x[:, k, i * 128:i * 128 + 128] for x in CKS[:2]),
                        tuple(x[:, k, :, 64:128] for x in wv), k == 0, k == 1)
        t_m = mms(jobs, read[b])
        t = act(VV[:, i, 0:512], bank[b][:, :], ACT.Copy, t_m, qk_read)
        read[b] = (t,)
        t_v.append(t)
    done(h, t_m)

    def first(u):
        b, t = pair_scores(u, QT[0:96, u, :], KT[0:96, u, :], None, t_q, t_k)
        return softmax(u, b, t, 2, 96 ** -0.5, E=E_[u % 3])

    staged(8, first, second, lambda u, t: third_half(u, t, 64 * u, 4 + u // 2))

    def into_t1(toks):
        def evac(m, b, t):
            t = stt(T1[:, m:m + 2, :], XT[:, m:m + 2, :], ALPHA, bank[b][:, :].rearrange("p (j t) -> p j t", j=2),
                    ALU.mult, ALU.add, t)
            toks.append(t)
            return (t,)
        return evac

    def layer_norm(gname, bname, i, toks, meanwhile=None):
        b = pick()
        t = sum_by_parts(b, T1, toks)
        t = vts(SR[:, 256:512], bank[b][:, 0:NT], 1.0 / 1024, None, ALU.mult, None, t)
        read[b] = (t,)
        if meanwhile:
            meanwhile()
        t_sq = []
        for j in range(0, 8, 2):
            x = T1[:, j:j + 2, :]
            t1 = vtt(x, x, wide(SR[:, 256:512], 2), ALU.subtract, t)
            t_sq.append(act(XT[:, j:j + 2, :], x, ACT.Square, t1))
        b = pick()
        t = sum_by_parts(b, XT, t_sq)
        t_r, t = inv_root(bank[b][:, 0:NT], NT, 1024, 1e-5, SR[:, 0:NT], t)
        read[b] = (t_r,)
        ts, t1 = [], {}

        def front(n):
            x = T1[:, 2 * n:2 * n + 2, :]
            t1[n] = vtt(x, x, wide(SR[:, 0:NT], 2), ALU.mult, t)

        def back(n):
            j = 2 * n
            t2 = [act(XT[:, k, :], T1[:, k, :], ACT.Identity, t1[n], scale=vcol(gname, 8 * i + k),
                      bias=vcol(bname, 8 * i + k)) for k in (j, j + 1)]
            ts.extend(t2)
            XS.toks[j:j + 2] = cut_pair(part(XS, j, j + 2), XT[:, j:j + 2, :], t2) * 2

        in_turn(front, back)
        return ts

    def mix_out(wname):
        toks = []
        project(D[wname], 0, 8, (XS,), 8, into_t1(toks))
        return toks

    def ffn(i):
        mark[0] = base
        A0 = mem(1024, 2)
        HF_ = pair(11)
        wg_, wu_, wd_ = D["ffn_w_gate"][i], D["ffn_w_up"][i], D["ffn_w_down"][i]
        a_free = {}
        h_free = {}
        t_h = {}
        blocks = [(0, 512), (512, 512), (1024, 512), (1536, 512), (2048, 512), (2560, 256)]

        def hid(c):
            c0, n = blocks[c]
            nb = n // 256
            par0 = c0 // 256
            t_b = {}
            for w, o in ((wg_, 0), (wu_, 1)):
                for p in pieces(w, c0, n, 8):
                    h = need(p)
                    for q in range(nb):
                        b = 4 + 2 * ((par0 + q) % 2) + o
                        steps = []
                        for j in range(2):
                            c_ = slice((2 * q + j) * 128, (2 * q + j) * 128 + 128)
                            for k in range(p.nk):
                                steps.append((XS.toks[p.k0 + k],
                                              mm3(bank[b][:, j * 256:j * 256 + 256], (h.hi[:, k, c_], h.lo[:, k, c_]),
                                                  (XS[0][:, p.k0 + k, :], XS[1][:, p.k0 + k, :]),
                                                  p.k0 + k == 0 and j == 0, p.k0 + k == 7)))
                        t_b[b] = t = sweep(steps, h.tok, read[b])
                    done(h, t)
            return t_b

        def activate(c, t_b):
            c0, n = blocks[c]
            nb = n // 256
            par0 = c0 // 256
            v = 66 * i
            parts = [(2 * q + c0 // 128, (par0 + q) % 2) for q in range(nb)]
            t_a = {}
            for m0, par in parts:
                bg, t1 = 4 + 2 * par, t_b[4 + 2 * par]
                tc = [act(A0[:, par, j * 256:j * 256 + 256], bank[bg][:, j * 256:j * 256 + 256], ACT.Identity,
                          t1, a_free.get(par, ()), scale=vcol("ffn_conv_w_2", v + 22 + m0 + j),
                          bias=vcol("ffn_conv_b_2", 22 * i + m0 + j)) for j in range(2)]
                ta = []
                for j in range(2):
                    src = bank[bg][:, j * 256:j * 256 + 256]
                    dst = A0[:, par, j * 256:j * 256 + 256]
                    t = stt(dst[:, 1:256], src[:, 0:255], vcol("ffn_conv_w_2", v + m0 + j), dst[:, 1:256],
                            ALU.mult, ALU.add, tc)
                    ta.append(stt(dst[:, 0:255], src[:, 1:256], vcol("ffn_conv_w_2", v + 44 + m0 + j), dst[:, 0:255],
                                  ALU.mult, ALU.add, t))
                read[bg] = tuple(ta)
                t_a[par] = act(A0[:, par, :], A0[:, par, :], ACT.Gelu_apprx_tanh, ta)
            for m0, par in parts:
                bu, t2 = 5 + 2 * par, t_b[5 + 2 * par]
                t3 = vtt(A0[:, par, :], A0[:, par, :], bank[bu][:, :], ALU.mult, t_a[par], t2)
                read[bu] = (t3,)
                ts = []
                for j in range(2):
                    m = m0 + j
                    tc = cut_pair(part(HF_, m % 11, m % 11 + 1),
                                  A0[:, par, j * 256:j * 256 + 256].unsqueeze(1), t3, h_free.get(m % 11, ()))
                    t_h[m] = tc
                    ts += tc
                a_free[par] = ts

        def dn(c, between):
            c0, n = blocks[c]
            nk = n // 128
            t = accumulate(wd_, HF_, nk, c0 // 128, lambda k: (c0 // 128 + k) % 11, c == 0, c == 5,
                           [t_h[c0 // 128 + k] for k in range(nk)], read[0:4] if c == 0 else (), between=between)
            for k in range(nk):
                h_free[(c0 // 128 + k) % 11] = t
            return t

        for c in range(7):
            if c < 6:
                t_b = hid(c)
            if c >= 1:
                t = dn(c - 1, (lambda: activate(c, t_b)) if c < 6 else None)
            else:
                activate(c, t_b)
        ts = []
        for j in range(4):
            t2 = stt(T1[:, 2 * j:2 * j + 2, :], XT[:, 2 * j:2 * j + 2, :], ALPHA,
                     bank[j][:, :].rearrange("p (a t) -> p a t", a=2), ALU.mult, ALU.add, t)
            read[j] = (t2,)
            ts.append(t2)
        return ts

    PJ = MX

    def ple_project(i):
        t_pj = []

        def evac(m, b, t):
            t = act(PJ[:, m:m + 2, :], bank[b][:, :].rearrange("p (j t) -> p j t", j=2), ACT.Copy, t)
            t_pj.append(t)
            return (t,)
        P_ = part(PP, 2 * i, 2 * i + 2)
        project(D["ple_w_proj"][i], 0, 8, (P_,), 2, evac, t_pp)
        return t_pj

    def ple(i, t_pj, dst):
        ts = []

        def evac(m, b, t):
            g, x = T1[:, m:m + 2, :], XT[:, m:m + 2, :]
            t = act(g, bank[b][:, :].rearrange("p (j t) -> p j t", j=2), ACT.Sigmoid, t)
            t2 = vtt(g, g, PJ[:, m:m + 2, :], ALU.mult, t, t_pj)
            t2 = vtt(x, x, g, ALU.add, t2)
            if dst is None:
                SP.dma(lambda e: e.dma_start(out[:, m:m + 2, :], x), sem("s_out"), t2)
            else:
                dst.toks[m:m + 2] = cut_pair(part(dst, m, m + 2), x, t2) * 2
            ts.append(t2)
            return (t,)
        project(D["ple_w_gate"][i], 0, 8, (XS,), 8, evac)
        return ts

    def after_mixer(i, wname, dst):
        layer_norm("ln_mix_g_2", "ln_mix_b_2", i, mix_out(wname))
        toks = ffn(i)
        t_pj = []
        layer_norm("ln_ffn_g_2", "ln_ffn_b_2", i, toks, lambda: t_pj.extend(ple_project(i)))
        return ple(i, t_pj, dst)

    XC_ = pair_at(base + 6144, 8)
    t_x = after_mixer(0, "ab_w_out", XC_)

    mark[0] = base
    W = D["c_w_qkv"]
    XA, XS = XS, XC_
    QT = mem(2048, 8)
    KT = mem(2048, 8)
    VV = mem(2048, 2)
    E_ = [mem(512), mem(512)]
    E2_ = [mem(512), mem(512)]
    PT_ = [mem(512), mem(512)]
    RQ, RR = mem(512), mem(512)
    RN = mem(512)
    T1f = T1.rearrange("p k t -> p (k t)")
    E_.append(T1f[:, 0:512])
    E2_.append(T1f[:, 512:1024])
    RN_, RC_ = [RN, T1f[:, 1024:1536]], [RC, T1f[:, 1536:2048]]
    RQ_, RR_ = [RQ], [RR]
    TOK2 = [tokens_of(XS, i) for i in range(2)]
    t_q = rope_proj(QT, 0, 8, cosA, sinA, C("Ra"))
    t_k = rope_proj(KT, 1024, 8, cosA, sinA, C("Ra"))
    t_v = []
    for c in range(2):
        t_v += token_major(W, 2048 + 512 * c, 512, TOK2, 8, lambda i, c=c: VV[:, i:i + 1, 512 * c:512 * c + 512],
                           wait=(XS,))
    XS = XA
    t_mx = []

    def first(u):
        b, t = pair_scores(u, QT[0:64, u, :], KT[0:64, u, :], None, t_q, t_k)
        b2 = 2 + u % 2
        jobs = []
        for i in range(2):
            jobs += chain(bank[b2][:, i * 256:i * 256 + 256], [(QT[64:128, u, i * 128:i * 128 + 128], KT[64:128, u, :])])
        tb = mms(jobs, read[b2])
        tail2 = softmax(u, b2, (tb, t_nl), 2, 0.125, E=E2_[u % 3], key="e2", factor=NL[:, 0:1])
        tail1 = softmax(u, b, t, 2, 0.125, E=E_[u % 3], plus=E2_[u % 3])

        def tail():
            at[("e2", u % 3)] = t = tail1(tail2())
            return t
        return tail

    def normed(u, t):
        dst = MX[:, u - 1:u + 1, :]
        flat_ = dst.rearrange("p a t -> p (a t)")
        t = yield from head_norm(0, t, SLN, flat_, 512, eps=1e-5, among=(1,))
        XS.toks[u - 1:u + 1] = cut_pair(part(XS, u - 1, u + 1), dst, t, t_sln) * 2

    def third(u, t):
        PT = PT_[u % 2]
        o = 256 * (u % 2)
        t = mms([(bank[0][:, o:o + 256], VV[:, j, 128 * u:128 * u + 128], PT[:, j * 256:j * 256 + 256],
                  j == 0 and u % 2 == 0, j == 1) for j in range(2)], t, t_v, read[0])
        at[("pt", u % 2)] = t
        if u % 2 == 1:
            lagging.append(normed(u, t))

    staged(8, first, second, third)
    after_mixer(1, "c_w_out", None)
    SP.wait(Tok(sem("s_out"), 64))

    if not final:
        return
    with nc.Block() as block:

        @block.tensor
        def _(e):
            PE.run(e)

        @block.vector
        def _(e):
            V.run(e)

        @block.scalar
        def _(e):
            A.run(e)

        @block.gpsimd
        def _(e):
            G.run(e)

        @block.sync
        def _(e):
            SP.run(e)


def arrays(x):
    a = {k: np.asarray(v) for k, v in x.items()}
    tile = lambda v: v.reshape(-1, 128).T
    fm = lambda v: v.reshape(NT, -1, 128).transpose(2, 1, 0)
    d = {n: a[n][0] for n in ("w_mod", "w_in", "w_br_hy", "w_br_gla", "w_br_att", "w_out", "moe_w_gate",
                              "moe_w_up", "moe_w_down", "hy_pos_w1", "hy_pos_w2", "hy_pos_w3")}
    d |= {"consts": CONSTS, "dft": DFT, "amask": AMASK, "posemb": POSEMB}
    d["vecs"] = np.concatenate([tile(a[n]) for n, _ in VECS], axis=1)
    d["cc"] = np.stack([tile(a["c"]), tile(a["c_ctx"])], axis=2).reshape(128, 16)
    d["xT"] = fm(a["x"])
    d["ctxT"] = fm(a["ctx"])
    d["hy_decay"] = a["hy_decay"].reshape(2048)
    d["hy64"] = np.stack([a["hy_pos_b1"][0], a["hy_sin_freq"][0], a["hy_pos_b2"][0]], axis=1)
    w2z = np.zeros((33, 512), np.float32)
    w2z[0:16, 0:256] = a["gla_wa2"][0, 0]
    w2z[16:32, 256:512] = a["gla_wa2"][0, 1]
    w2z[32] = a["gla_ba"].reshape(512)
    d["w2z"] = w2z
    d["router_w"], d["router_b"] = a["router_w"], a["router_b"]
    d["pT"] = a["p_2"].reshape(2, NT, 2, 128).transpose(3, 0, 2, 1).reshape(128, 4, NT)
    d["positions"] = a["positions_2"].reshape(NT)
    for n in ("ab_w_in", "ab_w_q_up", "ab_w_kv_up", "ab_w_out", "c_w_qkv", "c_w_out"):
        d[n] = a[n + "_2"][0]
    d["c_lambda"] = a["c_lambda_2"].reshape(256)
    for n in ("ffn_w_gate", "ffn_w_up", "ffn_w_down", "ple_w_gate", "ple_w_proj"):
        d[n] = a[n + "_2"]
    return {k: np.ascontiguousarray(v) for k, v in d.items()}


def kernel(**inputs):
    import concourse.bacc as bacc
    from concourse.bass_utils import run_bass_kernel_spmd

    nc = bacc.Bacc("TRN2", target_bir_lowering=False, num_devices=1)
    d = arrays(inputs)
    aps = {k: nc.dram_tensor(f"in_{k}", v.shape, mybir.dt.from_np(v.dtype), kind="ExternalInput").ap()
           for k, v in d.items()}
    out = nc.dram_tensor("out_0", (128, 8, NT), F32, kind="ExternalOutput").ap()
    build(nc, aps, out)
    r = run_bass_kernel_spmd(nc, [{f"in_{k}": v for k, v in d.items()}], core_ids=[0])
    return r.results[0]["out_0"].transpose(2, 1, 0).reshape(1, NT, 1024)
```
